# Optimizing a Trainium2 kernel written in Bass

```python
import math
import jax, jax.numpy as jnp
from jax import lax
import numpy as np

D_MODEL = 1024
BATCH = 1
SEQ = 128
DEPTH = 2
DEC_BATCH = 1
DEC_SEQ = 512
PAST_LEN = 128

GRID_W = 64
A_HEADS = 8
A_QK_DIM = 64
A_V_DIM = 128
A_WIDTH = A_HEADS * A_V_DIM
ROPE_BASE = 10000.0
Q_BLOCK = 128
POOL_WINDOWS = (2, 4, 8, 16)
POOL_GROUP = 128
POOL_WIDTH = len(POOL_WINDOWS) * POOL_GROUP
CONV_WIDTH = 512
CONV_K = 31
N_BRANCH = 3
N_EXPERTS = 16
EXPERT_FF = 1024
CAPACITY_FACTOR = 2
Q_COLS = A_HEADS * 2 * A_QK_DIM
K_COLS = A_HEADS * 2 * A_QK_DIM
V_COLS = A_WIDTH
CONV_IN = 2 * CONV_WIDTH
IN_WIDTH = Q_COLS + K_COLS + V_COLS + POOL_WIDTH + CONV_IN
SPLIT_POINTS = (Q_COLS, Q_COLS + K_COLS, Q_COLS + K_COLS + V_COLS, Q_COLS + K_COLS + V_COLS + POOL_WIDTH)
EPS = 1e-6

kernel_name = "hybrid_diffattn_pool_conformer_ec_moe_diffusion_step"

def rms_norm(x, g):
    xf = x.astype(jnp.float32)
    y = xf * lax.rsqrt(jnp.mean(xf * xf, axis=-1, keepdims=True) + EPS)
    return y.astype(x.dtype) * g

def layer_norm(x, g, b):
    xf = x.astype(jnp.float32)
    mu = jnp.mean(xf, axis=-1, keepdims=True)
    var = jnp.mean(jnp.square(xf - mu), axis=-1, keepdims=True)
    return ((xf - mu) * lax.rsqrt(var + EPS)).astype(x.dtype) * g + b

def axial_rope(x):
    L = x.shape[1]
    rows = L // GRID_W
    row = jnp.repeat(jnp.arange(rows), GRID_W)
    col = jnp.tile(jnp.arange(GRID_W), rows)
    half = A_QK_DIM // 2
    nf = half // 2
    inv = ROPE_BASE ** (-jnp.arange(nf, dtype=jnp.float32) / nf)

    def rot(xp, pos):
        ang = pos.astype(jnp.float32)[:, None] * inv[None, :]
        cos = jnp.cos(ang)[None, :, None, None, :].astype(x.dtype)
        sin = jnp.sin(ang)[None, :, None, None, :].astype(x.dtype)
        x1, x2 = xp[..., :nf], xp[..., nf:]
        return jnp.concatenate([x1 * cos - x2 * sin, x1 * sin + x2 * cos], axis=-1)

    return jnp.concatenate([rot(x[..., :half], row), rot(x[..., half:], col)], axis=-1)

def diff_attention(q, k, v, lam):
    B, Lq, H = q.shape[:3]
    nblk = Lq // Q_BLOCK
    scale = A_QK_DIM ** -0.5
    qb = jnp.moveaxis(q.reshape(B, nblk, Q_BLOCK, H, 2, A_QK_DIM), 1, 0)

    def block(qblk):
        s = jnp.einsum('bqhmd,bkhmd->bmhqk', qblk, k).astype(jnp.float32) * scale
        p = jax.nn.softmax(s, axis=-1)
        a = p[:, 0] - lam * p[:, 1]
        return jnp.einsum('bhqk,bkhe->bqhe', a.astype(v.dtype), v)

    o = lax.map(block, qb)
    return jnp.moveaxis(o, 0, 1).reshape(B, Lq, H, A_V_DIM)

def multiscale_pool(u, pool_w, pool_scale):
    B, L, _ = u.shape
    ug = u.reshape(B, L, len(POOL_WINDOWS), POOL_GROUP)
    cs = jnp.cumsum(ug.astype(jnp.float32), axis=1)
    S = jnp.concatenate([jnp.zeros_like(cs[:, :1]), cs], axis=1)
    t = jnp.arange(L)
    outs = []
    for g, w in enumerate(POOL_WINDOWS):
        lo = jnp.clip(t - w // 2, 0, L)
        hi = jnp.clip(t + w // 2, 0, L)
        Sg = S[:, :, g]
        cnt = (hi - lo).astype(jnp.float32)[None, :, None]
        outs.append((Sg[:, hi] - Sg[:, lo]) / cnt)
    pooled = (jnp.stack(outs, axis=2) - ug.astype(jnp.float32)).astype(u.dtype)
    y = jnp.einsum('blgc,gcd->blgd', pooled, pool_w).reshape(B, L, POOL_WIDTH)
    return y * pool_scale

def conformer_conv(u, conv_w, conv_b, ln_g, ln_b):
    a, b = jnp.split(u, 2, axis=-1)
    z = a * jax.nn.sigmoid(b)
    pad = (CONV_K - 1) // 2
    z = lax.conv_general_dilated(z, conv_w[:, None, :], window_strides=(1,), padding=[(pad, pad)],
                                 dimension_numbers=('NWC', 'WIO', 'NWC'),
                                 feature_group_count=CONV_WIDTH) + conv_b
    return jax.nn.silu(layer_norm(z, ln_g, ln_b))

def expert_choice_ffn(h, w_router, w1, w3, w2):
    B, L, D = h.shape
    cap = CAPACITY_FACTOR * L // N_EXPERTS
    aff = jax.nn.softmax(jnp.einsum('bld,de->ble', h, w_router).astype(jnp.float32), axis=-1)
    gate, idx = lax.top_k(jnp.swapaxes(aff, 1, 2), cap)
    xs = jax.vmap(lambda hb, ib: hb[ib])(h, idx)
    hid = jax.nn.silu(jnp.einsum('becd,edf->becf', xs, w1)) * jnp.einsum('becd,edf->becf', xs, w3)
    ye = jnp.einsum('becf,efd->becd', hid, w2) * gate[..., None].astype(h.dtype)

    def combine(ib, yb):
        return jnp.zeros((L, D), yb.dtype).at[ib.reshape(-1)].add(yb.reshape(-1, D))

    return jax.vmap(combine)(idx, ye)

def trunk_layer(x, cvec, lp, lam_init, ctx_kv):
    B, L, _ = x.shape
    mod = jnp.einsum('bd,de->be', jax.nn.silu(cvec), lp['w_ada']) + lp['b_ada']
    sh1, sc1, g1, sh2, sc2, g2 = [m[:, None, :] for m in jnp.split(mod, 6, axis=-1)]

    h = rms_norm(x, lp['rms1_g']) * (1 + sc1) + sh1
    u = h @ lp['w_in']
    q, k, v, up, uc = jnp.split(u, SPLIT_POINTS, axis=-1)
    q = rms_norm(q.reshape(B, L, A_HEADS, 2, A_QK_DIM), lp['q_norm_g'])
    k = rms_norm(k.reshape(B, L, A_HEADS, 2, A_QK_DIM), lp['k_norm_g'])
    v = v.reshape(B, L, A_HEADS, A_V_DIM)
    own_kv = (k, v)
    if ctx_kv is None:
        k_all, v_all = k, v
    else:
        q = axial_rope(q)
        k_all = jnp.concatenate([ctx_kv[0], axial_rope(k)], axis=1)
        v_all = jnp.concatenate([ctx_kv[1], v], axis=1)
    lv = lp['lam_vec'].astype(jnp.float32)
    lam = jnp.exp(jnp.sum(lv[0] * lv[1])) - jnp.exp(jnp.sum(lv[2] * lv[3])) + lam_init
    o = diff_attention(q, k_all, v_all, lam)
    o = rms_norm(o, lp['subln_g']) * (1.0 - lam_init)
    y_a = o.reshape(B, L, A_WIDTH) @ lp['w_proj_a']
    y_b = multiscale_pool(up, lp['pool_w'], lp['pool_scale']) @ lp['w_proj_b']
    y_c = conformer_conv(uc, lp['conv_w'], lp['conv_b'], lp['conv_ln_g'], lp['conv_ln_b']) @ lp['w_proj_c']
    ga, gb, gc = jnp.split(jax.nn.sigmoid(h @ lp['w_gate'] + lp['b_gate']), N_BRANCH, axis=-1)
    x = x + g1 * ((ga * y_a + gb * y_b + gc * y_c) @ lp['w_out'])

    h2 = rms_norm(x, lp['rms2_g']) * (1 + sc2) + sh2
    x = x + g2 * expert_choice_ffn(h2, lp['w_router'], lp['w1'], lp['w3'], lp['w2'])
    return x, own_kv

def setup_inputs(seed: int = 0) -> dict:
    key = jax.random.key(seed)
    ks = jax.random.split(key, 32)
    f32 = jnp.float32

    def nrm(k, shape, scale):
        return jax.random.normal(k, shape, f32) * scale

    D = D_MODEL
    return {
        'x_prompt': nrm(ks[0], (BATCH, SEQ, D), 1.0),
        'x_sample': nrm(ks[1], (DEC_BATCH, DEC_SEQ, D), 1.0),
        'c': nrm(ks[2], (DEC_BATCH, D), 1.0),
        'cache_k': nrm(ks[3], (DEC_BATCH, DEPTH, PAST_LEN, A_HEADS, 2, A_QK_DIM), 1.0),
        'cache_v': nrm(ks[4], (DEC_BATCH, DEPTH, PAST_LEN, A_HEADS, A_V_DIM), 1.0),
        'c_ctx': nrm(ks[5], (D,), 1.0),
        'rms1_g': 1.0 + nrm(ks[6], (DEPTH, D), 0.01),
        'rms2_g': 1.0 + nrm(ks[7], (DEPTH, D), 0.01),
        'w_ada': nrm(ks[8], (DEPTH, D, 6 * D), 0.5 * D ** -0.5),
        'b_ada': nrm(ks[9], (DEPTH, 6 * D), 0.01),
        'w_in': nrm(ks[10], (DEPTH, D, IN_WIDTH), D ** -0.5),
        'q_norm_g': 1.0 + nrm(ks[11], (DEPTH, A_QK_DIM), 0.01),
        'k_norm_g': 1.0 + nrm(ks[12], (DEPTH, A_QK_DIM), 0.01),
        'lam_vec': nrm(ks[13], (DEPTH, 4, A_QK_DIM), 0.1),
        'subln_g': 1.0 + nrm(ks[14], (DEPTH, A_V_DIM), 0.01),
        'w_proj_a': nrm(ks[15], (DEPTH, A_WIDTH, D), A_WIDTH ** -0.5),
        'pool_w': nrm(ks[16], (DEPTH, len(POOL_WINDOWS), POOL_GROUP, POOL_GROUP), POOL_GROUP ** -0.5),
        'pool_scale': 1.0 + nrm(ks[17], (DEPTH, POOL_WIDTH), 0.01),
        'w_proj_b': nrm(ks[18], (DEPTH, POOL_WIDTH, D), POOL_WIDTH ** -0.5),
        'conv_w': nrm(ks[19], (DEPTH, CONV_K, CONV_WIDTH), CONV_K ** -0.5),
        'conv_b': nrm(ks[20], (DEPTH, CONV_WIDTH), 0.01),
        'conv_ln_g': 1.0 + nrm(ks[21], (DEPTH, CONV_WIDTH), 0.01),
        'conv_ln_b': nrm(ks[22], (DEPTH, CONV_WIDTH), 0.01),
        'w_proj_c': nrm(ks[23], (DEPTH, CONV_WIDTH, D), CONV_WIDTH ** -0.5),
        'w_gate': nrm(ks[24], (DEPTH, D, N_BRANCH * D), D ** -0.5),
        'b_gate': nrm(ks[25], (DEPTH, N_BRANCH * D), 0.01),
        'w_out': nrm(ks[26], (DEPTH, D, D), D ** -0.5),
        'w_router': nrm(ks[27], (DEPTH, D, N_EXPERTS), D ** -0.5),
        'w1': nrm(ks[28], (DEPTH, N_EXPERTS, D, EXPERT_FF), D ** -0.5),
        'w3': nrm(ks[29], (DEPTH, N_EXPERTS, D, EXPERT_FF), D ** -0.5),
        'w2': nrm(ks[30], (DEPTH, N_EXPERTS, EXPERT_FF, D), EXPERT_FF ** -0.5),
    }

def reference(x_prompt, x_sample, c, cache_k, cache_v, c_ctx,
              rms1_g, rms2_g, w_ada, b_ada, w_in, q_norm_g, k_norm_g, lam_vec, subln_g, w_proj_a,
              pool_w, pool_scale, w_proj_b, conv_w, conv_b, conv_ln_g, conv_ln_b, w_proj_c,
              w_gate, b_gate, w_out, w_router, w1, w3, w2):
    params = {
        'rms1_g': rms1_g, 'rms2_g': rms2_g, 'w_ada': w_ada, 'b_ada': b_ada, 'w_in': w_in,
        'q_norm_g': q_norm_g, 'k_norm_g': k_norm_g, 'lam_vec': lam_vec, 'subln_g': subln_g,
        'w_proj_a': w_proj_a, 'pool_w': pool_w, 'pool_scale': pool_scale, 'w_proj_b': w_proj_b,
        'conv_w': conv_w, 'conv_b': conv_b, 'conv_ln_g': conv_ln_g, 'conv_ln_b': conv_ln_b,
        'w_proj_c': w_proj_c, 'w_gate': w_gate, 'b_gate': b_gate, 'w_out': w_out,
        'w_router': w_router, 'w1': w1, 'w3': w3, 'w2': w2,
    }
    x_ctx = x_prompt
    x_lat = x_sample
    cvec_ctx = c_ctx[None, :]
    ks, vs = [], []
    for l in range(DEPTH):
        lp = {name: arr[l] for name, arr in params.items()}
        lam_init = 0.8 - 0.6 * math.exp(-0.3 * l)
        x_ctx, (k_l, v_l) = trunk_layer(x_ctx, cvec_ctx, lp, lam_init, None)
        ks.append(k_l)
        vs.append(v_l)
        x_lat, _ = trunk_layer(x_lat, c, lp, lam_init, (cache_k[:, l], cache_v[:, l]))
    new_k = jnp.stack(ks, axis=1)
    new_v = jnp.stack(vs, axis=1)
    return (x_ctx, x_lat, new_k, new_v)


_drawn_inputs = setup_inputs


def setup_inputs(seed=0):
    import zlib

    import numpy as np

    out = dict(_drawn_inputs(seed))
    spreads = {}
    factors = {'rms1_g': 5.686,
     'rms2_g': 8.0,
     'b_ada': 3.713,
     'q_norm_g': 8.0,
     'k_norm_g': 6.127,
     'lam_vec': 6.401,
     'subln_g': 8.0,
     'pool_scale': 8.0,
     'conv_b': 8.0,
     'conv_ln_g': 8.0,
     'conv_ln_b': 40.436,
     'b_gate': 8.0}
    for name, (base, spread) in spreads.items():
        noise = np.random.default_rng([zlib.crc32(name.encode()), seed]).standard_normal(out[name].shape)
        drawn = base * np.exp(spread * noise) if base else spread * noise
        out[name] = __import__('jax').numpy.asarray(drawn.astype(out[name].dtype))
    for name, factor in factors.items():
        out[name] = (out[name] * factor).astype(out[name].dtype)
    return out
```

```python
from contextlib import ExitStack, contextmanager

import numpy as np

import concourse.bass as bass
from concourse import mybir

F32 = mybir.dt.float32
F32R = mybir.dt.float32r
ACT = mybir.ActivationFunctionType
ALU = mybir.AluOpType
AX = mybir.AxisListType

P = 128
D = 1024
KT = D // P
LAT, CTX = 512, 128
TOK = LAT + CTX
HALF = TOK // 2
TT = TOK // P
DEPTH = 2
HEADS, HD, DV = 8, 64, 128
PAIRS = HEADS // 2
CW = 256
EXPERTS, FF = 16, 1024
CAP_LAT, CAP_CTX = 2 * LAT // EXPERTS, 2 * CTX // EXPERTS
SLOTS = CAP_LAT + CAP_CTX
EPS = 1e-6
SCALE = HD ** -0.5
GROUPS = 4
TAPS, CPAD = 31, 15
CLEN = CPAD + LAT + CPAD + CTX + CPAD
CRUN = LAT + CPAD + CTX
PPAD = 8
PLEN = PPAD + LAT + PPAD + CTX + PPAD
PRUN = LAT + PPAD + CTX
Q0, K0, V0, POOL0, CONVA0, CONVB0 = 0, 1024, 2048, 3072, 3584, 4096
RING = 6
EW = 512

SMALL = {}
_at = 0
for _name, _n in (("rms1", 8), ("rms2", 8), ("b_ada", 48), ("pool_scale", 4), ("conv_b", 4), ("ln_g", 4),
                  ("ln_b", 4), ("b_gate", 24), ("subln", 1), ("conv_w", 4 * TAPS), ("router", 8 * 16),
                  ("lam_vec", 256), ("qkg", 256), ("qkg_swapped", 256), ("lam_init", 1), ("one_minus", 1),
                  ("pool_w", 512)):
    SMALL[_name] = (_at, _at + _n)
    _at += _n
NSMALL = _at

PER_TURN = {}


class Seen:

    def __init__(self, eng, name, settled):
        self.eng, self.name, self.n, self.base, self.settled = eng, name, {}, {}, settled

    def settle(self):
        self.eng.sem_inc(self.settled, 1)

    def __call__(self, sem, k=1):
        self.n[sem] = self.n.get(sem, 0) + k
        return self.base.get(sem, 0) + self.n[sem]

    @contextmanager
    def loop(self, what, count):
        key = f"{self.name}.{what}"
        per = PER_TURN.get(key, {})
        n, base = dict(self.n), dict(self.base)
        self.settle()
        with self.eng.Fori(0, count) as i:
            for sem in set(n) | set(per):
                b = base.get(sem, 0) + n.get(sem, 0)
                self.base[sem] = b + per[sem] * i if per.get(sem) else b
            self.n = {}
            yield i
            used = {k: v for k, v in self.n.items() if v}
            if used != per:
                PER_TURN[key] = used
                PER_TURN["changed"] = True
        self.base = base
        self.n = {s: n.get(s, 0) + count * used.get(s, 0) for s in set(n) | set(used)}


def build(nc, x_prompt, x_sample, cvecs, cache_k, cache_v, small, w_ada, w_in, w_proj_a, w_proj_b,
          w_proj_c, w_gate, w_out, w1, w3, w2, ident_in, cos_in, sin_in, inv_in, slot_in,
          y_prompt, y_sample, new_k, new_v, dbg=None):
    ctx = ExitStack()
    with ctx:
        start = (nc.sbuf_base + 63) // 64 * 64
        free = {"at": start}

        def region(nbytes):
            at = free["at"]
            free["at"] = at + (nbytes + 31) // 32 * 32
            return at

        def sb(name, shape, at, dt=F32):
            return nc.alloc_sbuf_tensor_at(name, shape, dt, offset=at)

        r_x, r_m, r_ring, r_raw, r_t2 = region(20480), region(20608), region(98304), region(16384), region(40960)
        x = sb("x", [P, KT, TOK], r_x)
        mm_ = sb("m", [P, KT, TOK], r_m)
        xtok = sb("xtok", [P, TT, D], r_m)
        sg = sb("conv_gate", [P, GROUPS, TOK], r_m)
        inv = sb("inv_count", [P, GROUPS, PRUN], r_m + 10240)
        rope_c = sb("rope_c", [P, TT * CW], r_m)
        rope_s = sb("rope_s", [P, TT * CW], r_m + 5120)
        qk_a = sb("qk_a", [P, TT * CW], r_m + 10240)
        qk_b = sb("qk_b", [P, TT * CW], r_m + 15360)
        xs = sb("xs", [P, KT, SLOTS], r_m)
        pick = sb("pick", [P, TT, SLOTS], r_m + 2560, F32R)
        gated = sb("hid_silu", [P, KT, SLOTS], r_m + 4160)
        hid = sb("hid", [P, KT, SLOTS], r_m + 6720)
        yt = sb("expert_out", [P, KT, SLOTS], r_m + 9280)
        ye_lo = sb("ye_lo", [SLOTS, D], r_m + 11840, F32R)
        ring = sb("ring", [P, RING, KT, EW], r_ring)
        h_hi = sb("h_hi", [P, KT, TOK], r_ring, F32R)
        h_lo = sb("h_lo", [P, KT, TOK], r_ring + 20480, F32R)
        w_hi = sb("w_hi", [P, 2, KT, CW], r_ring + 40960, F32R)
        w_lo = sb("w_lo", [P, 2, KT, CW], r_ring + 57344, F32R)
        ot = sb("ot", [P, HEADS, TOK], r_ring + 73728)
        at_ = sb("attn_t", [P, TT, P], r_ring + 94208)
        ck = sb("cache_k_tok", [P, CW], r_ring + 94208 + 2560)
        raw = sb("raw", [P, 2, KT, CW], r_raw)
        affw = sb("affw", [EXPERTS, TOK], r_raw)
        cum = sb("cum", [EXPERTS, TOK], r_raw + 2560)
        mask = sb("mask", [EXPERTS, TOK], r_raw + 5120)
        sigd = sb("sigd", [P, 4, HALF], r_t2 + 13728)
        prod = sb("prod", [P, 4, HALF], r_t2 + 13728 + 5120)
        zc = sb("zc", [P, GROUPS + 1, CLEN], r_t2)
        brp = sb("pool_branch", [P, GROUPS, TOK], r_t2 + 13728)
        up = sb("up", [P, GROUPS, PLEN], r_t2 + 23968)
        pt1 = sb("pool_t1", [P, PLEN], r_t2 + 34592)
        pt2 = sb("pool_t2", [P, PLEN], r_t2 + 37248)
        qk_t = sb("qk_t", [P, 2, TOK + TOK + CTX], r_t2 + 23968)
        probs = sb("probs", [P, 2, TOK], r_t2 + 23968 + 11264)
        brc = sb("conv_branch", [P, GROUPS, TOK], r_t2 + 23968)
        sigd = sb("sigd", [P, 4, HALF], r_t2 + 34208)
        prod = sb("prod", [P, 4, HALF], r_t2)
        t_hi = sb("h2tok_hi", [P, TT, D], r_t2, F32R)
        t_lo = sb("h2tok_lo", [P, TT, D], r_t2 + 20480, F32R)
        ident = sb("ident", [P, P], region(512))
        ones = sb("ones", [P, P], region(512))
        sm = sb("small", [P, NSMALL], region(4 * NSMALL))
        mods = sb("mods", [P, 48, 2], region(384))
        coef = sb("coef", [P, KT, 2], region(64))
        cs = sb("cs", [P, KT, 2], region(64))
        slot_no = sb("slot_no", [P, SLOTS], region(4 * SLOTS))
        pos = sb("pos", [P, TT, EXPERTS + 1], region(352))
        aff = sb("aff", [P, TT, EXPERTS], region(320))
        st = sb("stats", [P, 64], region(256))
        top8 = sb("top8", [EXPERTS, 8], region(32))
        r_v = region(6656)
        vb = sb("v_pair", [P, TT + 1, CW], r_v)
        row = sb("row", [P, TOK], r_v)
        row2 = sb("row2", [P, TOK], r_v + 2560)
        ye_hi = sb("ye_hi", [SLOTS, D], r_v, F32R)
        ptk = sb("pick_t", [SLOTS, TOK], r_v + 4096, F32R)
        assert free["at"] <= nc.sbuf_usable_end, (free["at"], nc.sbuf_usable_end)

        ps = ctx.enter_context(nc.psum_tensor("ps", [P, 8, 512], F32))
        flat = ps[:].rearrange("p b n -> p (b n)")
        ada_ps = ps[:, 7, 0:96].rearrange("p (m c) -> p m c", c=2)

        def small_at(name):
            a, b = SMALL[name]
            return sm[:, a:b]

        names = """raw_full0 raw_full1 raw_free0 raw_free1 hi_done split0 split1 split_free0 split_free1 proj
        set_free0 set_free1 const_in x_in small_in small_free tr_in tr_out sq ss row_a row_b row_c tnorm hnorm hready
        cs_ready ada mods_ready lam_a lam_b lam_c z_ready pads up_ready pool_in pooled poolmm pool_br table_in
        table_ready qksq qkss qksqrt qkxn qkt2 roped qkT qkT_out newk_out newv_out newk_free newv_free v_ready cache_in s_done expd
        maxd a_ready aT aT_out av o_out conv_done ln_sum ln_d ln_sq ln_var ln_sqrt ln_n branch_c o_sq o_ss o_var
        o_sqrt o_norm sig merged xo_done logits rt_a rt_b aff_r affT topk posT pos_r h2tok_ps h2tok_hi h2tok_lo
        wfull0 wfull1 wfull2 wfull3 wfull4 wfull5 wfree hh silu hidd picked pt_ps pt_out xs_ps xs_out yt_ps yt_out
        ye_ps ye_hi ye_lo scat scat_out layer_done m_ready ada_out out_ps out_sb y_out attn_free d_done
        dve act pool settled""".split()
        s = {n: ctx.enter_context(nc.semaphore("s_" + n)) for n in names}
        assert len(set(names)) == len(names)

        block = ctx.enter_context(nc.Block())
        xin = (x_sample, x_prompt)
        yout = (y_sample, y_prompt)

        @block.sync
        def _(sp):
            seen = Seen(sp, "sp", s["settled"])
            sp.dma_start(ident[:], ident_in).then_inc(s["const_in"], 16)
            sp.dma_start(slot_no[:], slot_in).then_inc(s["const_in"], 16)
            sp.dma_start(cs[:], cvecs).then_inc(s["const_in"], 16)
            sp.dma_start(xtok[:, 0:4, :], x_sample[0].rearrange("(t p) d -> p t d", p=P)).then_inc(s["x_in"], 16)
            sp.dma_start(xtok[:, 4, :], x_prompt[0]).then_inc(s["x_in"], 16)
            sp.sem_inc(s["raw_free0"], 1)
            sp.sem_inc(s["raw_free1"], 1)
            sp.sem_inc(s["wfree"], RING)

            def chunk(slot, *parts):
                sp.wait_ge(s[f"raw_free{slot}"], seen(f"raw_free{slot}"))
                for dst, src in parts:
                    sp.dma_start(dst, src).then_inc(s[f"raw_full{slot}"], 16)

            def wide(slot, src):
                chunk(slot, (raw[:, slot, 0:4, :], src[:, 0:4, :]), (raw[:, slot, 4:8, :], src[:, 4:8, :]))

            ada_v = w_ada.rearrange("l (k p) (c n) -> l c p k n", p=P, n=CW)
            in_v = w_in.rearrange("l (k p) (c n) -> l c p k n", p=P, n=CW)
            in_h = w_in.rearrange("l (k p) (c n) -> l c p k n", p=P, n=P)
            gate_v = w_gate.rearrange("l (k p) (c n) -> l c p k n", p=P, n=CW)
            pa_v = w_proj_a.rearrange("l (k p) (c n) -> l c p k n", p=P, n=CW)
            pb_v = w_proj_b.rearrange("l (k p) (c n) -> l c p k n", p=P, n=CW)
            pc_v = w_proj_c.rearrange("l (k p) (c n) -> l c p k n", p=P, n=CW)
            out_v = w_out.rearrange("l (k p) (c n) -> l c p k n", p=P, n=CW)
            ex_v = [w.rearrange("l e (k p) n -> l e p k n", p=P) for w in (w1, w3, w2)]
            with seen.loop("layer", DEPTH) as l:
                with seen.loop("ada1", 4) as i:
                    for u in range(2):
                        wide(u, ada_v[l, 2 * i + u])
                for n, c0 in enumerate((CONVB0, CONVA0, POOL0)):
                    for u in range(2):
                        wide(u, in_v[l, c0 // CW + u])
                with seen.loop("ada2", 2) as i:
                    for u in range(2):
                        wide(u, ada_v[l, 2 * i + u + 8])
                with seen.loop("pair", PAIRS) as g:
                    for u in range(2):
                        chunk(0, (raw[:, 0, :, 0:P], in_h[l, Q0 // P + 2 * g + u]),
                              (raw[:, 0, :, P:CW], in_h[l, K0 // P + 2 * g + u]))
                        wide(1, ada_v[l, 3 * g + 12 + u])
                    wide(0, in_v[l, g + V0 // CW])
                    wide(1, ada_v[l, 3 * g + 14])
                with seen.loop("merge", 4) as n:
                    wide(0, gate_v[l, n])
                    wide(1, pa_v[l, n])
                    for u, (w, gate) in enumerate(((pb_v, 4), (pc_v, 8))):
                        wide(0, gate_v[l, n + gate])
                        src = w[l, n]
                        chunk(1, (raw[:, 1, 0:2, :], src[:, 0:2, :]), (raw[:, 1, 2:4, :], src[:, 2:4, :]))
                with seen.loop("out", 2) as i:
                    for u in range(2):
                        wide(u, out_v[l, 2 * i + u])
                sp.wait_ge(s["d_done"], seen("d_done"))
                with seen.loop("experts", EXPERTS) as e:
                    for n, (w, c) in enumerate(((0, 0), (1, 0), (0, 1), (1, 1), (2, 0), (2, 1))):
                        sp.wait_ge(s["wfree"], seen("wfree"))
                        sp.dma_start(ring[:, n], ex_v[w][l, e][:, :, c * EW:(c + 1) * EW]).then_inc(s[f"wfull{n}"], 16)
            y_v = y_sample[0].rearrange("(t p) d -> p t d", p=P)
            for t in range(TT):
                sp.wait_ge(s["out_sb"], seen("out_sb"))
                sp.dma_start(y_v[:, t] if t < 4 else y_prompt[0], xtok[:, t, :]).then_inc(s["y_out"], 16)
            sp.wait_ge(s["y_out"], 16 * TT)

        @block.gpsimd
        def _(pool):
            seen = Seen(pool, "pool", s["settled"])
            nc.gpsimd.memset(ones[:], 1.0).then_inc(s["const_in"], 16)
            nk_v = new_k.rearrange("b l s h m d -> (b l) h s (m d)")
            nv_v = new_v.rearrange("b l s (g h) d -> (b l) g s (h d)", h=2)
            ck_v = cache_k.rearrange("b l s (g h) m d -> (b l) g s (h m d)", h=2)
            cv_v = cache_v.rearrange("b l s (g h) d -> (b l) g s (h d)", h=2)
            pool.sem_inc(s["small_free"], 1)
            pool.sem_inc(s["attn_free"], 1)
            pool.sem_inc(s["newk_free"], 1)
            pool.sem_inc(s["newv_free"], 1)

            def link(ins):
                ins.then_inc(s["pool"], 1)
                pool.wait_ge(s["pool"], seen("pool"))

            with seen.loop("layer", DEPTH) as l:
                pool.wait_ge(s["small_free"], seen("small_free"))
                seen.settle()
                pool.dma_start(sm[:], small[l]).then_inc(s["small_in"], 16)
                pool.wait_ge(s["hready"], seen("hready"))
                seen.settle()
                pool.dma_start(inv[:], inv_in.partition_broadcast(P)).then_inc(s["pool_in"], 16)
                for a in (0, CPAD + LAT, CLEN - CPAD):
                    nc.gpsimd.memset(zc[:, 1:, a:a + CPAD], 0.0)
                for n, a in enumerate((0, PPAD + LAT, PLEN - PPAD)):
                    ins = nc.gpsimd.memset(up[:, :, a:a + PPAD], 0.0)
                ins.then_inc(s["pads"], 1)
                pool.wait_ge(s["pads"], seen("pads"))
                pool.wait_ge(s["pool_in"], seen("pool_in", 16))
                pool.wait_ge(s["up_ready"], seen("up_ready", 2))
                for g in range(GROUPS):
                    src, dst = up[:, g], pt1
                    link(nc.gpsimd.tensor_tensor(dst[:, 1:PLEN], src[:, 0:PLEN - 1], src[:, 1:PLEN], ALU.add))
                    lo, hi = 1, PLEN
                    cur, nxt = pt1, pt2
                    for j in range(g):
                        w = 1 << j
                        lo, hi = lo + w, hi - w
                        link(nc.gpsimd.tensor_tensor(nxt[:, lo:hi], cur[:, lo - w:hi - w], cur[:, lo + w:hi + w], ALU.add))
                        cur, nxt = nxt, cur
                    link(nc.gpsimd.tensor_tensor(nxt[:, PPAD:PPAD + PRUN], cur[:, PPAD:PPAD + PRUN], inv[:, g], ALU.mult))
                    nc.gpsimd.tensor_tensor(up[:, g, PPAD:PPAD + PRUN], nxt[:, PPAD:PPAD + PRUN],
                                            up[:, g, PPAD:PPAD + PRUN], ALU.subtract).then_inc(s["pooled"], 1)
                    pool.wait_ge(s["pooled"], seen("pooled"))
                pool.wait_ge(s["z_ready"], seen("z_ready", 4))
                seen.settle()
                pool.dma_start(rope_c[:], cos_in).then_inc(s["table_in"], 16)
                seen.settle()
                pool.dma_start(rope_s[:], sin_in).then_inc(s["table_in"], 16)
                with seen.loop("pair", PAIRS) as g:
                    pool.wait_ge(s["attn_free"], seen("attn_free"))
                    seen.settle()
                    pool.dma_start(ck[:], ck_v[l, g]).then_inc(s["cache_in"], 16)
                    seen.settle()
                    pool.dma_start(vb[:, 4, :], cv_v[l, g]).then_inc(s["cache_in"], 16)
                    for u in range(2):
                        pool.wait_ge(s["qkt2"], seen("qkt2"))
                        nc.gpsimd.tensor_tensor(qk_a[:], qk_a[:], qk_b[:], ALU.add).then_inc(s["roped"], 1)
                        pool.wait_ge(s["roped"], seen("roped"))
                        seen.settle()
                        pool.dma_start(nk_v[l, 2 * g + u], qk_a[:, 4 * CW + P:5 * CW]).then_inc(s["newk_out"], 16)
                        pool.wait_ge(s["newk_out"], seen("newk_out", 16))
                        pool.sem_inc(s["newk_free"], 1)
                    pool.wait_ge(s["v_ready"], seen("v_ready", 2))
                    seen.settle()
                    pool.dma_start(nv_v[l, g], vb[:, 5, :]).then_inc(s["newv_out"], 16)
                    pool.wait_ge(s["newv_out"], seen("newv_out", 16))
                    pool.sem_inc(s["newv_free"], 1)

        def qkT_evac(act, seen, u):
            act.wait_ge(s["qkT"], seen("qkT"))
            nc.scalar.copy(qk_t[:, u, 0:2 * TOK].rearrange("p (a n) -> p a n", a=2)[:, :, 0:LAT], ps[:, 6:8, :])
            nc.scalar.copy(qk_t[:, u, :].rearrange("p (a n) -> p a n", n=P)[:, 4:11:6, :],
                           ps[:, 2 + 3 * u, 256:512].rearrange("p (a n) -> p a n", a=2)).then_inc(s["qkT_out"], 1)

        def exp_unit(act, seen, t):
            for m in range(2):
                act.wait_ge(s["maxd"], seen("maxd"))
                if m == 0:
                    act.wait_ge(s["aT"], seen("aT"))
                src = ps[:, 3 * m:3 * m + 2, 0:HALF] if t < 4 else ps[:, 3 * m, 0:CTX]
                dst = probs[:, m].rearrange("p (a n) -> p a n", a=2) if t < 4 else probs[:, m, 0:CTX]
                nc.scalar.activation(dst, src, ACT.Exp, scale=SCALE, bias=st[:, 36 + m:37 + m],
                                     accum_out=st[:, 40 + m:41 + m]).then_inc(s["expd"], 1)
            act.wait_ge(s["aT"], seen("aT", 0) + 1)
            act.wait_ge(s["av"], seen("av"))
            if t < 4:
                nc.scalar.copy(at_[:].rearrange("p a n -> p (a n)"), flat[:, 6 * 512:6 * 512 + TOK]).then_inc(s["aT_out"], 1)
            else:
                nc.scalar.copy(at_[:, 0], ps[:, 6, 0:P]).then_inc(s["aT_out"], 1)

        @block.scalar
        def _(act):
            seen = Seen(act, "act", s["settled"])

            def link(ins):
                ins.then_inc(s["act"], 1)
                act.wait_ge(s["act"], seen("act"))

            def split_high(slot, rslot):
                act.wait_ge(s[f"raw_full{rslot}"], seen(f"raw_full{rslot}", 32))
                act.wait_ge(s[f"split_free{slot}"], seen(f"split_free{slot}"))
                nc.scalar.copy(w_hi[:, slot], raw[:, rslot]).then_inc(s["hi_done"], 1)

            def skip_raw(rslot, n=1):
                seen(f"raw_full{rslot}", 32 * n)

            def norm(shift):
                for k in range(KT):
                    nc.scalar.activation(mm_[:, k], x[:, k], ACT.Square).then_inc(s["sq"], 1)
                act.wait_ge(s["row_a"], seen("row_a"))
                nc.scalar.activation(row[:], row[:], ACT.Sqrt).then_inc(s["row_b"], 1)
                act.wait_ge(s["mods_ready"], seen("mods_ready"))
                for k in range(KT):
                    act.wait_ge(s["tnorm"], seen("tnorm"))
                    for c, (a, b) in ((1, (0, LAT)), (0, (LAT, TOK))):
                        ins = nc.scalar.activation(mm_[:, k, a:b], mm_[:, k, a:b], ACT.Identity,
                                                   scale=coef[:, k, c:c + 1], bias=mods[:, shift + k, c:c + 1])
                    ins.then_inc(s["hnorm"], 1)

            act.wait_ge(s["const_in"], 64)
            nc.scalar.activation(cs[:], cs[:], ACT.Silu).then_inc(s["cs_ready"], 1)
            for k in range(KT):
                act.wait_ge(s["tr_in"], seen("tr_in"))
                b = 2 * (k % 2)
                nc.scalar.copy(x[:, k], flat[:, b * 512:b * 512 + TOK]).then_inc(s["tr_out"], 1)
            act.wait_ge(s["tr_out"], seen("tr_out", KT))
            with seen.loop("layer", DEPTH) as l:
                skip_raw(0, 4)
                skip_raw(1, 4)
                norm(0)
                for k in range(KT):
                    act.wait_ge(s["hnorm"], seen("hnorm"))
                    ins = nc.scalar.copy(h_hi[:, k], mm_[:, k])
                    ins.then_inc(s["row_c"], 1)
                act.wait_ge(s["lam_a"], seen("lam_a"))
                nc.scalar.activation(st[:, 2:4], st[:, 0:2], ACT.Exp).then_inc(s["lam_b"], 1)
                act.wait_ge(s["pads"], seen("pads"))
                act.wait_ge(s["hready"], seen("hready"))
                split_high(0, 0)
                split_high(1, 1)
                for n in range(3):
                    for u in range(2):
                        if n < 2:
                            split_high(u, u)
                        act.wait_ge(s["proj"], seen("proj"))
                        lat = ps[:, 4 * u:4 * u + 4, :].rearrange("p (j h) q -> p j h q", h=2)[:, :, 0, :]
                        cx = ps[:, 4 * u:4 * u + 4, 0:CTX].rearrange("p (j h) q -> p j h q", h=2)[:, :, 1, :]
                        if n == 0:
                            nc.scalar.activation(sg[:, 2 * u:2 * u + 2, 0:LAT], lat, ACT.Sigmoid)
                            nc.scalar.activation(sg[:, 2 * u:2 * u + 2, LAT:TOK], cx, ACT.Sigmoid).then_inc(s[f"set_free{u}"], 1)
                        if n == 2:
                            nc.scalar.copy(up[:, 2 * u:2 * u + 2, PPAD:PPAD + LAT], lat)
                            nc.scalar.copy(up[:, 2 * u:2 * u + 2, 2 * PPAD + LAT:2 * PPAD + TOK], cx).then_inc(s["up_ready"], 1)
                skip_raw(0, 2)
                skip_raw(1, 2)
                for g in range(GROUPS):
                    act.wait_ge(s["poolmm"], seen("poolmm"))
                    b = 2 * (g % 2)
                    nc.scalar.mul(brp[:, g], flat[:, b * 512:b * 512 + TOK],
                                  small_at("pool_scale")[:, g:g + 1]).then_inc(s["pool_br"], 1)
                with seen.loop("pair", PAIRS) as g:
                    split_high(0, 0)
                    split_high(1, 0)
                    skip_raw(1, 2)
                    for u in range(2):
                        act.wait_ge(s["proj"], seen("proj"))
                        act.wait_ge(s["newk_free"], seen("newk_free"))
                        nc.scalar.activation(qk_a[:], flat[:, 1536 * u:1536 * u + 1280], ACT.Square).then_inc(s["qksq"], 1)
                        act.wait_ge(s["qkss"], seen("qkss"))
                        nc.scalar.activation(st[:, 8:28], st[:, 8:28], ACT.Sqrt).then_inc(s["qksqrt"], 1)
                        if u == 0:
                            split_high(0, 0)
                            skip_raw(1)
                            qkT_evac(act, seen, 0)
                    act.wait_ge(s["proj"], seen("proj"))
                    act.wait_ge(s["newv_free"], seen("newv_free"))
                    nc.scalar.copy(vb[:, 0:4, :], flat[:, 0:1024].rearrange("p (t n) -> p t n", n=CW)).then_inc(s["v_ready"], 1)
                    nc.scalar.copy(vb[:, 5, :], flat[:, 1024:1280]).then_inc(s["v_ready"], 1)
                    qkT_evac(act, seen, 1)
                    act.wait_ge(s["qkT"], seen("qkT"))
                    nc.scalar.copy(qk_t[:, :, 1152:1280], ps[:, 6, 0:CW].rearrange("p (u n) -> p u n", u=2)).then_inc(s["qkT_out"], 1)
                    act.wait_ge(s["qkT_out"], seen("qkT_out", 3))
                    for u in range(2):
                        for t in range(TT):
                            exp_unit(act, seen, t)
                        act.wait_ge(s["av"], seen("av", 0) + 1)
                        nc.scalar.copy(ot[:, 2 * g + u, 0:LAT], ps[:, 2, :])
                        nc.scalar.copy(ot[:, 2 * g + u, LAT:TOK], ps[:, 5, 0:CTX]).then_inc(s["o_out"], 1)
                act.wait_ge(s["o_out"], seen("o_out", 2 * PAIRS))
                act.wait_ge(s["newk_free"], seen("newk_free", 0) + 1)
                act.wait_ge(s["newv_free"], seen("newv_free", 0) + 1)
                for h in range(HEADS):
                    nc.scalar.activation(mm_[:, h], ot[:, h], ACT.Square).then_inc(s["o_sq"], 1)
                for h in range(HEADS):
                    act.wait_ge(s["o_var"], seen("o_var"))
                    nc.scalar.activation(row[:], row[:], ACT.Sqrt).then_inc(s["o_sqrt"], 1)
                act.wait_ge(s["ln_d"], seen("ln_d"))
                for j in range(GROUPS):
                    nc.scalar.activation(mm_[:, j, 0:LAT], zc[:, j, 0:LAT], ACT.Square)
                    nc.scalar.activation(mm_[:, j, LAT:TOK], zc[:, j, LAT + CPAD:CRUN], ACT.Square).then_inc(s["ln_sq"], 1)
                act.wait_ge(s["ln_var"], seen("ln_var"))
                nc.scalar.activation(row2[:], row2[:], ACT.Sqrt).then_inc(s["ln_sqrt"], 1)
                act.wait_ge(s["ln_n"], seen("ln_n"))
                for j in range(GROUPS):
                    for a, b, z in ((0, LAT, 0), (LAT, TOK, CPAD)):
                        ins = nc.scalar.activation(brc[:, j, a:b], zc[:, j, a + z:b + z], ACT.Silu,
                                                   scale=small_at("ln_g")[:, j:j + 1], bias=small_at("ln_b")[:, j:j + 1])
                    ins.then_inc(s["branch_c"], 1)
                act.wait_ge(s["branch_c"], seen("branch_c", GROUPS))
                with seen.loop("merge", 4) as n:
                    for b in range(3):
                        split_high(b % 2, 0)
                        skip_raw(1)
                        act.wait_ge(s["proj"], seen("proj"))
                        act.wait_ge(s["merged"], seen("merged"))
                        for j in range(2):
                            for h in range(2):
                                ins = nc.scalar.activation(sigd[:, 2 * j + h], ps[:, 2 * j + h, 0:HALF], ACT.Sigmoid,
                                                           bias=sm[:, bass.ds(2 * n + (SMALL["b_gate"][0] + 8 * b + j), 1)])
                        ins.then_inc(s["sig"], 1)
                        act.wait_ge(s["sig"], seen("sig"))
                        seen("proj")
                skip_raw(0, 2)
                skip_raw(1, 2)
                seen("proj", 4)
                act.wait_ge(s["xo_done"], seen("xo_done"))
                norm(24)
                seen("hnorm", KT)
                act.wait_ge(s["rt_a"], seen("rt_a"))
                nc.scalar.activation(aff[:], aff[:], ACT.Exp).then_inc(s["rt_b"], 1)
                for t in range(TT):
                    act.wait_ge(s["h2tok_ps"], seen("h2tok_ps"))
                    b = 2 * (t % 2)
                    nc.scalar.copy(t_hi[:, t], flat[:, b * 512:b * 512 + D]).then_inc(s["h2tok_hi"], 1)
                act.wait_ge(s["xs_ps"], seen("xs_ps"))
                nc.scalar.copy(xs[:], ps[:, 4:6, :].rearrange("p b (k n) -> p (b k) n", k=4)[:, :, 0:SLOTS]).then_inc(s["xs_out"], 1)
                with seen.loop("experts", EXPERTS) as e:
                    for f in range(2):
                        act.wait_ge(s["hh"], seen("hh", 2))
                        nc.scalar.activation(gated[:, 4 * f:4 * f + 4], ps[:, 2 * f, :].rearrange("p (k n) -> p k n", k=4)[:, :, 0:SLOTS],
                                             ACT.Silu).then_inc(s["silu"], 1)
                    act.wait_ge(s["pt_ps"], seen("pt_ps"))
                    nc.scalar.copy(st[0:SLOTS, 32:33], ps[0:SLOTS, 7, P:P + 1])
                    nc.scalar.copy(ptk[:], flat[0:SLOTS, 6 * 512:6 * 512 + TOK]).then_inc(s["pt_out"], 1)
                    for f in range(2):
                        act.wait_ge(s["yt_ps"], seen("yt_ps"))
                        nc.scalar.copy(yt[:, 4 * f:4 * f + 4], ps[:, 4 + f, :].rearrange("p (k n) -> p k n", k=4)[:, :, 0:SLOTS]).then_inc(s["yt_out"], 1)
                    act.wait_ge(s["ye_ps"], seen("ye_ps"))
                    act.wait_ge(s["pt_out"], seen("pt_out"))
                    nc.scalar.activation(ye_hi[:], flat[0:SLOTS, 6 * 512:8 * 512], ACT.Copy, scale=st[0:SLOTS, 32:33]).then_inc(s["ye_hi"], 1)
                    act.wait_ge(s["xs_ps"], seen("xs_ps"))
                    nc.scalar.copy(xs[:], ps[:, 4:6, :].rearrange("p b (k n) -> p (b k) n", k=4)[:, :, 0:SLOTS]).then_inc(s["xs_out"], 1)
                act.wait_ge(s["xs_out"], seen("xs_out", EXPERTS + 1))
                act.wait_ge(s["layer_done"], seen("layer_done"))
            for t in range(TT):
                act.wait_ge(s["out_ps"], seen("out_ps"))
                b = 2 * (t % 2)
                nc.scalar.copy(xtok[:, t], flat[:, b * 512:b * 512 + D]).then_inc(s["out_sb"], 1)

        @block.vector
        def _(dve):
            seen = Seen(dve, "dve", s["settled"])

            def link(ins):
                ins.then_inc(s["dve"], 1)
                dve.wait_ge(s["dve"], seen("dve"))

            def link2(ins):
                ins.then_inc(s["ada_out"], 1)
                dve.wait_ge(s["ada_out"], seen("ada_out"))

            def add_mods_of(a):
                dve.wait_ge(s["ada"], seen("ada"))
                b0 = SMALL["b_ada"][0]
                nc.vector.tensor_tensor(mods[:, bass.ds(2 * a, 2), :], ada_ps[:, 0:2, :],
                                        sm[:, bass.ds(2 * a + b0, 2)].unsqueeze(2).to_broadcast([P, 2, 2]), ALU.add).then_inc(s["ada_out"], 1)
                seen("ada_out")

            def split_low(slot, rslot):
                dve.wait_ge(s["hi_done"], seen("hi_done"))
                nc.vector.tensor_tensor(w_lo[:, slot], raw[:, rslot], w_hi[:, slot].bitcast(F32),
                                        ALU.subtract).then_inc(s[f"split{slot}"], 1)
                dve.wait_ge(s[f"split{slot}"], seen(f"split{slot}"))
                dve.sem_inc(s[f"raw_free{rslot}"], 1)

            def norm():
                dve.wait_ge(s["ss"], seen("ss"))
                nc.vector.tensor_scalar(row[:].rearrange("p (a n) -> p a n", a=2), ps[:, 0:2, 0:HALF], 1.0 / D, EPS,
                                        ALU.mult, ALU.add).then_inc(s["row_a"], 1)
                dve.wait_ge(s["row_b"], seen("row_b"))
                link(nc.vector.reciprocal(row[:], row[:]))
                for k in range(KT):
                    nc.vector.tensor_tensor(mm_[:, k], x[:, k], row[:], ALU.mult).then_inc(s["tnorm"], 1)

            def coefficients(scale, g):
                for c in range(2):
                    ins = nc.vector.scalar_tensor_tensor(coef[:, :, c], mods[:, scale:scale + KT, c], 1.0, small_at(g), ALU.add, ALU.mult)
                ins.then_inc(s["mods_ready"], 1)

            def add_mods(a, b):
                link2(nc.vector.tensor_tensor(mods[:, a:b, :], ada_ps[:, a:b, :],
                                             small_at("b_ada")[:, a:b].unsqueeze(2).to_broadcast([P, b - a, 2]), ALU.add))

            dve.sem_inc(s["set_free0"], 1)
            dve.sem_inc(s["set_free1"], 1)
            dve.sem_inc(s["merged"], 1)
            with seen.loop("layer", DEPTH) as l:
                dve.wait_ge(s["small_in"], seen("small_in", 16))
                dve.wait_ge(s["ada"], seen("ada", 8))
                add_mods(0, 16)
                coefficients(8, "rms1")
                lv = small_at("lam_vec").rearrange("p (a b n) -> p a b n", a=2, b=2)
                link(nc.vector.tensor_tensor(st[:, 0:2], st[:, 0:2], st[:, 0:2], ALU.bypass) if False else
                     nc.vector.tensor_tensor(row2[:, 0:128].rearrange("p (a n) -> p a n", a=2), lv[:, :, 0, :], lv[:, :, 1, :], ALU.mult))
                nc.vector.tensor_reduce(st[:, 0:2], row2[:, 0:128].rearrange("p (a n) -> p a n", a=2), AX.X, ALU.add).then_inc(s["lam_a"], 1)
                norm()
                for k in range(KT):
                    dve.wait_ge(s["row_c"], seen("row_c"))
                    ins = nc.vector.tensor_tensor(h_lo[:, k], mm_[:, k], h_hi[:, k].bitcast(F32), ALU.subtract)
                ins.then_inc(s["hready"], 1)
                dve.wait_ge(s["lam_b"], seen("lam_b"))
                link(nc.vector.scalar_tensor_tensor(st[:, 4:5], st[:, 3:4], small_at("lam_init"), st[:, 2:3], ALU.subtract, ALU.subtract))
                link(nc.vector.tensor_tensor(st[:, 5:6], small_at("subln"), small_at("one_minus"), ALU.mult))
                split_low(0, 0)
                split_low(1, 1)
                for n in range(3):
                    for u in range(2):
                        if n < 2:
                            split_low(u, u)
                        if n == 1:
                            dve.wait_ge(s["proj"], seen("proj", 3 if u == 0 else 1))
                            lat = ps[:, 4 * u:4 * u + 4, :].rearrange("p (j h) q -> p j h q", h=2)[:, :, 0, :]
                            cx = ps[:, 4 * u:4 * u + 4, 0:CTX].rearrange("p (j h) q -> p j h q", h=2)[:, :, 1, :]
                            if u == 0:
                                dve.wait_ge(s["pads"], seen("pads"))
                            nc.vector.tensor_tensor(zc[:, 2 * u + 1:2 * u + 3, CPAD:CPAD + LAT], lat, sg[:, 2 * u:2 * u + 2, 0:LAT], ALU.mult).then_inc(s["z_ready"], 1)
                            nc.vector.tensor_tensor(zc[:, 2 * u + 1:2 * u + 3, 2 * CPAD + LAT:CLEN - CPAD], cx, sg[:, 2 * u:2 * u + 2, LAT:TOK], ALU.mult).then_inc(s["z_ready"], 1)
                            dve.wait_ge(s["z_ready"], seen("z_ready", 2))
                            dve.sem_inc(s[f"set_free{u}"], 1)
                seen("proj", 2)
                dve.wait_ge(s["ada"], seen("ada", 4))
                add_mods(16, 24)
                dve.wait_ge(s["table_in"], seen("table_in", 32))
                for tab, g in ((rope_c, "qkg"), (rope_s, "qkg_swapped")):
                    v = tab[:].rearrange("p (t n) -> p t n", n=CW)
                    link(nc.vector.tensor_tensor(v, v, small_at(g).unsqueeze(1).to_broadcast([P, TT, CW]), ALU.mult))

                with seen.loop("pair", PAIRS) as g:
                    taps = [0]

                    def conv(n):
                        for _ in range(n):
                            j = taps[0]
                            if j == TAPS:
                                return
                            w = sm[:, bass.ds(TAPS * g + (SMALL["conv_w"][0] + j), 1)]
                            src = zc[:, bass.ds(g + 1, 1), j:j + CRUN].rearrange("p a n -> p (a n)")
                            dst = zc[:, bass.ds(g, 1), 0:CRUN].rearrange("p a n -> p (a n)")
                            if j == 0:
                                link(nc.vector.tensor_scalar(dst, src, w, sm[:, bass.ds(g + SMALL["conv_b"][0], 1)], ALU.mult, ALU.add))
                            else:
                                link(nc.vector.scalar_tensor_tensor(dst, src, w, dst, ALU.mult, ALU.add))
                            taps[0] += 1

                    add_mods_of(3 * g + 12)
                    split_low(0, 0)
                    split_low(1, 0)
                    seen("proj", 3)
                    for u in range(2):
                        main = flat[:, 1536 * u:1536 * u + 1280]
                        dve.wait_ge(s["qksq"], seen("qksq"))
                        link(nc.vector.tensor_reduce(st[:, 8:28], qk_a[:].rearrange("p (a n) -> p a n", n=HD), AX.X, ALU.add))
                        nc.vector.tensor_scalar(st[:, 8:28], st[:, 8:28], 1.0 / HD, EPS, ALU.mult, ALU.add).then_inc(s["qkss"], 1)
                        dve.wait_ge(s["qksqrt"], seen("qksqrt"))
                        link(nc.vector.reciprocal(st[:, 8:28], st[:, 8:28]))
                        main3 = main.rearrange("p (a n) -> p a n", n=HD)
                        link(nc.vector.tensor_tensor(main3, main3, st[:, 8:28].unsqueeze(2).to_broadcast([P, 20, HD]), ALU.mult))
                        nc.vector.tensor_tensor(qk_a[:], main, rope_c[:], ALU.mult)
                        m4 = main.rearrange("p (a r n) -> p a r n", r=2, n=16)
                        b4 = qk_b[:].rearrange("p (a r n) -> p a r n", r=2, n=16)
                        s4 = rope_s[:].rearrange("p (a r n) -> p a r n", r=2, n=16)
                        nc.vector.tensor_tensor(b4[:, :, 0], m4[:, :, 1], s4[:, :, 0], ALU.mult)
                        nc.vector.tensor_tensor(b4[:, :, 1], m4[:, :, 0], s4[:, :, 1], ALU.mult).then_inc(s["qkt2"], 1)
                        if u == 0:
                            add_mods_of(3 * g + 13)
                            split_low(0, 0)
                    add_mods_of(3 * g + 14)
                    for u in range(2):
                        for t in range(TT):
                            n = TOK if t < 4 else CTX
                            for m in range(2):
                                dve.wait_ge(s["s_done"], seen("s_done"))
                                src = ps[:, 3 * m:3 * m + 2, 0:HALF] if t < 4 else ps[:, 3 * m, 0:CTX]
                                link(nc.vector.tensor_reduce(st[:, 44 + m:45 + m], src, AX.XY if t < 4 else AX.X, ALU.max))
                                nc.vector.tensor_scalar(st[:, 36 + m:37 + m], st[:, 44 + m:45 + m], -SCALE, None, ALU.mult).then_inc(s["maxd"], 1)
                            conv(2)
                            dve.wait_ge(s["expd"], seen("expd", 2))
                            link(nc.vector.reciprocal(st[:, 48:50], st[:, 40:42]))
                            link(nc.vector.tensor_scalar(st[:, 50:51], st[:, 49:50], st[:, 4:5], None, ALU.mult))
                            link(nc.vector.tensor_scalar(probs[:, 1, 0:n], probs[:, 1, 0:n], st[:, 50:51], None, ALU.mult))
                            nc.vector.scalar_tensor_tensor(probs[:, 0, 0:n], probs[:, 0, 0:n], st[:, 48:49], probs[:, 1, 0:n],
                                                           ALU.mult, ALU.add).then_inc(s["a_ready"], 1)
                            conv(1 if (u, t) != (1, 4) else TAPS)
                    assert taps[0] == TAPS
                nc.vector.tensor_copy(st[:, 60:61], st[:, 4:5]).then_inc(s["conv_done"], 1)
                for h in range(HEADS):
                    b = 2 * (h % 2)
                    dve.wait_ge(s["o_ss"], seen("o_ss"))
                    nc.vector.tensor_scalar(row[:].rearrange("p (a n) -> p a n", a=2), ps[:, b:b + 2, 0:HALF], 1.0 / DV, EPS,
                                            ALU.mult, ALU.add).then_inc(s["o_var"], 1)
                    dve.wait_ge(s["o_sqrt"], seen("o_sqrt"))
                    link(nc.vector.reciprocal(row[:], row[:]))
                    nc.vector.scalar_tensor_tensor(ot[:, h], ot[:, h], st[:, 5:6], row[:], ALU.mult, ALU.mult).then_inc(s["o_norm"], 1)
                    dve.wait_ge(s["o_norm"], seen("o_norm"))
                dve.wait_ge(s["ln_sum"], seen("ln_sum"))
                link(nc.vector.tensor_scalar(row2[:], flat[:, 4 * 512:4 * 512 + TOK], 1.0 / 512, None, ALU.mult))
                for j in range(GROUPS):
                    nc.vector.tensor_tensor(zc[:, j, 0:LAT], zc[:, j, 0:LAT], row2[:, 0:LAT], ALU.subtract)
                    ins = nc.vector.tensor_tensor(zc[:, j, LAT + CPAD:CRUN], zc[:, j, LAT + CPAD:CRUN], row2[:, LAT:TOK], ALU.subtract)
                ins.then_inc(s["ln_d"], 1)
                dve.wait_ge(s["ln_sum"], seen("ln_sum"))
                dve.wait_ge(s["ln_d"], seen("ln_d"))
                nc.vector.tensor_scalar(row2[:], flat[:, 6 * 512:6 * 512 + TOK], 1.0 / 512, EPS, ALU.mult, ALU.add).then_inc(s["ln_var"], 1)
                dve.wait_ge(s["ln_sqrt"], seen("ln_sqrt"))
                link(nc.vector.reciprocal(row2[:], row2[:]))
                for j in range(GROUPS):
                    nc.vector.tensor_tensor(zc[:, j, 0:LAT], zc[:, j, 0:LAT], row2[:, 0:LAT], ALU.mult)
                    ins = nc.vector.tensor_tensor(zc[:, j, LAT + CPAD:CRUN], zc[:, j, LAT + CPAD:CRUN], row2[:, LAT:TOK], ALU.mult)
                ins.then_inc(s["ln_n"], 1)
                merged4 = mm_[:].rearrange("p (n j) (h q) -> p n (j h) q", j=2, h=2)
                dve.wait_ge(s["branch_c"], seen("branch_c", GROUPS))
                with seen.loop("merge", 4) as n:
                    for b in range(3):
                        split_low(b % 2, 0)
                        dve.wait_ge(s["sig"], seen("sig"))
                        dve.sem_inc(s["set_free0"], 1)
                        dve.wait_ge(s["proj"], seen("proj", 2))
                        if b == 0:
                            nc.vector.tensor_tensor(merged4[:, n], ps[:, 4:8, 0:HALF], sigd[:], ALU.mult).then_inc(s["merged"], 1)
                            dve.wait_ge(s["merged"], seen("merged") + 1)
                        else:
                            nc.vector.tensor_tensor(prod[:], ps[:, 4:8, 0:HALF], sigd[:], ALU.mult).then_inc(s["merged"], 1)
                            dve.wait_ge(s["merged"], seen("merged") + 1)
                            link(nc.vector.tensor_tensor(merged4[:, n], merged4[:, n], prod[:], ALU.add))
                        dve.sem_inc(s["set_free1"], 1)
                dve.sem_inc(s["m_ready"], 1)
                for c in range(4):
                    u = c % 2
                    dve.wait_ge(s["proj"], seen("proj"))
                    for j in range(2):
                        ct = 2 * c + j
                        nc.vector.scalar_tensor_tensor(x[:, ct, 0:LAT], ps[:, 4 * u + 2 * j, :], mods[:, 16 + ct, 1:2],
                                                       x[:, ct, 0:LAT], ALU.mult, ALU.add)
                        ins = nc.vector.scalar_tensor_tensor(x[:, ct, LAT:TOK], ps[:, 4 * u + 2 * j + 1, 0:CTX], mods[:, 16 + ct, 0:1],
                                                             x[:, ct, LAT:TOK], ALU.mult, ALU.add)
                    link(ins)
                    dve.sem_inc(s[f"set_free{u}"], 1)
                dve.sem_inc(s["xo_done"], 1)
                coefficients(32, "rms2")
                norm()
                dve.wait_ge(s["logits"], seen("logits"))
                lg = ps[:, 4, 0:TT * EXPERTS].rearrange("p (t e) -> p t e", e=EXPERTS)
                link(nc.vector.tensor_reduce(st[:, 8:13], lg, AX.X, ALU.max))
                nc.vector.tensor_tensor(aff[:], lg, st[:, 8:13].unsqueeze(2).to_broadcast([P, TT, EXPERTS]), ALU.subtract).then_inc(s["rt_a"], 1)
                dve.wait_ge(s["rt_b"], seen("rt_b"))
                link(nc.vector.tensor_reduce(st[:, 8:13], aff[:], AX.X, ALU.add))
                link(nc.vector.reciprocal(st[:, 8:13], st[:, 8:13]))
                nc.vector.tensor_tensor(aff[:], aff[:], st[:, 8:13].unsqueeze(2).to_broadcast([P, TT, EXPERTS]), ALU.mult).then_inc(s["aff_r"], 1)
                dve.sem_inc(s["small_free"], 1)
                dve.wait_ge(s["affT"], seen("affT"))
                link(nc.vector.tensor_copy(affw[:], flat[0:EXPERTS, 5 * 512:5 * 512 + TOK]))
                for a, b, rounds, tag in ((0, LAT, CAP_LAT // 8, "top_lat"), (LAT, TOK, CAP_CTX // 8, "top_ctx")):
                    with seen.loop(tag, rounds) as i:
                        link(nc.vector.max(top8[:], affw[:, a:b]))
                        seen.settle()
                        link(nc.vector.match_replace(affw[:, a:b], top8[:], affw[:, a:b], -1.0))
                link(nc.vector.tensor_scalar(mask[:], affw[:], 0.0, None, ALU.is_lt))
                link(nc.vector.memset(affw[:], 1.0))
                nc.vector.tensor_tensor_scan(cum[:, 0:LAT], affw[:, 0:LAT], mask[:, 0:LAT], 0.0, ALU.mult, ALU.add)
                link(nc.vector.tensor_tensor_scan(cum[:, LAT:TOK], affw[:, LAT:TOK], mask[:, LAT:TOK], float(CAP_LAT), ALU.mult, ALU.add))
                link(nc.vector.tensor_tensor(cum[:], cum[:], mask[:], ALU.mult))
                nc.vector.tensor_scalar(cum[:], cum[:], -1.0, None, ALU.add).then_inc(s["topk"], 1)
                nc.vector.memset(pos[:], -1.0).then_inc(s["pos_r"], 1)
                for t in range(TT):
                    dve.wait_ge(s["h2tok_hi"], seen("h2tok_hi"))
                    b = 2 * (t % 2)
                    nc.vector.tensor_tensor(t_lo[:, t], flat[:, b * 512:b * 512 + D], t_hi[:, t].bitcast(F32), ALU.subtract).then_inc(s["h2tok_lo"], 1)
                dve.wait_ge(s["posT"], seen("posT"))
                dve.wait_ge(s["pos_r"], seen("pos_r"))
                link(nc.vector.tensor_copy(pos[:, :, 0:EXPERTS], ps[:, 7, 0:TT * EXPERTS].rearrange("p (t e) -> p t e", e=EXPERTS)))

                def choose(e):
                    nc.vector.tensor_tensor(pick[:], slot_no[:].unsqueeze(1).to_broadcast([P, TT, SLOTS]),
                                            pos[:, :, bass.ds(e, 1)].to_broadcast([P, TT, SLOTS]), ALU.is_equal).then_inc(s["picked"], 1)

                choose(0)
                with seen.loop("experts", EXPERTS) as e:
                    for f in range(2):
                        dve.wait_ge(s["silu"], seen("silu"))
                        nc.vector.tensor_tensor(hid[:, 4 * f:4 * f + 4], gated[:, 4 * f:4 * f + 4],
                                                ps[:, 2 * f + 1, :].rearrange("p (k n) -> p k n", k=4)[:, :, 0:SLOTS], ALU.mult).then_inc(s["hidd"], 1)
                    dve.wait_ge(s["pt_ps"], seen("pt_ps"))
                    choose(e + 1)
                    dve.wait_ge(s["ye_hi"], seen("ye_hi"))
                    nc.vector.scalar_tensor_tensor(ye_lo[:], flat[0:SLOTS, 6 * 512:8 * 512], st[0:SLOTS, 32:33], ye_hi[:].bitcast(F32),
                                                   ALU.mult, ALU.subtract).then_inc(s["ye_lo"], 1)
                    dve.wait_ge(s["scat"], seen("scat"))
                    for i in range(KT):
                        nc.vector.scalar_tensor_tensor(x[:, i, LAT:TOK], ps[:, 6 + i // 4, (i % 4) * P:(i % 4 + 1) * P],
                                                       mods[:, 40 + i, 0:1], x[:, i, LAT:TOK], ALU.mult, ALU.add)
                    for i in range(KT):
                        dve.wait_ge(s["scat"], seen("scat"))
                        nc.vector.scalar_tensor_tensor(x[:, i, 0:LAT], ps[:, i % 4, :], mods[:, 40 + i, 1:2], x[:, i, 0:LAT],
                                                       ALU.mult, ALU.add).then_inc(s["scat_out"], 1)
                    dve.wait_ge(s["scat_out"], seen("scat_out", KT))
                dve.sem_inc(s["layer_done"], 1)

        @block.tensor
        def _(pe):
            seen = Seen(pe, "pe", s["settled"])
            pe.sem_inc(s["split_free0"], 1)
            pe.sem_inc(s["split_free1"], 1)
            pe.sem_inc(s["aT"], 1)
            pe.sem_inc(s["av"], 1)

            def three(out, wh, wl, xh, xl, first, last):
                pe.matmul(out, wh, xh, start=first, stop=False)
                pe.matmul(out, wh, xl, start=False, stop=False)
                return pe.matmul(out, wl, xh, start=False, stop=last)

            def wait_split(slot):
                pe.wait_ge(s[f"split{slot}"], seen(f"split{slot}"))

            def wait_set(u):
                pe.wait_ge(s[f"set_free{u}"], seen(f"set_free{u}"))

            seq = ((0, LAT), (LAT, TOK))
            halves = ((0, HALF), (HALF, TOK))

            def feature_split(slot, u, cuts):
                for j in range(2):
                    for c, (a, b) in enumerate(cuts):
                        for k in range(KT):
                            ins = three(ps[:, 4 * u + 2 * j + c, 0:b - a], w_hi[:, slot, k, j * P:(j + 1) * P],
                                        w_lo[:, slot, k, j * P:(j + 1) * P], h_hi[:, k, a:b], h_lo[:, k, a:b], k == 0, k == KT - 1)
                ins.then_inc(s["proj"], 1)

            def feature_raw(rslot, u, cuts, src, kt, free_raw):
                for j in range(2):
                    for c, (a, b) in enumerate(cuts):
                        for k in range(kt):
                            ins = pe.matmul(ps[:, 4 * u + 2 * j + c, 0:b - a], raw[:, rslot, k, j * P:(j + 1) * P],
                                            src[:, k, a:b], start=(k == 0), stop=(k == kt - 1))
                ins.then_inc(s["proj"], 1)
                pe.wait_ge(s["proj"], seen("proj", 0))
                pe.sem_inc(s[f"raw_free{rslot}"], 1)

            def ada(a, rslot):
                pe.wait_ge(s[f"raw_full{rslot}"], seen(f"raw_full{rslot}", 32))
                for j in range(2):
                    for k in range(KT):
                        out = ps[:, 7, 2 * j:2 * j + 2] if a is None else flat[:, bass.ds(4 * a + (7 * 512 + 2 * j), 2)]
                        ins = pe.matmul(out, raw[:, rslot, k, j * P:(j + 1) * P], cs[:, k, :], start=(k == 0), stop=(k == KT - 1))
                ins.then_inc(s["ada"], 1)
                pe.wait_ge(s["ada"], seen("ada"))
                pe.sem_inc(s[f"raw_free{rslot}"], 1)

            def sum_squares(n_in, sem_in):
                for k in range(n_in):
                    pe.wait_ge(s[sem_in], seen(sem_in))
                    for c, (a, b) in enumerate(halves):
                        ins = pe.matmul(ps[:, c, 0:HALF], ones[:], mm_[:, k, a:b], start=(k == 0), stop=(k == n_in - 1), skip_group_check=True)
                ins.then_inc(s["ss"], 1)

            def token_major(slot, off, last_wait=False):
                for t in range(TT):
                    if last_wait and t == 4:
                        pe.wait_ge(s["qkT_out"], seen("qkT_out"))
                    for k in range(KT):
                        ins = three(flat[:, off + t * CW:off + (t + 1) * CW], h_hi[:, k, t * P:(t + 1) * P], h_lo[:, k, t * P:(t + 1) * P],
                                    w_hi[:, slot, k, :], w_lo[:, slot, k, :], k == 0, k == KT - 1)
                ins.then_inc(s["proj"], 1)
                pe.wait_ge(s["proj"], seen("proj", 0))
                pe.sem_inc(s[f"split_free{slot}"], 1)

            def turn_qk(u):
                pe.wait_ge(s["roped"], seen("roped"))
                for b in range(2):
                    if b == 1:
                        pe.wait_ge(s["ada_out"], seen("ada_out"))
                    for t in range(4):
                        pe.transpose(ps[:, 6 + b, t * P:(t + 1) * P], qk_a[:, t * CW + b * P:t * CW + (b + 1) * P], ident[:])
                for b in range(2):
                    ins = pe.transpose(ps[:, 2 + 3 * u, 256 + b * P:256 + (b + 1) * P], qk_a[:, 4 * CW + b * P:4 * CW + (b + 1) * P], ident[:])
                ins.then_inc(s["qkT"], 1)

            def scores(i):
                u, t = divmod(i, TT)
                for m in range(2):
                    if i:
                        pe.wait_ge(s["expd"], seen("expd"))
                    q = qk_t[64 * m:64 * m + 64, u, t * P:(t + 1) * P]
                    if t < 4:
                        for c in range(2):
                            ins = pe.matmul(ps[:, 3 * m + c, 0:HALF], q, qk_t[64 * m:64 * m + 64, u, TOK + c * HALF:TOK + (c + 1) * HALF],
                                            start=True, stop=True)
                    else:
                        ins = pe.matmul(ps[:, 3 * m, 0:CTX], q, qk_t[64 * m:64 * m + 64, u, 2 * TOK:2 * TOK + CTX], start=True, stop=True)
                    ins.then_inc(s["s_done"], 1)

            def values(i):
                u, t = divmod(i, TT)
                pe.wait_ge(s["a_ready"], seen("a_ready"))
                nk = TT if t < 4 else 1
                for c in range(nk):
                    ins = pe.transpose(flat[:, 6 * 512 + c * P:6 * 512 + (c + 1) * P], probs[:, 0, c * P:(c + 1) * P], ident[:])
                ins.then_inc(s["aT"], 1)
                pe.wait_ge(s["aT_out"], seen("aT_out"))
                if t == 0 and u == 1:
                    pe.wait_ge(s["o_out"], seen("o_out"))
                out = ps[:, 2, t * P:(t + 1) * P] if t < 4 else ps[:, 5, 0:P]
                for c in range(nk):
                    ins = pe.matmul(out, vb[:, c if t < 4 else 5, u * P:(u + 1) * P], at_[:, c, :], start=(c == 0), stop=(c == nk - 1))
                ins.then_inc(s["av"], 1)

            pe.wait_ge(s["const_in"], 64)
            pe.wait_ge(s["x_in"], 32)
            for k in range(KT):
                if k >= 2:
                    pe.wait_ge(s["tr_out"], seen("tr_out"))
                b = 2 * (k % 2)
                for t in range(TT):
                    ins = pe.transpose(flat[:, b * 512 + t * P:b * 512 + (t + 1) * P], xtok[:, t, k * P:(k + 1) * P], ident[:])
                ins.then_inc(s["tr_in"], 1)
            pe.wait_ge(s["tr_out"], seen("tr_out", 2))
            pe.wait_ge(s["cs_ready"], 1)
            with seen.loop("layer", DEPTH) as l:
                sum_squares(KT, "sq")
                with seen.loop("ada1", 4) as i:
                    for u in range(2):
                        ada(2 * i + u, u)
                seen("raw_full0", 96)
                seen("raw_full1", 96)
                pe.wait_ge(s["row_a"], seen("row_a"))
                pe.wait_ge(s["hready"], seen("hready"))
                pe.wait_ge(s["ada_out"], seen("ada_out"))
                with seen.loop("conv_pool", 3) as i:
                    for u in range(2):
                        wait_split(u)
                        wait_set(u)
                        feature_split(u, u, seq)
                        pe.wait_ge(s["proj"], seen("proj"))
                        pe.sem_inc(s[f"split_free{u}"], 1)
                pe.wait_ge(s["up_ready"], seen("up_ready", 2))
                pe.sem_inc(s["set_free0"], 1)
                pe.sem_inc(s["set_free1"], 1)
                with seen.loop("ada2", 2) as i:
                    for u in range(2):
                        ada(2 * i + (8 + u), u)
                for g in range(GROUPS):
                    pe.wait_ge(s["pooled"], seen("pooled"))
                    if g >= 2:
                        pe.wait_ge(s["pool_br"], seen("pool_br"))
                    b = 2 * (g % 2)
                    pw = small_at("pool_w")[:, g * P:(g + 1) * P]
                    pe.matmul(ps[:, b, :], pw, up[:, g, PPAD:PPAD + LAT], start=True, stop=True)
                    pe.matmul(ps[:, b + 1, 0:CTX], pw, up[:, g, 2 * PPAD + LAT:2 * PPAD + TOK], start=True, stop=True).then_inc(s["poolmm"], 1)
                pe.wait_ge(s["pool_br"], seen("pool_br", 2))
                pe.wait_ge(s["ada_out"], seen("ada_out"))
                with seen.loop("pair", PAIRS) as g:
                    for u in range(2):
                        if u == 1:
                            pe.wait_ge(s["ada_out"], seen("ada_out"))
                        ada(None, 1)
                        wait_split(u)
                        seen("raw_full0", 32)
                        seen("proj")
                        token_major(u, 1536 * u)
                    turn_qk(0)
                    wait_split(0)
                    seen("raw_full0", 32)
                    seen("proj")
                    token_major(0, 0, True)
                    ada(None, 1)
                    turn_qk(1)
                    pe.wait_ge(s["qkT_out"], seen("qkT_out"))
                    pe.wait_ge(s["cache_in"], seen("cache_in", 32))
                    for u in range(2):
                        ins = pe.transpose(ps[:, 6, u * P:(u + 1) * P], ck[:, u * P:(u + 1) * P], ident[:])
                    ins.then_inc(s["qkT"], 1)
                    pe.wait_ge(s["qkT_out"], seen("qkT_out"))
                    pe.wait_ge(s["v_ready"], seen("v_ready", 2))
                    scores(0)
                    for i in range(2 * TT):
                        if i + 1 < 2 * TT:
                            scores(i + 1)
                        values(i)
                    pe.wait_ge(s["av"], seen("av", 10) + 1)
                    pe.sem_inc(s["attn_free"], 1)
                    pe.wait_ge(s["expd"], seen("expd", 2))
                    pe.wait_ge(s["o_out"], seen("o_out"))
                for h in range(HEADS):
                    b = 2 * (h % 2)
                    pe.wait_ge(s["o_sq"], seen("o_sq"))
                    if h >= 2:
                        pe.wait_ge(s["o_var"], seen("o_var"))
                    for c, (a, e) in enumerate(halves):
                        ins = pe.matmul(ps[:, b + c, 0:HALF], ones[:], mm_[:, h, a:e], start=True, stop=True)
                    ins.then_inc(s["o_ss"], 1)
                pe.wait_ge(s["conv_done"], seen("conv_done"))
                for j in range(GROUPS):
                    pe.matmul(ps[:, 4, :], ones[:], zc[:, j, 0:LAT], start=(j == 0), stop=(j == GROUPS - 1), skip_group_check=True)
                    ins = pe.matmul(ps[:, 5, 0:CTX], ones[:], zc[:, j, LAT + CPAD:CRUN], start=(j == 0), stop=(j == GROUPS - 1), skip_group_check=True)
                ins.then_inc(s["ln_sum"], 1)
                for j in range(GROUPS):
                    pe.wait_ge(s["ln_sq"], seen("ln_sq"))
                    pe.matmul(ps[:, 6, :], ones[:], mm_[:, j, 0:LAT], start=(j == 0), stop=(j == GROUPS - 1), skip_group_check=True)
                    ins = pe.matmul(ps[:, 7, 0:CTX], ones[:], mm_[:, j, LAT:TOK], start=(j == 0), stop=(j == GROUPS - 1), skip_group_check=True)
                ins.then_inc(s["ln_sum"], 1)
                pe.wait_ge(s["o_norm"], seen("o_norm", HEADS))
                pe.wait_ge(s["o_var"], seen("o_var", 2))
                pe.wait_ge(s["branch_c"], seen("branch_c", GROUPS))
                with seen.loop("merge", 4) as n:
                    for b, (src, kt) in enumerate(((ot, KT), (brp, GROUPS), (brc, GROUPS))):
                        wait_split(b % 2)
                        seen("raw_full0", 32)
                        wait_set(0)
                        feature_split(b % 2, 0, halves)
                        pe.wait_ge(s["proj"], seen("proj"))
                        pe.sem_inc(s[f"split_free{b % 2}"], 1)
                        pe.wait_ge(s["raw_full1"], seen("raw_full1", 32))
                        wait_set(1)
                        seen("proj")
                        feature_raw(1, 1, halves, src, kt, True)
                pe.wait_ge(s["proj"], seen("proj", 0))
                pe.sem_inc(s["d_done"], 1)
                pe.wait_ge(s["m_ready"], seen("m_ready"))
                with seen.loop("out", 2) as i:
                    for u in range(2):
                        pe.wait_ge(s[f"raw_full{u}"], seen(f"raw_full{u}", 32))
                        wait_set(u)
                        seen("proj")
                        feature_raw(u, u, seq, mm_, KT, True)
                pe.wait_ge(s["xo_done"], seen("xo_done"))
                sum_squares(KT, "sq")
                pe.wait_ge(s["hnorm"], seen("hnorm", 2 * KT))
                for t in range(TT):
                    for k in range(KT):
                        ins = pe.matmul(ps[:, 4, t * EXPERTS:(t + 1) * EXPERTS], mm_[:, k, t * P:(t + 1) * P],
                                        small_at("router")[:, k * EXPERTS:(k + 1) * EXPERTS], start=(k == 0), stop=(k == KT - 1))
                ins.then_inc(s["logits"], 1)
                pe.wait_ge(s["row_a"], seen("row_a"))
                for t in range(TT):
                    if t >= 2:
                        pe.wait_ge(s["h2tok_lo"], seen("h2tok_lo"))
                    b = 2 * (t % 2)
                    for k in range(KT):
                        ins = pe.transpose(flat[:, b * 512 + k * P:b * 512 + (k + 1) * P], mm_[:, k, t * P:(t + 1) * P], ident[:])
                    ins.then_inc(s["h2tok_ps"], 1)
                    if t == 1:
                        pe.wait_ge(s["aff_r"], seen("aff_r"))
                        for c in range(TT):
                            ins = pe.transpose(flat[0:EXPERTS, 5 * 512 + c * P:5 * 512 + (c + 1) * P], aff[:, c, :], ident[:])
                        ins.then_inc(s["affT"], 1)
                        pe.wait_ge(s["topk"], seen("topk"))
                        seen.settle()
                        for c in range(TT):
                            ins = pe.transpose(ps[:, 7, c * EXPERTS:(c + 1) * EXPERTS], cum[:, c * P:(c + 1) * P], ident[0:EXPERTS, 0:EXPERTS])
                        ins.then_inc(s["posT"], 1)

                def gather():
                    pe.wait_ge(s["picked"], seen("picked"))
                    for k in range(KT):
                        out = ps[:, 4 + k // 4, (k % 4) * P:(k % 4) * P + SLOTS]
                        for t in range(TT):
                            pe.matmul(out, t_hi[:, t, k * P:(k + 1) * P], pick[:, t, :], start=(t == 0), stop=False)
                            ins = pe.matmul(out, t_lo[:, t, k * P:(k + 1) * P], pick[:, t, :], start=False, stop=(t == TT - 1))
                    ins.then_inc(s["xs_ps"], 1)

                def two(out, i, a, b):
                    pe.matmul(out, ye_hi[:, i * P:(i + 1) * P], ptk[:, a:b], start=True, stop=False)
                    return pe.matmul(out, ye_lo[:, i * P:(i + 1) * P], ptk[:, a:b], start=False, stop=True)

                pe.wait_ge(s["h2tok_lo"], seen("h2tok_lo", 2))
                gather()
                with seen.loop("experts", EXPERTS) as e:
                    pe.wait_ge(s["xs_out"], seen("xs_out"))
                    for n in range(4):
                        pe.wait_ge(s[f"wfull{n}"], seen(f"wfull{n}", 16))
                        for j in range(4):
                            for k in range(KT):
                                ins = pe.matmul(ps[:, n, j * P:j * P + SLOTS], ring[:, n, k, j * P:(j + 1) * P], xs[:, k, :], start=(k == 0), stop=(k == KT - 1))
                        ins.then_inc(s["hh"], 1)
                        pe.wait_ge(s["hh"], seen("hh"))
                        pe.sem_inc(s["wfree"], 1)
                    for t in range(TT):
                        pe.matmul(ps[0:SLOTS, 7, P:P + 1], pick[:, t, :].bitcast(F32), aff[:, t, bass.ds(e, 1)], start=(t == 0), stop=(t == TT - 1))
                    for t in range(TT):
                        ins = pe.transpose(flat[0:SLOTS, 6 * 512 + t * P:6 * 512 + (t + 1) * P], pick[:, t, :].bitcast(F32), ident[:])
                    ins.then_inc(s["pt_ps"], 1)
                    for f in range(2):
                        pe.wait_ge(s["hidd"], seen("hidd"))
                    for f in range(2):
                        pe.wait_ge(s[f"wfull{4 + f}"], seen(f"wfull{4 + f}", 16))
                        for j in range(4):
                            for k in range(KT):
                                ins = pe.matmul(ps[:, 4 + f, j * P:j * P + SLOTS], ring[:, 4 + f, k, j * P:(j + 1) * P], hid[:, k, :], start=(k == 0), stop=(k == KT - 1))
                        ins.then_inc(s["yt_ps"], 1)
                        pe.wait_ge(s["yt_ps"], seen("yt_ps"))
                        pe.sem_inc(s["wfree"], 1)
                    pe.wait_ge(s["pt_out"], seen("pt_out"))
                    for k in range(KT):
                        if k % 4 == 0:
                            pe.wait_ge(s["yt_out"], seen("yt_out"))
                        ins = pe.transpose(flat[0:SLOTS, 6 * 512 + k * P:6 * 512 + (k + 1) * P], yt[:, k, :], ident[:])
                    ins.then_inc(s["ye_ps"], 1)
                    gather()
                    pe.wait_ge(s["ye_hi"], seen("ye_hi"))
                    pe.wait_ge(s["ye_lo"], seen("ye_lo"))
                    for i in range(KT):
                        ins = two(ps[:, 6 + i // 4, (i % 4) * P:(i % 4 + 1) * P], i, LAT, TOK)
                    ins.then_inc(s["scat"], 1)
                    for i in range(KT):
                        if i >= 4:
                            pe.wait_ge(s["scat_out"], seen("scat_out"))
                        two(ps[:, i % 4, :], i, 0, LAT).then_inc(s["scat"], 1)
                    pe.wait_ge(s["scat_out"], seen("scat_out", 4))
                pe.wait_ge(s["xs_out"], seen("xs_out"))
            for t in range(TT):
                if t >= 2:
                    pe.wait_ge(s["out_sb"], seen("out_sb"))
                b = 2 * (t % 2)
                for k in range(KT):
                    ins = pe.transpose(flat[:, b * 512 + k * P:b * 512 + (k + 1) * P], x[:, k, t * P:(t + 1) * P], ident[:])
                ins.then_inc(s["out_ps"], 1)


def constants():
    ident = np.eye(P, dtype=np.float32)
    rows, cols = np.divmod(np.arange(LAT), 64)
    inv = (10000.0 ** (-np.arange(16, dtype=np.float32) / np.float32(16))).astype(np.float32)
    c = np.ones((TT, P, 4, 2, 2, 16), np.float32)
    sn = np.zeros((TT, P, 4, 2, 2, 16), np.float32)
    for a, at in enumerate((rows, cols)):
        ang = (at.astype(np.float32)[:, None] * inv[None]).reshape(4, P, 1, 1, 16)
        c[:4, :, :, a] = np.cos(ang)
        sn[:4, :, :, a] = np.sin(ang) * np.array([-1, 1], np.float32)[:, None]
    cos = np.ascontiguousarray(c.transpose(1, 0, 2, 3, 4, 5)).reshape(P, TT * CW)
    sin = np.ascontiguousarray(sn.transpose(1, 0, 2, 3, 4, 5)).reshape(P, TT * CW)
    cnt = np.zeros((GROUPS, PRUN), np.float32)
    for g in range(GROUPS):
        w = 1 << g
        for at, n in ((0, LAT), (LAT + PPAD, CTX)):
            t = np.arange(n)
            cnt[g, at:at + n] = 1.0 / (np.clip(t + w, 0, n) - np.clip(t - w, 0, n))
    slot = np.ascontiguousarray(np.broadcast_to(np.arange(SLOTS, dtype=np.float32), (P, SLOTS)))
    return ident, cos, sin, cnt, slot


def kernel(**inputs):
    import math
    import concourse.bacc as _bacc
    from concourse.bass_utils import run_bass_kernel_spmd as _run

    a = {k: np.ascontiguousarray(v) for k, v in inputs.items()}

    def cols(v, n):
        return v.reshape(DEPTH, n, P).transpose(0, 2, 1)

    def rows(v):
        return np.broadcast_to(v.reshape(DEPTH, 1, -1), (DEPTH, P, v[0].size))

    qg, kg = a["q_norm_g"], a["k_norm_g"]
    qkg = np.concatenate([qg, qg, kg, kg], 1)
    swapped = qkg.reshape(DEPTH, 8, 2, 16)[:, :, ::-1].reshape(DEPTH, 256)
    lam_init = np.array([0.8 - 0.6 * math.exp(-0.3 * l) for l in range(DEPTH)], np.float32)
    one_minus = np.array([1.0 - (0.8 - 0.6 * math.exp(-0.3 * l)) for l in range(DEPTH)], np.float32)
    parts = {
        "rms1": cols(a["rms1_g"], 8), "rms2": cols(a["rms2_g"], 8), "b_ada": cols(a["b_ada"], 48),
        "pool_scale": cols(a["pool_scale"], 4), "conv_b": cols(a["conv_b"], 4), "ln_g": cols(a["conv_ln_g"], 4),
        "ln_b": cols(a["conv_ln_b"], 4), "b_gate": cols(a["b_gate"], 24), "subln": cols(a["subln_g"], 1),
        "conv_w": a["conv_w"].reshape(DEPTH, TAPS, 4, P).transpose(0, 3, 2, 1).reshape(DEPTH, P, 4 * TAPS),
        "router": a["w_router"].reshape(DEPTH, 8, P, 16).transpose(0, 2, 1, 3).reshape(DEPTH, P, 128),
        "lam_vec": rows(a["lam_vec"]), "qkg": rows(qkg), "qkg_swapped": rows(swapped),
        "lam_init": rows(lam_init), "one_minus": rows(one_minus),
        "pool_w": a["pool_w"].transpose(0, 2, 1, 3).reshape(DEPTH, P, 512),
    }
    small = np.concatenate([parts[n] for n in SMALL], axis=2)
    ident, cos, sin, cnt, slot = constants()
    cvecs = np.stack([a["c_ctx"], a["c"][0]], 1).reshape(KT, P, 2).transpose(1, 0, 2)
    given = {
        "x_prompt": a["x_prompt"], "x_sample": a["x_sample"], "cvecs": cvecs, "cache_k": a["cache_k"], "cache_v": a["cache_v"],
        "small": small, "w_ada": a["w_ada"], "w_in": a["w_in"], "w_proj_a": a["w_proj_a"], "w_proj_b": a["w_proj_b"],
        "w_proj_c": a["w_proj_c"], "w_gate": a["w_gate"], "w_out": a["w_out"], "w1": a["w1"], "w3": a["w3"], "w2": a["w2"],
        "ident_in": ident, "cos_in": cos, "sin_in": sin, "inv_in": cnt, "slot_in": slot,
    }
    shapes = [a["x_prompt"].shape, a["x_sample"].shape, (1, DEPTH, CTX, HEADS, 2, HD), (1, DEPTH, CTX, HEADS, DV)]

    def program():
        nc = _bacc.Bacc("TRN2", target_bir_lowering=False, num_devices=1)
        args = [nc.dram_tensor(f"in_{n}", v.shape, F32, kind="ExternalInput").ap() for n, v in given.items()]
        args += [nc.dram_tensor(f"out_{i}", sh, F32, kind="ExternalOutput").ap() for i, sh in enumerate(shapes)]
        build(nc, *args)
        return nc

    for _ in range(6):
        PER_TURN.pop("changed", None)
        nc = program()
        if not PER_TURN.get("changed"):
            break
    arrays = {f"in_{n}": np.ascontiguousarray(v) for n, v in given.items()}
    r = _run(nc, [arrays], core_ids=[0])
    return tuple(r.results[0][f"out_{i}"] for i in range(4))
```

```python
from contextlib import ExitStack, contextmanager

import numpy as np

import concourse.bass as bass
from concourse import mybir

F32 = mybir.dt.float32
F32R = mybir.dt.float32r
ACT = mybir.ActivationFunctionType
ALU = mybir.AluOpType
AX = mybir.AxisListType

P = 128
D = 1024
KT = D // P
LAT, CTX = 512, 128
TOK = LAT + CTX
HALF = TOK // 2
TT = TOK // P
DEPTH = 2
HEADS, HD, DV = 8, 64, 128
PAIRS = HEADS // 2
CW = 256
EXPERTS, FF = 16, 1024
CAP_LAT, CAP_CTX = 2 * LAT // EXPERTS, 2 * CTX // EXPERTS
SLOTS = CAP_LAT + CAP_CTX
EPS = 1e-6
SCALE = HD ** -0.5
GROUPS = 4
TAPS, CPAD = 31, 15
CLEN = CPAD + LAT + CPAD + CTX + CPAD
CRUN = LAT + CPAD + CTX
PPAD = 8
PLEN = PPAD + LAT + PPAD + CTX + PPAD
PRUN = LAT + PPAD + CTX
Q0, K0, V0, POOL0, CONVA0, CONVB0 = 0, 1024, 2048, 3072, 3584, 4096
EW = 512
EK = 4
RING = 4
CHUNKS = [(0, 0, 0, 0), (0, 4, 0, 0), (1, 0, 0, 1), (1, 4, 0, 1), (0, 0, 1, 2), (0, 4, 1, 2), (1, 0, 1, 3), (1, 4, 1, 3),
          (2, 0, 0, 4), (2, 0, 1, 5), (2, 4, 0, 4), (2, 4, 1, 5)]
NCH = len(CHUNKS)
LATBANK = (0, 1, 4, 5)

SMALL = {}
_at = 0
for _name, _n in (("rms1", 8), ("rms2", 8), ("b_ada", 48), ("pool_scale", 4), ("conv_b", 4), ("ln_g", 4),
                  ("ln_b", 4), ("b_gate", 24), ("subln", 1), ("conv_w", 4 * TAPS), ("router", 8 * 16),
                  ("lam_vec", 256), ("lam_init", 1), ("one_minus", 1),
                  ("pool_w", 512)):
    SMALL[_name] = (_at, _at + _n)
    _at += _n
NSMALL = _at

PER_TURN = {}


class Seen:

    def __init__(self, eng, name, settled):
        self.eng, self.name, self.n, self.base, self.settled = eng, name, {}, {}, settled

    def settle(self):
        self.eng.sem_inc(self.settled, 1)

    def __call__(self, sem, k=1):
        self.n[sem] = self.n.get(sem, 0) + k
        return self.base.get(sem, 0) + self.n[sem]

    @contextmanager
    def loop(self, what, count):
        key = f"{self.name}.{what}"
        per = PER_TURN.get(key, {})
        n, base = dict(self.n), dict(self.base)
        self.settle()
        with self.eng.Fori(0, count) as i:
            for sem in set(n) | set(per):
                b = base.get(sem, 0) + n.get(sem, 0)
                self.base[sem] = b + per[sem] * i if per.get(sem) else b
            self.n = {}
            yield i
            used = {k: v for k, v in self.n.items() if v}
            if used != per:
                PER_TURN[key] = used
                PER_TURN["changed"] = True
        self.base = base
        self.n = {s: n.get(s, 0) + count * used.get(s, 0) for s in set(n) | set(used)}


def build(nc, x_prompt, x_sample, cvecs, cache_k, cache_v, small, gains_in, w_ada, w_in, w_proj_a, w_proj_b,
          w_proj_c, w_gate, w_out, w1, w3, w2, ident_in, cos_in, sin_in, inv_in, slot_in,
          y_prompt, y_sample, new_k, new_v, dbg=None):
    ctx = ExitStack()
    with ctx:
        start = (nc.sbuf_base + 63) // 64 * 64
        free = {"at": start}

        def region(nbytes):
            at = free["at"]
            free["at"] = at + (nbytes + 31) // 32 * 32
            return at

        def sb(name, shape, at, dt=F32):
            return nc.alloc_sbuf_tensor_at(name, shape, dt, offset=at)

        r_x, r_m, r_ring, r_raw, r_t2 = region(20480), region(22176), region(98304), region(16384), region(40960)
        x = sb("x", [P, KT, TOK], r_x)
        mm_ = sb("m", [P, KT, TOK], r_m)
        xtok = sb("xtok", [P, TT, D], r_m)
        sg = sb("conv_gate", [P, GROUPS, TOK], r_m)
        inv = sb("inv_count", [P, GROUPS, PRUN], r_m + 10240)
        rope_c = sb("rope_c", [P, TT * CW], r_m)
        rope_s = sb("rope_s", [P, TT * CW], r_m + 5120)
        qk_a = sb("qk_a", [P, TT * CW], r_m + 10240)
        qk_b = sb("qk_b", [P, TT * CW], r_m + 15360)
        gains = sb("gains", [P, 2, CW], r_m + 15360)
        xg = sb("xg", [SLOTS, D], r_m)
        xs_hi = sb("xs_hi", [P, KT, SLOTS], r_m + 4096, F32R)
        xs_lo = sb("xs_lo", [P, KT, SLOTS], r_m + 6656, F32R)
        pick = sb("pick", [P, TT, SLOTS], r_m + 9216, F32R)
        hid = sb("hid", [SLOTS, EW], r_m + 10816)
        ht_hi = sb("hid_t_hi", [P, KT, SLOTS], r_m + 12864, F32R)
        ht_lo = sb("hid_t_lo", [P, KT, SLOTS], r_m + 15424, F32R)
        ye_lo = sb("ye_lo", [SLOTS, D], r_m + 17984, F32R)
        m_raw = sb("m_raw", [P, RING, EK, EW], r_ring)
        m_hi = sb("m_hi", [P, RING, EK, EW], r_ring + 32768, F32R)
        m_lo = sb("m_lo", [P, RING, EK, EW], r_ring + 65536, F32R)
        h_hi = sb("h_hi", [P, KT, TOK], r_ring, F32R)
        h_lo = sb("h_lo", [P, KT, TOK], r_ring + 20480, F32R)
        w_hi = sb("w_hi", [P, 2, KT, CW], r_ring + 40960, F32R)
        w_lo = sb("w_lo", [P, 2, KT, CW], r_ring + 57344, F32R)
        ot = sb("ot", [P, HEADS, TOK], r_ring + 73728)
        at_ = sb("attn_t", [P, TT, P], r_ring + 94208)
        ck = sb("cache_k_tok", [P, CW], r_ring + 94208 + 2560)
        raw = sb("raw", [P, 2, KT, CW], r_raw)
        affw = sb("affw", [EXPERTS, TOK], r_raw)
        cum = sb("cum", [EXPERTS, TOK], r_raw + 2560)
        mask = sb("mask", [EXPERTS, TOK], r_raw + 5120)
        sigd = sb("sigd", [P, 4, HALF], r_t2 + 13728)
        prod = sb("prod", [P, 4, HALF], r_t2 + 13728 + 5120)
        zc = sb("zc", [P, GROUPS + 1, CLEN], r_t2)
        brp = sb("pool_branch", [P, GROUPS, TOK], r_t2 + 13728)
        up = sb("up", [P, GROUPS, PLEN], r_t2 + 23968)
        pt1 = sb("pool_t1", [P, PLEN], r_t2 + 34592)
        pt2 = sb("pool_t2", [P, PLEN], r_t2 + 37248)
        qk_t = sb("qk_t", [P, 2, TOK + TOK + CTX], r_t2 + 23968)
        probs = sb("probs", [P, 2, TOK], r_t2 + 23968 + 11264)
        brc = sb("conv_branch", [P, GROUPS, TOK], r_t2 + 23968)
        sigd = sb("sigd", [P, 4, HALF], r_t2 + 34208)
        prod = sb("prod", [P, 4, HALF], r_t2)
        t_hi = sb("h2tok_hi", [P, TT, D], r_t2, F32R)
        t_lo = sb("h2tok_lo", [P, TT, D], r_t2 + 20480, F32R)
        ident = sb("ident", [P, P], region(512))
        ones = sb("ones", [P, P], region(512))
        sm = sb("small", [P, NSMALL], region(4 * NSMALL))
        mods = sb("mods", [P, 48, 2], region(384))
        coef = sb("coef", [P, KT, 2], region(64))
        cs = sb("cs", [P, KT, 2], region(64))
        slot_no = sb("slot_no", [P, SLOTS], region(4 * SLOTS))
        pos = sb("pos", [P, TT, EXPERTS + 1], region(352))
        aff = sb("aff", [P, TT, EXPERTS], region(320))
        st = sb("stats", [P, 64], region(256))
        top8 = sb("top8", [EXPERTS, 8], region(32))
        r_v = region(6656)
        vb = sb("v_pair", [P, TT + 1, CW], r_v)
        row = sb("row", [P, TOK], r_v)
        row2 = sb("row2", [P, TOK], r_v + 2560)
        ye_hi = sb("ye_hi", [SLOTS, D], r_v, F32R)
        ptk = sb("pick_t", [SLOTS, TOK], r_v + 4096, F32R)
        assert free["at"] <= nc.sbuf_usable_end, (free["at"], nc.sbuf_usable_end)

        ps = ctx.enter_context(nc.psum_tensor("ps", [P, 8, 512], F32))
        flat = ps[:].rearrange("p b n -> p (b n)")
        ada_ps = ps[:, 7, 0:96].rearrange("p (m c) -> p m c", c=2)

        def small_at(name):
            a, b = SMALL[name]
            return sm[:, a:b]

        names = """raw_full0 raw_full1 raw_free0 raw_free1 hi_done split0 split1 split_free0 split_free1 proj
        set_free0 set_free1 const_in x_in small_in small_free tr_in tr_out sq ss row_a row_b row_c tnorm hnorm hready
        cs_ready ada mods_ready lam_a lam_b lam_c z_ready pads up_ready pool_in pooled poolmm pool_br table_in
        table_ready qksq qkss qksqrt qkxn qkt2 roped qkT qkT_out newk_out newv_out newk_free newv_free v_ready cache_in s_done expd
        maxd a_ready aT aT_out av o_out conv_done ln_sum ln_d ln_sq ln_var ln_sqrt ln_n branch_c o_sq o_ss o_var
        o_sqrt o_norm sig merged xo_done logits rt_a rt_b aff_r affT topk posT pos_r h2tok_ps h2tok_hi h2tok_lo
        mfull0 mfull1 mfull2 mfull3 m_high msplit mdone silu hidd hid_t ht_high ht_out picked pt_ps pt_out xg_ps xg_out xs_ps
        xs_high xs_out ye_hi ye_lo scat scat_out layer_done m_ready ada_out out_ps out_sb y_out attn_free d_done
        dve act pool settled""".split()
        s = {n: ctx.enter_context(nc.semaphore("s_" + n)) for n in names}
        assert len(set(names)) == len(names)

        block = ctx.enter_context(nc.Block())
        xin = (x_sample, x_prompt)
        yout = (y_sample, y_prompt)

        @block.sync
        def _(sp):
            seen = Seen(sp, "sp", s["settled"])
            sp.dma_start(ident[:], ident_in).then_inc(s["const_in"], 16)
            sp.dma_start(slot_no[:], slot_in).then_inc(s["const_in"], 16)
            sp.dma_start(cs[:], cvecs).then_inc(s["const_in"], 16)
            sp.dma_start(xtok[:, 0:4, :], x_sample[0].rearrange("(t p) d -> p t d", p=P)).then_inc(s["x_in"], 16)
            sp.dma_start(xtok[:, 4, :], x_prompt[0]).then_inc(s["x_in"], 16)
            sp.sem_inc(s["raw_free0"], 1)
            sp.sem_inc(s["raw_free1"], 1)

            def chunk(slot, *parts):
                sp.wait_ge(s[f"raw_free{slot}"], seen(f"raw_free{slot}"))
                for dst, src in parts:
                    sp.dma_start(dst, src).then_inc(s[f"raw_full{slot}"], 16)

            def wide(slot, src):
                chunk(slot, (raw[:, slot, 0:4, :], src[:, 0:4, :]), (raw[:, slot, 4:8, :], src[:, 4:8, :]))

            ada_v = w_ada.rearrange("l (k p) (c n) -> l c p k n", p=P, n=CW)
            in_v = w_in.rearrange("l (k p) (c n) -> l c p k n", p=P, n=CW)
            in_h = w_in.rearrange("l (k p) (c n) -> l c p k n", p=P, n=P)
            gate_v = w_gate.rearrange("l (k p) (c n) -> l c p k n", p=P, n=CW)
            pa_v = w_proj_a.rearrange("l (k p) (c n) -> l c p k n", p=P, n=CW)
            pb_v = w_proj_b.rearrange("l (k p) (c n) -> l c p k n", p=P, n=CW)
            pc_v = w_proj_c.rearrange("l (k p) (c n) -> l c p k n", p=P, n=CW)
            out_v = w_out.rearrange("l (k p) (c n) -> l c p k n", p=P, n=CW)
            ex_v = [w.rearrange("l e (k p) n -> l e p k n", p=P) for w in (w1, w3, w2)]
            with seen.loop("layer", DEPTH) as l:
                with seen.loop("ada1", 4) as i:
                    for u in range(2):
                        wide(u, ada_v[l, 2 * i + u])
                for n, c0 in enumerate((CONVB0, CONVA0, POOL0)):
                    for u in range(2):
                        wide(u, in_v[l, c0 // CW + u])
                with seen.loop("ada2", 2) as i:
                    for u in range(2):
                        wide(u, ada_v[l, 2 * i + u + 8])
                with seen.loop("pair", PAIRS) as g:
                    for u in range(2):
                        chunk(0, (raw[:, 0, :, 0:P], in_h[l, Q0 // P + 2 * g + u]),
                              (raw[:, 0, :, P:CW], in_h[l, K0 // P + 2 * g + u]))
                        wide(1, ada_v[l, 3 * g + 12 + u])
                    wide(0, in_v[l, g + V0 // CW])
                    wide(1, ada_v[l, 3 * g + 14])
                with seen.loop("merge", 4) as n:
                    wide(0, gate_v[l, n])
                    wide(1, pa_v[l, n])
                    for u, (w, gate) in enumerate(((pb_v, 4), (pc_v, 8))):
                        wide(0, gate_v[l, n + gate])
                        src = w[l, n]
                        chunk(1, (raw[:, 1, 0:2, :], src[:, 0:2, :]), (raw[:, 1, 2:4, :], src[:, 2:4, :]))
                with seen.loop("out", 2) as i:
                    for u in range(2):
                        wide(u, out_v[l, 2 * i + u])
                sp.wait_ge(s["d_done"], seen("d_done"))
                seen.settle()
                def expert_chunk(e, n, wait=True):
                    w, k, c, _ = CHUNKS[n]
                    if wait:
                        sp.wait_ge(s["msplit"], seen("msplit"))
                        seen.settle()
                    sp.dma_start(m_raw[:, n % RING], ex_v[w][l, e][:, k:k + EK, c * EW:(c + 1) * EW]).then_inc(s[f"mfull{n % RING}"], 16)

                for n in range(RING):
                    expert_chunk(0, n, False)
                with seen.loop("experts", EXPERTS - 1) as e:
                    for n in range(RING, NCH):
                        expert_chunk(e, n)
                    for n in range(RING):
                        expert_chunk(e + 1, n)
                for n in range(RING, NCH):
                    expert_chunk(EXPERTS - 1, n)
                seen("msplit", RING)
            y_v = y_sample[0].rearrange("(t p) d -> p t d", p=P)
            for t in range(TT):
                sp.wait_ge(s["out_sb"], seen("out_sb"))
                sp.dma_start(y_v[:, t] if t < 4 else y_prompt[0], xtok[:, t, :]).then_inc(s["y_out"], 16)
            sp.wait_ge(s["y_out"], 16 * TT)

        @block.gpsimd
        def _(pool):
            seen = Seen(pool, "pool", s["settled"])
            nc.gpsimd.memset(ones[:], 1.0).then_inc(s["const_in"], 16)
            nk_v = new_k.rearrange("b l s h m d -> (b l) h s (m d)")
            nv_v = new_v.rearrange("b l s (g h) d -> (b l) g s (h d)", h=2)
            ck_v = cache_k.rearrange("b l s (g h) m d -> (b l) g s (h m d)", h=2)
            cv_v = cache_v.rearrange("b l s (g h) d -> (b l) g s (h d)", h=2)
            pool.sem_inc(s["small_free"], 1)
            pool.sem_inc(s["attn_free"], 1)
            pool.sem_inc(s["newk_free"], 1)
            pool.sem_inc(s["newv_free"], 1)

            def link(ins):
                ins.then_inc(s["pool"], 1)
                pool.wait_ge(s["pool"], seen("pool"))

            with seen.loop("layer", DEPTH) as l:
                pool.wait_ge(s["small_free"], seen("small_free"))
                seen.settle()
                pool.dma_start(sm[:], small[l]).then_inc(s["small_in"], 16)
                pool.wait_ge(s["hready"], seen("hready"))
                seen.settle()
                pool.dma_start(inv[:], inv_in.partition_broadcast(P)).then_inc(s["pool_in"], 16)
                for a in (0, CPAD + LAT, CLEN - CPAD):
                    nc.gpsimd.memset(zc[:, 1:, a:a + CPAD], 0.0)
                for n, a in enumerate((0, PPAD + LAT, PLEN - PPAD)):
                    ins = nc.gpsimd.memset(up[:, :, a:a + PPAD], 0.0)
                ins.then_inc(s["pads"], 1)
                pool.wait_ge(s["pads"], seen("pads"))
                pool.wait_ge(s["pool_in"], seen("pool_in", 16))
                pool.wait_ge(s["up_ready"], seen("up_ready", 2))
                for g in range(GROUPS):
                    src, dst = up[:, g], pt1
                    link(nc.gpsimd.tensor_tensor(dst[:, 1:PLEN], src[:, 0:PLEN - 1], src[:, 1:PLEN], ALU.add))
                    lo, hi = 1, PLEN
                    cur, nxt = pt1, pt2
                    for j in range(g):
                        w = 1 << j
                        lo, hi = lo + w, hi - w
                        link(nc.gpsimd.tensor_tensor(nxt[:, lo:hi], cur[:, lo - w:hi - w], cur[:, lo + w:hi + w], ALU.add))
                        cur, nxt = nxt, cur
                    link(nc.gpsimd.tensor_tensor(nxt[:, PPAD:PPAD + PRUN], cur[:, PPAD:PPAD + PRUN], inv[:, g], ALU.mult))
                    nc.gpsimd.tensor_tensor(up[:, g, PPAD:PPAD + PRUN], nxt[:, PPAD:PPAD + PRUN],
                                            up[:, g, PPAD:PPAD + PRUN], ALU.subtract).then_inc(s["pooled"], 1)
                    pool.wait_ge(s["pooled"], seen("pooled"))
                pool.wait_ge(s["z_ready"], seen("z_ready", 4))
                seen.settle()
                pool.dma_start(rope_c[:], cos_in).then_inc(s["table_in"], 16)
                seen.settle()
                pool.dma_start(rope_s[:], sin_in).then_inc(s["table_in"], 16)
                pool.dma_start(gains[:], gains_in[l]).then_inc(s["table_in"], 16)
                with seen.loop("pair", PAIRS) as g:
                    pool.wait_ge(s["attn_free"], seen("attn_free"))
                    seen.settle()
                    pool.dma_start(ck[:], ck_v[l, g]).then_inc(s["cache_in"], 16)
                    seen.settle()
                    pool.dma_start(vb[:, 4, :], cv_v[l, g]).then_inc(s["cache_in"], 16)
                    for u in range(2):
                        pool.wait_ge(s["qkt2"], seen("qkt2"))
                        nc.gpsimd.tensor_tensor(qk_a[:], qk_a[:], qk_b[:], ALU.add).then_inc(s["roped"], 1)
                        pool.wait_ge(s["roped"], seen("roped"))
                        seen.settle()
                        pool.dma_start(nk_v[l, 2 * g + u], qk_a[:, 4 * CW + P:5 * CW]).then_inc(s["newk_out"], 16)
                        pool.wait_ge(s["newk_out"], seen("newk_out", 16))
                        pool.sem_inc(s["newk_free"], 1)
                    pool.wait_ge(s["v_ready"], seen("v_ready", 2))
                    seen.settle()
                    pool.dma_start(nv_v[l, g], vb[:, 5, :]).then_inc(s["newv_out"], 16)
                    pool.wait_ge(s["newv_out"], seen("newv_out", 16))
                    pool.sem_inc(s["newv_free"], 1)

        def qkT_evac(act, seen, u):
            act.wait_ge(s["qkT"], seen("qkT"))
            nc.scalar.copy(qk_t[:, u, 0:2 * TOK].rearrange("p (a n) -> p a n", a=2)[:, :, 0:LAT], ps[:, 6:8, :])
            nc.scalar.copy(qk_t[:, u, :].rearrange("p (a n) -> p a n", n=P)[:, 4:11:6, :],
                           ps[:, 2 + 3 * u, 256:512].rearrange("p (a n) -> p a n", a=2)).then_inc(s["qkT_out"], 1)

        def exp_unit(act, seen, t):
            for m in range(2):
                act.wait_ge(s["maxd"], seen("maxd"))
                if m == 0:
                    act.wait_ge(s["aT"], seen("aT"))
                src = ps[:, 3 * m:3 * m + 2, 0:HALF] if t < 4 else ps[:, 3 * m, 0:CTX]
                dst = probs[:, m].rearrange("p (a n) -> p a n", a=2) if t < 4 else probs[:, m, 0:CTX]
                nc.scalar.activation(dst, src, ACT.Exp, scale=SCALE, bias=st[:, 36 + m:37 + m],
                                     accum_out=st[:, 40 + m:41 + m]).then_inc(s["expd"], 1)
            act.wait_ge(s["aT"], seen("aT", 0) + 1)
            act.wait_ge(s["av"], seen("av"))
            if t < 4:
                nc.scalar.copy(at_[:].rearrange("p a n -> p (a n)"), flat[:, 6 * 512:6 * 512 + TOK]).then_inc(s["aT_out"], 1)
            else:
                nc.scalar.copy(at_[:, 0], ps[:, 6, 0:P]).then_inc(s["aT_out"], 1)

        @block.scalar
        def _(act):
            seen = Seen(act, "act", s["settled"])

            def link(ins):
                ins.then_inc(s["act"], 1)
                act.wait_ge(s["act"], seen("act"))

            def split_high(slot, rslot):
                act.wait_ge(s[f"raw_full{rslot}"], seen(f"raw_full{rslot}", 32))
                act.wait_ge(s[f"split_free{slot}"], seen(f"split_free{slot}"))
                nc.scalar.copy(w_hi[:, slot], raw[:, rslot]).then_inc(s["hi_done"], 1)

            def skip_raw(rslot, n=1):
                seen(f"raw_full{rslot}", 32 * n)

            def norm(shift):
                for k in range(KT):
                    nc.scalar.activation(mm_[:, k], x[:, k], ACT.Square).then_inc(s["sq"], 1)
                act.wait_ge(s["row_a"], seen("row_a"))
                nc.scalar.activation(row[:], row[:], ACT.Sqrt).then_inc(s["row_b"], 1)
                act.wait_ge(s["mods_ready"], seen("mods_ready"))
                for k in range(KT):
                    act.wait_ge(s["tnorm"], seen("tnorm"))
                    for c, (a, b) in ((1, (0, LAT)), (0, (LAT, TOK))):
                        ins = nc.scalar.activation(mm_[:, k, a:b], mm_[:, k, a:b], ACT.Identity,
                                                   scale=coef[:, k, c:c + 1], bias=mods[:, shift + k, c:c + 1])
                    ins.then_inc(s["hnorm"], 1)

            act.wait_ge(s["const_in"], 64)
            nc.scalar.activation(cs[:], cs[:], ACT.Silu).then_inc(s["cs_ready"], 1)
            for k in range(KT):
                act.wait_ge(s["tr_in"], seen("tr_in"))
                b = 2 * (k % 2)
                nc.scalar.copy(x[:, k], flat[:, b * 512:b * 512 + TOK]).then_inc(s["tr_out"], 1)
            act.wait_ge(s["tr_out"], seen("tr_out", KT))
            with seen.loop("layer", DEPTH) as l:
                skip_raw(0, 4)
                skip_raw(1, 4)
                norm(0)
                for k in range(KT):
                    act.wait_ge(s["hnorm"], seen("hnorm"))
                    ins = nc.scalar.copy(h_hi[:, k], mm_[:, k])
                    ins.then_inc(s["row_c"], 1)
                act.wait_ge(s["lam_a"], seen("lam_a"))
                nc.scalar.activation(st[:, 2:4], st[:, 0:2], ACT.Exp).then_inc(s["lam_b"], 1)
                act.wait_ge(s["pads"], seen("pads"))
                act.wait_ge(s["hready"], seen("hready"))
                split_high(0, 0)
                split_high(1, 1)
                for n in range(3):
                    for u in range(2):
                        if n < 2:
                            split_high(u, u)
                        act.wait_ge(s["proj"], seen("proj"))
                        lat = ps[:, 4 * u:4 * u + 4, :].rearrange("p (j h) q -> p j h q", h=2)[:, :, 0, :]
                        cx = ps[:, 4 * u:4 * u + 4, 0:CTX].rearrange("p (j h) q -> p j h q", h=2)[:, :, 1, :]
                        if n == 0:
                            nc.scalar.activation(sg[:, 2 * u:2 * u + 2, 0:LAT], lat, ACT.Sigmoid)
                            nc.scalar.activation(sg[:, 2 * u:2 * u + 2, LAT:TOK], cx, ACT.Sigmoid).then_inc(s[f"set_free{u}"], 1)
                        if n == 2:
                            nc.scalar.copy(up[:, 2 * u:2 * u + 2, PPAD:PPAD + LAT], lat)
                            nc.scalar.copy(up[:, 2 * u:2 * u + 2, 2 * PPAD + LAT:2 * PPAD + TOK], cx).then_inc(s["up_ready"], 1)
                skip_raw(0, 2)
                skip_raw(1, 2)
                for g in range(GROUPS):
                    act.wait_ge(s["poolmm"], seen("poolmm"))
                    b = 2 * (g % 2)
                    nc.scalar.mul(brp[:, g], flat[:, b * 512:b * 512 + TOK],
                                  small_at("pool_scale")[:, g:g + 1]).then_inc(s["pool_br"], 1)
                with seen.loop("pair", PAIRS) as g:
                    split_high(0, 0)
                    split_high(1, 0)
                    skip_raw(1, 2)
                    for u in range(2):
                        act.wait_ge(s["proj"], seen("proj"))
                        act.wait_ge(s["newk_free"], seen("newk_free"))
                        nc.scalar.activation(qk_a[:], flat[:, 1536 * u:1536 * u + 1280], ACT.Square).then_inc(s["qksq"], 1)
                        act.wait_ge(s["qkss"], seen("qkss"))
                        nc.scalar.activation(st[:, 8:28], st[:, 8:28], ACT.Sqrt).then_inc(s["qksqrt"], 1)
                        if u == 0:
                            split_high(0, 0)
                            skip_raw(1)
                            qkT_evac(act, seen, 0)
                    act.wait_ge(s["proj"], seen("proj"))
                    act.wait_ge(s["newv_free"], seen("newv_free"))
                    nc.scalar.copy(vb[:, 0:4, :], flat[:, 0:1024].rearrange("p (t n) -> p t n", n=CW)).then_inc(s["v_ready"], 1)
                    nc.scalar.copy(vb[:, 5, :], flat[:, 1024:1280]).then_inc(s["v_ready"], 1)
                    qkT_evac(act, seen, 1)
                    act.wait_ge(s["qkT"], seen("qkT"))
                    nc.scalar.copy(qk_t[:, :, 1152:1280], ps[:, 6, 0:CW].rearrange("p (u n) -> p u n", u=2)).then_inc(s["qkT_out"], 1)
                    act.wait_ge(s["qkT_out"], seen("qkT_out", 3))
                    for u in range(2):
                        for t in range(TT):
                            exp_unit(act, seen, t)
                        act.wait_ge(s["av"], seen("av", 0) + 1)
                        nc.scalar.copy(ot[:, 2 * g + u, 0:LAT], ps[:, 2, :])
                        nc.scalar.copy(ot[:, 2 * g + u, LAT:TOK], ps[:, 5, 0:CTX]).then_inc(s["o_out"], 1)
                act.wait_ge(s["o_out"], seen("o_out", 2 * PAIRS))
                act.wait_ge(s["newk_free"], seen("newk_free", 0) + 1)
                act.wait_ge(s["newv_free"], seen("newv_free", 0) + 1)
                for h in range(HEADS):
                    nc.scalar.activation(mm_[:, h], ot[:, h], ACT.Square).then_inc(s["o_sq"], 1)
                for h in range(HEADS):
                    act.wait_ge(s["o_var"], seen("o_var"))
                    nc.scalar.activation(row[:], row[:], ACT.Sqrt).then_inc(s["o_sqrt"], 1)
                act.wait_ge(s["ln_d"], seen("ln_d"))
                for j in range(GROUPS):
                    nc.scalar.activation(mm_[:, j, 0:LAT], zc[:, j, 0:LAT], ACT.Square)
                    nc.scalar.activation(mm_[:, j, LAT:TOK], zc[:, j, LAT + CPAD:CRUN], ACT.Square).then_inc(s["ln_sq"], 1)
                act.wait_ge(s["ln_var"], seen("ln_var"))
                nc.scalar.activation(row2[:], row2[:], ACT.Sqrt).then_inc(s["ln_sqrt"], 1)
                act.wait_ge(s["ln_n"], seen("ln_n"))
                for j in range(GROUPS):
                    for a, b, z in ((0, LAT, 0), (LAT, TOK, CPAD)):
                        ins = nc.scalar.activation(brc[:, j, a:b], zc[:, j, a + z:b + z], ACT.Silu,
                                                   scale=small_at("ln_g")[:, j:j + 1], bias=small_at("ln_b")[:, j:j + 1])
                    ins.then_inc(s["branch_c"], 1)
                act.wait_ge(s["branch_c"], seen("branch_c", GROUPS))
                with seen.loop("merge", 4) as n:
                    for b in range(3):
                        split_high(b % 2, 0)
                        skip_raw(1)
                        act.wait_ge(s["proj"], seen("proj"))
                        act.wait_ge(s["merged"], seen("merged"))
                        for j in range(2):
                            for h in range(2):
                                ins = nc.scalar.activation(sigd[:, 2 * j + h], ps[:, 2 * j + h, 0:HALF], ACT.Sigmoid,
                                                           bias=sm[:, bass.ds(2 * n + (SMALL["b_gate"][0] + 8 * b + j), 1)])
                        ins.then_inc(s["sig"], 1)
                        act.wait_ge(s["sig"], seen("sig"))
                        seen("proj")
                skip_raw(0, 2)
                skip_raw(1, 2)
                seen("proj", 4)
                act.wait_ge(s["xo_done"], seen("xo_done"))
                norm(24)
                seen("hnorm", KT)
                act.wait_ge(s["rt_a"], seen("rt_a"))
                nc.scalar.activation(aff[:], aff[:], ACT.Exp).then_inc(s["rt_b"], 1)
                for t in range(TT):
                    act.wait_ge(s["h2tok_ps"], seen("h2tok_ps"))
                    b = 2 * (t % 2)
                    nc.scalar.copy(t_hi[:, t], flat[:, b * 512:b * 512 + D]).then_inc(s["h2tok_hi"], 1)

                def high(n, done):
                    r = n % RING
                    act.wait_ge(s[f"mfull{r}"], seen(f"mfull{r}", 16))
                    if done:
                        act.wait_ge(s["mdone"], seen("mdone", 0) + done)
                    nc.scalar.copy(m_hi[:, r], m_raw[:, r]).then_inc(s["m_high"], 1)

                def silu(c):
                    nc.scalar.activation(hid[:], ps[0:SLOTS, 2 * c, :], ACT.Silu).then_inc(s["silu"], 1)

                def turned_high(c):
                    act.wait_ge(s["hid_t"], seen("hid_t"))
                    nc.scalar.copy(ht_hi[:, 4 * c:4 * c + 4], ps[:, 6 + c, :].rearrange("p (k n) -> p k n", k=4)[:, :, 0:SLOTS]).then_inc(s["ht_high"], 1)

                def rows_out():
                    act.wait_ge(s["xg_ps"], seen("xg_ps"))
                    nc.scalar.copy(xg[:], flat[0:SLOTS, 0:D]).then_inc(s["xg_out"], 1)
                    act.wait_ge(s["xs_ps"], seen("xs_ps"))
                    nc.scalar.copy(xs_hi[:], ps[:, 2:4, :].rearrange("p b (k n) -> p (b k) n", k=4)[:, :, 0:SLOTS]).then_inc(s["xs_high"], 1)

                def expert(last):
                    high(4, 1)
                    high(5, 2)
                    silu(0)
                    for n in (6, 7, 8, 9):
                        high(n, n - 3)
                    turned_high(0)
                    silu(1)
                    high(10, 7)
                    high(11, 8)
                    act.wait_ge(s["pt_ps"], seen("pt_ps"))
                    nc.scalar.copy(st[0:SLOTS, 32:33], ps[0:SLOTS, 6, P:P + 1])
                    nc.scalar.copy(ptk[:, 0:LAT], ps[0:SLOTS, 7, :])
                    nc.scalar.copy(ptk[:, LAT:TOK], ps[0:SLOTS, 6, 0:CTX]).then_inc(s["pt_out"], 1)
                    if not last:
                        high(0, 9)
                    turned_high(1)
                    if not last:
                        high(1, 10)
                        high(2, 11)
                    act.wait_ge(s["mdone"], seen("mdone", 0) + NCH)
                    act.wait_ge(s["pt_out"], seen("pt_out"))
                    nc.scalar.activation(ye_hi[:], flat[0:SLOTS, 4 * 512:6 * 512], ACT.Copy, scale=st[0:SLOTS, 32:33]).then_inc(s["ye_hi"], 1)
                    if not last:
                        high(3, NCH)
                        rows_out()
                    seen("mdone", NCH)

                for n in range(RING):
                    high(n, 0)
                rows_out()
                with seen.loop("experts", EXPERTS - 1) as e:
                    expert(False)
                expert(True)
                act.wait_ge(s["layer_done"], seen("layer_done"))
            for t in range(TT):
                act.wait_ge(s["out_ps"], seen("out_ps"))
                b = 2 * (t % 2)
                nc.scalar.copy(xtok[:, t], flat[:, b * 512:b * 512 + D]).then_inc(s["out_sb"], 1)

        @block.vector
        def _(dve):
            seen = Seen(dve, "dve", s["settled"])

            def link(ins):
                ins.then_inc(s["dve"], 1)
                dve.wait_ge(s["dve"], seen("dve"))

            def link2(ins):
                ins.then_inc(s["ada_out"], 1)
                dve.wait_ge(s["ada_out"], seen("ada_out"))

            def add_mods_of(a):
                dve.wait_ge(s["ada"], seen("ada"))
                b0 = SMALL["b_ada"][0]
                nc.vector.tensor_tensor(mods[:, bass.ds(2 * a, 2), :], ada_ps[:, 0:2, :],
                                        sm[:, bass.ds(2 * a + b0, 2)].unsqueeze(2).to_broadcast([P, 2, 2]), ALU.add).then_inc(s["ada_out"], 1)
                seen("ada_out")

            def split_low(slot, rslot):
                dve.wait_ge(s["hi_done"], seen("hi_done"))
                nc.vector.tensor_tensor(w_lo[:, slot], raw[:, rslot], w_hi[:, slot].bitcast(F32),
                                        ALU.subtract).then_inc(s[f"split{slot}"], 1)
                dve.wait_ge(s[f"split{slot}"], seen(f"split{slot}"))
                dve.sem_inc(s[f"raw_free{rslot}"], 1)

            def norm():
                dve.wait_ge(s["ss"], seen("ss"))
                nc.vector.tensor_scalar(row[:].rearrange("p (a n) -> p a n", a=2), ps[:, 0:2, 0:HALF], 1.0 / D, EPS,
                                        ALU.mult, ALU.add).then_inc(s["row_a"], 1)
                dve.wait_ge(s["row_b"], seen("row_b"))
                link(nc.vector.reciprocal(row[:], row[:]))
                for k in range(KT):
                    nc.vector.tensor_tensor(mm_[:, k], x[:, k], row[:], ALU.mult).then_inc(s["tnorm"], 1)

            def coefficients(scale, g):
                for c in range(2):
                    ins = nc.vector.scalar_tensor_tensor(coef[:, :, c], mods[:, scale:scale + KT, c], 1.0, small_at(g), ALU.add, ALU.mult)
                ins.then_inc(s["mods_ready"], 1)

            def add_mods(a, b):
                link2(nc.vector.tensor_tensor(mods[:, a:b, :], ada_ps[:, a:b, :],
                                             small_at("b_ada")[:, a:b].unsqueeze(2).to_broadcast([P, b - a, 2]), ALU.add))

            dve.sem_inc(s["set_free0"], 1)
            dve.sem_inc(s["set_free1"], 1)
            dve.sem_inc(s["merged"], 1)
            dve.sem_inc(s["scat_out"], 1)
            with seen.loop("layer", DEPTH) as l:
                dve.wait_ge(s["small_in"], seen("small_in", 16))
                dve.wait_ge(s["ada"], seen("ada", 8))
                add_mods(0, 16)
                coefficients(8, "rms1")
                lv = small_at("lam_vec").rearrange("p (a b n) -> p a b n", a=2, b=2)
                link(nc.vector.tensor_tensor(st[:, 0:2], st[:, 0:2], st[:, 0:2], ALU.bypass) if False else
                     nc.vector.tensor_tensor(row2[:, 0:128].rearrange("p (a n) -> p a n", a=2), lv[:, :, 0, :], lv[:, :, 1, :], ALU.mult))
                nc.vector.tensor_reduce(st[:, 0:2], row2[:, 0:128].rearrange("p (a n) -> p a n", a=2), AX.X, ALU.add).then_inc(s["lam_a"], 1)
                norm()
                for k in range(KT):
                    dve.wait_ge(s["row_c"], seen("row_c"))
                    ins = nc.vector.tensor_tensor(h_lo[:, k], mm_[:, k], h_hi[:, k].bitcast(F32), ALU.subtract)
                ins.then_inc(s["hready"], 1)
                dve.wait_ge(s["lam_b"], seen("lam_b"))
                link(nc.vector.scalar_tensor_tensor(st[:, 4:5], st[:, 3:4], small_at("lam_init"), st[:, 2:3], ALU.subtract, ALU.subtract))
                link(nc.vector.tensor_tensor(st[:, 5:6], small_at("subln"), small_at("one_minus"), ALU.mult))
                split_low(0, 0)
                split_low(1, 1)
                for n in range(3):
                    for u in range(2):
                        if n < 2:
                            split_low(u, u)
                        if n == 1:
                            dve.wait_ge(s["proj"], seen("proj", 3 if u == 0 else 1))
                            lat = ps[:, 4 * u:4 * u + 4, :].rearrange("p (j h) q -> p j h q", h=2)[:, :, 0, :]
                            cx = ps[:, 4 * u:4 * u + 4, 0:CTX].rearrange("p (j h) q -> p j h q", h=2)[:, :, 1, :]
                            if u == 0:
                                dve.wait_ge(s["pads"], seen("pads"))
                            nc.vector.tensor_tensor(zc[:, 2 * u + 1:2 * u + 3, CPAD:CPAD + LAT], lat, sg[:, 2 * u:2 * u + 2, 0:LAT], ALU.mult).then_inc(s["z_ready"], 1)
                            nc.vector.tensor_tensor(zc[:, 2 * u + 1:2 * u + 3, 2 * CPAD + LAT:CLEN - CPAD], cx, sg[:, 2 * u:2 * u + 2, LAT:TOK], ALU.mult).then_inc(s["z_ready"], 1)
                            dve.wait_ge(s["z_ready"], seen("z_ready", 2))
                            dve.sem_inc(s[f"set_free{u}"], 1)
                seen("proj", 2)
                dve.wait_ge(s["ada"], seen("ada", 4))
                add_mods(16, 24)
                dve.wait_ge(s["table_in"], seen("table_in", 48))
                for g, tab in enumerate((rope_c, rope_s)):
                    v = tab[:].rearrange("p (t n) -> p t n", n=CW)
                    link(nc.vector.tensor_tensor(v, v, gains[:, g:g + 1, :].to_broadcast([P, TT, CW]), ALU.mult))

                with seen.loop("pair", PAIRS) as g:
                    taps = [0]

                    def conv(n):
                        for _ in range(n):
                            j = taps[0]
                            if j == TAPS:
                                return
                            w = sm[:, bass.ds(TAPS * g + (SMALL["conv_w"][0] + j), 1)]
                            src = zc[:, bass.ds(g + 1, 1), j:j + CRUN].rearrange("p a n -> p (a n)")
                            dst = zc[:, bass.ds(g, 1), 0:CRUN].rearrange("p a n -> p (a n)")
                            if j == 0:
                                link(nc.vector.tensor_scalar(dst, src, w, sm[:, bass.ds(g + SMALL["conv_b"][0], 1)], ALU.mult, ALU.add))
                            else:
                                link(nc.vector.scalar_tensor_tensor(dst, src, w, dst, ALU.mult, ALU.add))
                            taps[0] += 1

                    add_mods_of(3 * g + 12)
                    split_low(0, 0)
                    split_low(1, 0)
                    seen("proj", 3)
                    for u in range(2):
                        main = flat[:, 1536 * u:1536 * u + 1280]
                        dve.wait_ge(s["qksq"], seen("qksq"))
                        link(nc.vector.tensor_reduce(st[:, 8:28], qk_a[:].rearrange("p (a n) -> p a n", n=HD), AX.X, ALU.add))
                        nc.vector.tensor_scalar(st[:, 8:28], st[:, 8:28], 1.0 / HD, EPS, ALU.mult, ALU.add).then_inc(s["qkss"], 1)
                        dve.wait_ge(s["qksqrt"], seen("qksqrt"))
                        link(nc.vector.reciprocal(st[:, 8:28], st[:, 8:28]))
                        main3 = main.rearrange("p (a n) -> p a n", n=HD)
                        link(nc.vector.tensor_tensor(main3, main3, st[:, 8:28].unsqueeze(2).to_broadcast([P, 20, HD]), ALU.mult))
                        nc.vector.tensor_tensor(qk_a[:], main, rope_c[:], ALU.mult)
                        m4 = main.rearrange("p (a r n) -> p a r n", r=2, n=16)
                        b4 = qk_b[:].rearrange("p (a r n) -> p a r n", r=2, n=16)
                        s4 = rope_s[:].rearrange("p (a r n) -> p a r n", r=2, n=16)
                        nc.vector.tensor_tensor(b4[:, :, 0], m4[:, :, 1], s4[:, :, 0], ALU.mult)
                        nc.vector.tensor_tensor(b4[:, :, 1], m4[:, :, 0], s4[:, :, 1], ALU.mult).then_inc(s["qkt2"], 1)
                        if u == 0:
                            add_mods_of(3 * g + 13)
                            split_low(0, 0)
                    add_mods_of(3 * g + 14)
                    for u in range(2):
                        for t in range(TT):
                            n = TOK if t < 4 else CTX
                            for m in range(2):
                                dve.wait_ge(s["s_done"], seen("s_done"))
                                src = ps[:, 3 * m:3 * m + 2, 0:HALF] if t < 4 else ps[:, 3 * m, 0:CTX]
                                link(nc.vector.tensor_reduce(st[:, 44 + m:45 + m], src, AX.XY if t < 4 else AX.X, ALU.max))
                                nc.vector.tensor_scalar(st[:, 36 + m:37 + m], st[:, 44 + m:45 + m], -SCALE, None, ALU.mult).then_inc(s["maxd"], 1)
                            conv(2)
                            dve.wait_ge(s["expd"], seen("expd", 2))
                            link(nc.vector.reciprocal(st[:, 48:50], st[:, 40:42]))
                            link(nc.vector.tensor_scalar(st[:, 50:51], st[:, 49:50], st[:, 4:5], None, ALU.mult))
                            link(nc.vector.tensor_scalar(probs[:, 1, 0:n], probs[:, 1, 0:n], st[:, 50:51], None, ALU.mult))
                            nc.vector.scalar_tensor_tensor(probs[:, 0, 0:n], probs[:, 0, 0:n], st[:, 48:49], probs[:, 1, 0:n],
                                                           ALU.mult, ALU.add).then_inc(s["a_ready"], 1)
                            conv(1 if (u, t) != (1, 4) else TAPS)
                    assert taps[0] == TAPS
                nc.vector.tensor_copy(st[:, 60:61], st[:, 4:5]).then_inc(s["conv_done"], 1)
                for h in range(HEADS):
                    b = 2 * (h % 2)
                    dve.wait_ge(s["o_ss"], seen("o_ss"))
                    nc.vector.tensor_scalar(row[:].rearrange("p (a n) -> p a n", a=2), ps[:, b:b + 2, 0:HALF], 1.0 / DV, EPS,
                                            ALU.mult, ALU.add).then_inc(s["o_var"], 1)
                    dve.wait_ge(s["o_sqrt"], seen("o_sqrt"))
                    link(nc.vector.reciprocal(row[:], row[:]))
                    nc.vector.scalar_tensor_tensor(ot[:, h], ot[:, h], st[:, 5:6], row[:], ALU.mult, ALU.mult).then_inc(s["o_norm"], 1)
                    dve.wait_ge(s["o_norm"], seen("o_norm"))
                dve.wait_ge(s["ln_sum"], seen("ln_sum"))
                link(nc.vector.tensor_scalar(row2[:], flat[:, 4 * 512:4 * 512 + TOK], 1.0 / 512, None, ALU.mult))
                for j in range(GROUPS):
                    nc.vector.tensor_tensor(zc[:, j, 0:LAT], zc[:, j, 0:LAT], row2[:, 0:LAT], ALU.subtract)
                    ins = nc.vector.tensor_tensor(zc[:, j, LAT + CPAD:CRUN], zc[:, j, LAT + CPAD:CRUN], row2[:, LAT:TOK], ALU.subtract)
                ins.then_inc(s["ln_d"], 1)
                dve.wait_ge(s["ln_sum"], seen("ln_sum"))
                dve.wait_ge(s["ln_d"], seen("ln_d"))
                nc.vector.tensor_scalar(row2[:], flat[:, 6 * 512:6 * 512 + TOK], 1.0 / 512, EPS, ALU.mult, ALU.add).then_inc(s["ln_var"], 1)
                dve.wait_ge(s["ln_sqrt"], seen("ln_sqrt"))
                link(nc.vector.reciprocal(row2[:], row2[:]))
                for j in range(GROUPS):
                    nc.vector.tensor_tensor(zc[:, j, 0:LAT], zc[:, j, 0:LAT], row2[:, 0:LAT], ALU.mult)
                    ins = nc.vector.tensor_tensor(zc[:, j, LAT + CPAD:CRUN], zc[:, j, LAT + CPAD:CRUN], row2[:, LAT:TOK], ALU.mult)
                ins.then_inc(s["ln_n"], 1)
                merged4 = mm_[:].rearrange("p (n j) (h q) -> p n (j h) q", j=2, h=2)
                dve.wait_ge(s["branch_c"], seen("branch_c", GROUPS))
                with seen.loop("merge", 4) as n:
                    for b in range(3):
                        split_low(b % 2, 0)
                        dve.wait_ge(s["sig"], seen("sig"))
                        dve.sem_inc(s["set_free0"], 1)
                        dve.wait_ge(s["proj"], seen("proj", 2))
                        if b == 0:
                            nc.vector.tensor_tensor(merged4[:, n], ps[:, 4:8, 0:HALF], sigd[:], ALU.mult).then_inc(s["merged"], 1)
                            dve.wait_ge(s["merged"], seen("merged") + 1)
                        else:
                            nc.vector.tensor_tensor(prod[:], ps[:, 4:8, 0:HALF], sigd[:], ALU.mult).then_inc(s["merged"], 1)
                            dve.wait_ge(s["merged"], seen("merged") + 1)
                            link(nc.vector.tensor_tensor(merged4[:, n], merged4[:, n], prod[:], ALU.add))
                        dve.sem_inc(s["set_free1"], 1)
                dve.sem_inc(s["m_ready"], 1)
                for c in range(4):
                    u = c % 2
                    dve.wait_ge(s["proj"], seen("proj"))
                    for j in range(2):
                        ct = 2 * c + j
                        nc.vector.scalar_tensor_tensor(x[:, ct, 0:LAT], ps[:, 4 * u + 2 * j, :], mods[:, 16 + ct, 1:2],
                                                       x[:, ct, 0:LAT], ALU.mult, ALU.add)
                        ins = nc.vector.scalar_tensor_tensor(x[:, ct, LAT:TOK], ps[:, 4 * u + 2 * j + 1, 0:CTX], mods[:, 16 + ct, 0:1],
                                                             x[:, ct, LAT:TOK], ALU.mult, ALU.add)
                    link(ins)
                    dve.sem_inc(s[f"set_free{u}"], 1)
                dve.sem_inc(s["xo_done"], 1)
                coefficients(32, "rms2")
                norm()
                dve.wait_ge(s["logits"], seen("logits"))
                lg = ps[:, 4, 0:TT * EXPERTS].rearrange("p (t e) -> p t e", e=EXPERTS)
                link(nc.vector.tensor_reduce(st[:, 8:13], lg, AX.X, ALU.max))
                nc.vector.tensor_tensor(aff[:], lg, st[:, 8:13].unsqueeze(2).to_broadcast([P, TT, EXPERTS]), ALU.subtract).then_inc(s["rt_a"], 1)
                dve.wait_ge(s["rt_b"], seen("rt_b"))
                link(nc.vector.tensor_reduce(st[:, 8:13], aff[:], AX.X, ALU.add))
                link(nc.vector.reciprocal(st[:, 8:13], st[:, 8:13]))
                nc.vector.tensor_tensor(aff[:], aff[:], st[:, 8:13].unsqueeze(2).to_broadcast([P, TT, EXPERTS]), ALU.mult).then_inc(s["aff_r"], 1)
                dve.sem_inc(s["small_free"], 1)
                dve.wait_ge(s["affT"], seen("affT"))
                link(nc.vector.tensor_copy(affw[:], flat[0:EXPERTS, 5 * 512:5 * 512 + TOK]))
                for a, b, rounds, tag in ((0, LAT, CAP_LAT // 8, "top_lat"), (LAT, TOK, CAP_CTX // 8, "top_ctx")):
                    with seen.loop(tag, rounds) as i:
                        link(nc.vector.max(top8[:], affw[:, a:b]))
                        seen.settle()
                        link(nc.vector.match_replace(affw[:, a:b], top8[:], affw[:, a:b], -1.0))
                link(nc.vector.tensor_scalar(mask[:], affw[:], 0.0, None, ALU.is_lt))
                link(nc.vector.memset(affw[:], 1.0))
                nc.vector.tensor_tensor_scan(cum[:, 0:LAT], affw[:, 0:LAT], mask[:, 0:LAT], 0.0, ALU.mult, ALU.add)
                link(nc.vector.tensor_tensor_scan(cum[:, LAT:TOK], affw[:, LAT:TOK], mask[:, LAT:TOK], float(CAP_LAT), ALU.mult, ALU.add))
                link(nc.vector.tensor_tensor(cum[:], cum[:], mask[:], ALU.mult))
                nc.vector.tensor_scalar(cum[:], cum[:], -1.0, None, ALU.add).then_inc(s["topk"], 1)
                nc.vector.memset(pos[:], -1.0).then_inc(s["pos_r"], 1)
                for t in range(TT):
                    dve.wait_ge(s["h2tok_hi"], seen("h2tok_hi"))
                    b = 2 * (t % 2)
                    nc.vector.tensor_tensor(t_lo[:, t], flat[:, b * 512:b * 512 + D], t_hi[:, t].bitcast(F32), ALU.subtract).then_inc(s["h2tok_lo"], 1)
                dve.wait_ge(s["posT"], seen("posT"))
                dve.wait_ge(s["pos_r"], seen("pos_r"))
                link(nc.vector.tensor_copy(pos[:, :, 0:EXPERTS], ps[:, 7, 0:TT * EXPERTS].rearrange("p (t e) -> p t e", e=EXPERTS)))

                def choose(e):
                    nc.vector.tensor_tensor(pick[:], slot_no[:].unsqueeze(1).to_broadcast([P, TT, SLOTS]),
                                            pos[:, :, bass.ds(e, 1)].to_broadcast([P, TT, SLOTS]), ALU.is_equal).then_inc(s["picked"], 1)

                def low(n):
                    r = n % RING
                    dve.wait_ge(s["m_high"], seen("m_high"))
                    nc.vector.tensor_tensor(m_lo[:, r], m_raw[:, r], m_hi[:, r].bitcast(F32), ALU.subtract).then_inc(s["msplit"], 1)

                def gate_up(c):
                    dve.wait_ge(s["silu"], seen("silu"))
                    dve.wait_ge(s["mdone"], seen("mdone", 0) + 4 * c + 4)
                    nc.vector.tensor_tensor(hid[:], hid[:], ps[0:SLOTS, 2 * c + 1, :], ALU.mult).then_inc(s["hidd"], 1)

                def turned_low(c):
                    dve.wait_ge(s["ht_high"], seen("ht_high"))
                    nc.vector.tensor_tensor(ht_lo[:, 4 * c:4 * c + 4], ps[:, 6 + c, :].rearrange("p (k n) -> p k n", k=4)[:, :, 0:SLOTS],
                                            ht_hi[:, 4 * c:4 * c + 4].bitcast(F32), ALU.subtract).then_inc(s["ht_out"], 1)

                def rows_low():
                    dve.wait_ge(s["xs_high"], seen("xs_high"))
                    nc.vector.tensor_tensor(xs_lo[:], ps[:, 2:4, :].rearrange("p b (k n) -> p (b k) n", k=4)[:, :, 0:SLOTS],
                                            xs_hi[:].bitcast(F32), ALU.subtract).then_inc(s["xs_out"], 1)

                def expert(e, last):
                    for n in (4, 5, 6):
                        low(n)
                    gate_up(0)
                    for n in (7, 8, 9):
                        low(n)
                    turned_low(0)
                    low(10)
                    gate_up(1)
                    low(11)
                    dve.wait_ge(s["pt_ps"], seen("pt_ps"))
                    if not last:
                        choose(e + 1)
                        low(0)
                    turned_low(1)
                    if not last:
                        low(1)
                        low(2)
                    dve.wait_ge(s["ye_hi"], seen("ye_hi"))
                    nc.vector.scalar_tensor_tensor(ye_lo[:], flat[0:SLOTS, 4 * 512:6 * 512], st[0:SLOTS, 32:33], ye_hi[:].bitcast(F32),
                                                   ALU.mult, ALU.subtract).then_inc(s["ye_lo"], 1)
                    if not last:
                        low(3)
                    dve.wait_ge(s["scat"], seen("scat"))
                    for i in range(KT):
                        nc.vector.scalar_tensor_tensor(x[:, i, LAT:TOK], ps[:, 6 + i // 4, (i % 4) * P:(i % 4 + 1) * P],
                                                       mods[:, 40 + i, 0:1], x[:, i, LAT:TOK], ALU.mult, ALU.add)
                    for i in range(KT):
                        if i == 2 and not last:
                            rows_low()
                        dve.wait_ge(s["scat"], seen("scat"))
                        nc.vector.scalar_tensor_tensor(x[:, i, 0:LAT], ps[:, LATBANK[i % 4], :], mods[:, 40 + i, 1:2], x[:, i, 0:LAT],
                                                       ALU.mult, ALU.add).then_inc(s["scat_out"], 1)
                    seen("mdone", NCH)
                    dve.wait_ge(s["scat_out"], seen("scat_out", KT) + 1)

                choose(0)
                for n in range(RING):
                    low(n)
                rows_low()
                with seen.loop("experts", EXPERTS - 1) as e:
                    expert(e, False)
                expert(EXPERTS - 1, True)
                dve.sem_inc(s["layer_done"], 1)

        @block.tensor
        def _(pe):
            seen = Seen(pe, "pe", s["settled"])
            pe.sem_inc(s["split_free0"], 1)
            pe.sem_inc(s["split_free1"], 1)
            pe.sem_inc(s["aT"], 1)
            pe.sem_inc(s["av"], 1)

            def three(out, wh, wl, xh, xl, first, last):
                pe.matmul(out, wh, xh, start=first, stop=False)
                pe.matmul(out, wh, xl, start=False, stop=False)
                return pe.matmul(out, wl, xh, start=False, stop=last)

            def wait_split(slot):
                pe.wait_ge(s[f"split{slot}"], seen(f"split{slot}"))

            def wait_set(u):
                pe.wait_ge(s[f"set_free{u}"], seen(f"set_free{u}"))

            seq = ((0, LAT), (LAT, TOK))
            halves = ((0, HALF), (HALF, TOK))

            def feature_split(slot, u, cuts):
                for j in range(2):
                    for c, (a, b) in enumerate(cuts):
                        for k in range(KT):
                            ins = three(ps[:, 4 * u + 2 * j + c, 0:b - a], w_hi[:, slot, k, j * P:(j + 1) * P],
                                        w_lo[:, slot, k, j * P:(j + 1) * P], h_hi[:, k, a:b], h_lo[:, k, a:b], k == 0, k == KT - 1)
                ins.then_inc(s["proj"], 1)

            def feature_raw(rslot, u, cuts, src, kt, free_raw):
                for j in range(2):
                    for c, (a, b) in enumerate(cuts):
                        for k in range(kt):
                            ins = pe.matmul(ps[:, 4 * u + 2 * j + c, 0:b - a], raw[:, rslot, k, j * P:(j + 1) * P],
                                            src[:, k, a:b], start=(k == 0), stop=(k == kt - 1))
                ins.then_inc(s["proj"], 1)
                pe.wait_ge(s["proj"], seen("proj", 0))
                pe.sem_inc(s[f"raw_free{rslot}"], 1)

            def ada(a, rslot):
                pe.wait_ge(s[f"raw_full{rslot}"], seen(f"raw_full{rslot}", 32))
                for j in range(2):
                    for k in range(KT):
                        out = ps[:, 7, 2 * j:2 * j + 2] if a is None else flat[:, bass.ds(4 * a + (7 * 512 + 2 * j), 2)]
                        ins = pe.matmul(out, raw[:, rslot, k, j * P:(j + 1) * P], cs[:, k, :], start=(k == 0), stop=(k == KT - 1))
                ins.then_inc(s["ada"], 1)
                pe.wait_ge(s["ada"], seen("ada"))
                pe.sem_inc(s[f"raw_free{rslot}"], 1)

            def sum_squares(n_in, sem_in):
                for k in range(n_in):
                    pe.wait_ge(s[sem_in], seen(sem_in))
                    for c, (a, b) in enumerate(halves):
                        ins = pe.matmul(ps[:, c, 0:HALF], ones[:], mm_[:, k, a:b], start=(k == 0), stop=(k == n_in - 1), skip_group_check=True)
                ins.then_inc(s["ss"], 1)

            def token_major(slot, off, last_wait=False):
                for t in range(TT):
                    if last_wait and t == 4:
                        pe.wait_ge(s["qkT_out"], seen("qkT_out"))
                    for k in range(KT):
                        ins = three(flat[:, off + t * CW:off + (t + 1) * CW], h_hi[:, k, t * P:(t + 1) * P], h_lo[:, k, t * P:(t + 1) * P],
                                    w_hi[:, slot, k, :], w_lo[:, slot, k, :], k == 0, k == KT - 1)
                ins.then_inc(s["proj"], 1)
                pe.wait_ge(s["proj"], seen("proj", 0))
                pe.sem_inc(s[f"split_free{slot}"], 1)

            def turn_qk(u):
                pe.wait_ge(s["roped"], seen("roped"))
                for b in range(2):
                    if b == 1:
                        pe.wait_ge(s["ada_out"], seen("ada_out"))
                    for t in range(4):
                        pe.transpose(ps[:, 6 + b, t * P:(t + 1) * P], qk_a[:, t * CW + b * P:t * CW + (b + 1) * P], ident[:])
                for b in range(2):
                    ins = pe.transpose(ps[:, 2 + 3 * u, 256 + b * P:256 + (b + 1) * P], qk_a[:, 4 * CW + b * P:4 * CW + (b + 1) * P], ident[:])
                ins.then_inc(s["qkT"], 1)

            def scores(i):
                u, t = divmod(i, TT)
                for m in range(2):
                    if i:
                        pe.wait_ge(s["expd"], seen("expd"))
                    q = qk_t[64 * m:64 * m + 64, u, t * P:(t + 1) * P]
                    if t < 4:
                        for c in range(2):
                            ins = pe.matmul(ps[:, 3 * m + c, 0:HALF], q, qk_t[64 * m:64 * m + 64, u, TOK + c * HALF:TOK + (c + 1) * HALF],
                                            start=True, stop=True)
                    else:
                        ins = pe.matmul(ps[:, 3 * m, 0:CTX], q, qk_t[64 * m:64 * m + 64, u, 2 * TOK:2 * TOK + CTX], start=True, stop=True)
                    ins.then_inc(s["s_done"], 1)

            def values(i):
                u, t = divmod(i, TT)
                pe.wait_ge(s["a_ready"], seen("a_ready"))
                nk = TT if t < 4 else 1
                for c in range(nk):
                    ins = pe.transpose(flat[:, 6 * 512 + c * P:6 * 512 + (c + 1) * P], probs[:, 0, c * P:(c + 1) * P], ident[:])
                ins.then_inc(s["aT"], 1)
                pe.wait_ge(s["aT_out"], seen("aT_out"))
                if t == 0 and u == 1:
                    pe.wait_ge(s["o_out"], seen("o_out"))
                out = ps[:, 2, t * P:(t + 1) * P] if t < 4 else ps[:, 5, 0:P]
                for c in range(nk):
                    ins = pe.matmul(out, vb[:, c if t < 4 else 5, u * P:(u + 1) * P], at_[:, c, :], start=(c == 0), stop=(c == nk - 1))
                ins.then_inc(s["av"], 1)

            pe.wait_ge(s["const_in"], 64)
            pe.wait_ge(s["x_in"], 32)
            for k in range(KT):
                if k >= 2:
                    pe.wait_ge(s["tr_out"], seen("tr_out"))
                b = 2 * (k % 2)
                for t in range(TT):
                    ins = pe.transpose(flat[:, b * 512 + t * P:b * 512 + (t + 1) * P], xtok[:, t, k * P:(k + 1) * P], ident[:])
                ins.then_inc(s["tr_in"], 1)
            pe.wait_ge(s["tr_out"], seen("tr_out", 2))
            pe.wait_ge(s["cs_ready"], 1)
            with seen.loop("layer", DEPTH) as l:
                sum_squares(KT, "sq")
                with seen.loop("ada1", 4) as i:
                    for u in range(2):
                        ada(2 * i + u, u)
                seen("raw_full0", 96)
                seen("raw_full1", 96)
                pe.wait_ge(s["row_a"], seen("row_a"))
                pe.wait_ge(s["hready"], seen("hready"))
                pe.wait_ge(s["ada_out"], seen("ada_out"))
                with seen.loop("conv_pool", 3) as i:
                    for u in range(2):
                        wait_split(u)
                        wait_set(u)
                        feature_split(u, u, seq)
                        pe.wait_ge(s["proj"], seen("proj"))
                        pe.sem_inc(s[f"split_free{u}"], 1)
                pe.wait_ge(s["up_ready"], seen("up_ready", 2))
                pe.sem_inc(s["set_free0"], 1)
                pe.sem_inc(s["set_free1"], 1)
                with seen.loop("ada2", 2) as i:
                    for u in range(2):
                        ada(2 * i + (8 + u), u)
                for g in range(GROUPS):
                    pe.wait_ge(s["pooled"], seen("pooled"))
                    if g >= 2:
                        pe.wait_ge(s["pool_br"], seen("pool_br"))
                    b = 2 * (g % 2)
                    pw = small_at("pool_w")[:, g * P:(g + 1) * P]
                    pe.matmul(ps[:, b, :], pw, up[:, g, PPAD:PPAD + LAT], start=True, stop=True)
                    pe.matmul(ps[:, b + 1, 0:CTX], pw, up[:, g, 2 * PPAD + LAT:2 * PPAD + TOK], start=True, stop=True).then_inc(s["poolmm"], 1)
                pe.wait_ge(s["pool_br"], seen("pool_br", 2))
                pe.wait_ge(s["ada_out"], seen("ada_out"))
                with seen.loop("pair", PAIRS) as g:
                    for u in range(2):
                        if u == 1:
                            pe.wait_ge(s["ada_out"], seen("ada_out"))
                        ada(None, 1)
                        wait_split(u)
                        seen("raw_full0", 32)
                        seen("proj")
                        token_major(u, 1536 * u)
                    turn_qk(0)
                    wait_split(0)
                    seen("raw_full0", 32)
                    seen("proj")
                    token_major(0, 0, True)
                    ada(None, 1)
                    turn_qk(1)
                    pe.wait_ge(s["qkT_out"], seen("qkT_out"))
                    pe.wait_ge(s["cache_in"], seen("cache_in", 32))
                    for u in range(2):
                        ins = pe.transpose(ps[:, 6, u * P:(u + 1) * P], ck[:, u * P:(u + 1) * P], ident[:])
                    ins.then_inc(s["qkT"], 1)
                    pe.wait_ge(s["qkT_out"], seen("qkT_out"))
                    pe.wait_ge(s["v_ready"], seen("v_ready", 2))
                    scores(0)
                    for i in range(2 * TT):
                        if i + 1 < 2 * TT:
                            scores(i + 1)
                        values(i)
                    pe.wait_ge(s["av"], seen("av", 10) + 1)
                    pe.sem_inc(s["attn_free"], 1)
                    pe.wait_ge(s["expd"], seen("expd", 2))
                    pe.wait_ge(s["o_out"], seen("o_out"))
                for h in range(HEADS):
                    b = 2 * (h % 2)
                    pe.wait_ge(s["o_sq"], seen("o_sq"))
                    if h >= 2:
                        pe.wait_ge(s["o_var"], seen("o_var"))
                    for c, (a, e) in enumerate(halves):
                        ins = pe.matmul(ps[:, b + c, 0:HALF], ones[:], mm_[:, h, a:e], start=True, stop=True)
                    ins.then_inc(s["o_ss"], 1)
                pe.wait_ge(s["conv_done"], seen("conv_done"))
                for j in range(GROUPS):
                    pe.matmul(ps[:, 4, :], ones[:], zc[:, j, 0:LAT], start=(j == 0), stop=(j == GROUPS - 1), skip_group_check=True)
                    ins = pe.matmul(ps[:, 5, 0:CTX], ones[:], zc[:, j, LAT + CPAD:CRUN], start=(j == 0), stop=(j == GROUPS - 1), skip_group_check=True)
                ins.then_inc(s["ln_sum"], 1)
                for j in range(GROUPS):
                    pe.wait_ge(s["ln_sq"], seen("ln_sq"))
                    pe.matmul(ps[:, 6, :], ones[:], mm_[:, j, 0:LAT], start=(j == 0), stop=(j == GROUPS - 1), skip_group_check=True)
                    ins = pe.matmul(ps[:, 7, 0:CTX], ones[:], mm_[:, j, LAT:TOK], start=(j == 0), stop=(j == GROUPS - 1), skip_group_check=True)
                ins.then_inc(s["ln_sum"], 1)
                pe.wait_ge(s["o_norm"], seen("o_norm", HEADS))
                pe.wait_ge(s["o_var"], seen("o_var", 2))
                pe.wait_ge(s["branch_c"], seen("branch_c", GROUPS))
                with seen.loop("merge", 4) as n:
                    for b, (src, kt) in enumerate(((ot, KT), (brp, GROUPS), (brc, GROUPS))):
                        wait_split(b % 2)
                        seen("raw_full0", 32)
                        wait_set(0)
                        feature_split(b % 2, 0, halves)
                        pe.wait_ge(s["proj"], seen("proj"))
                        pe.sem_inc(s[f"split_free{b % 2}"], 1)
                        pe.wait_ge(s["raw_full1"], seen("raw_full1", 32))
                        wait_set(1)
                        seen("proj")
                        feature_raw(1, 1, halves, src, kt, True)
                pe.wait_ge(s["proj"], seen("proj", 0))
                pe.sem_inc(s["d_done"], 1)
                pe.wait_ge(s["m_ready"], seen("m_ready"))
                with seen.loop("out", 2) as i:
                    for u in range(2):
                        pe.wait_ge(s[f"raw_full{u}"], seen(f"raw_full{u}", 32))
                        wait_set(u)
                        seen("proj")
                        feature_raw(u, u, seq, mm_, KT, True)
                pe.wait_ge(s["xo_done"], seen("xo_done"))
                sum_squares(KT, "sq")
                pe.wait_ge(s["hnorm"], seen("hnorm", 2 * KT))
                for t in range(TT):
                    for k in range(KT):
                        ins = pe.matmul(ps[:, 4, t * EXPERTS:(t + 1) * EXPERTS], mm_[:, k, t * P:(t + 1) * P],
                                        small_at("router")[:, k * EXPERTS:(k + 1) * EXPERTS], start=(k == 0), stop=(k == KT - 1))
                ins.then_inc(s["logits"], 1)
                pe.wait_ge(s["row_a"], seen("row_a"))
                for t in range(TT):
                    if t >= 2:
                        pe.wait_ge(s["h2tok_lo"], seen("h2tok_lo"))
                    b = 2 * (t % 2)
                    for k in range(KT):
                        ins = pe.transpose(flat[:, b * 512 + k * P:b * 512 + (k + 1) * P], mm_[:, k, t * P:(t + 1) * P], ident[:])
                    ins.then_inc(s["h2tok_ps"], 1)
                    if t == 1:
                        pe.wait_ge(s["aff_r"], seen("aff_r"))
                        for c in range(TT):
                            ins = pe.transpose(flat[0:EXPERTS, 5 * 512 + c * P:5 * 512 + (c + 1) * P], aff[:, c, :], ident[:])
                        ins.then_inc(s["affT"], 1)
                        pe.wait_ge(s["topk"], seen("topk"))
                        seen.settle()
                        for c in range(TT):
                            ins = pe.transpose(ps[:, 7, c * EXPERTS:(c + 1) * EXPERTS], cum[:, c * P:(c + 1) * P], ident[0:EXPERTS, 0:EXPERTS])
                        ins.then_inc(s["posT"], 1)

                def gather():
                    pe.wait_ge(s["picked"], seen("picked"))
                    for c in range(2):
                        for t in range(TT):
                            for part in (t_hi, t_lo):
                                ins = pe.matmul(ps[0:SLOTS, c, :], pick[:, t, :], part[:, t, c * EW:(c + 1) * EW],
                                                start=(t == 0 and part is t_hi), stop=(t == TT - 1 and part is t_lo))
                    ins.then_inc(s["xg_ps"], 1)

                def turn_rows():
                    for k in range(KT):
                        ins = pe.transpose(flat[:, 2 * 512 + k * P:2 * 512 + k * P + SLOTS], xg[:, k * P:(k + 1) * P], ident[0:SLOTS, 0:SLOTS])
                    ins.then_inc(s["xs_ps"], 1)

                def product(n):
                    w, k0, c, bank = CHUNKS[n]
                    hi, lo = (xs_hi, xs_lo) if w < 2 else (ht_hi, ht_lo)
                    pe.wait_ge(s["msplit"], seen("msplit"))
                    for k in range(EK):
                        ins = three(ps[0:SLOTS, bank, :], hi[:, k0 + k, :], lo[:, k0 + k, :], m_hi[:, n % RING, k, :], m_lo[:, n % RING, k, :],
                                    k0 + k == 0, k0 + k == KT - 1)
                    ins.then_inc(s["mdone"], 1)

                def turn_hid(c):
                    pe.wait_ge(s["hidd"], seen("hidd"))
                    for k in range(4):
                        ins = pe.transpose(ps[:, 6 + c, k * P:k * P + SLOTS], hid[:, k * P:(k + 1) * P], ident[0:SLOTS, 0:SLOTS])
                    ins.then_inc(s["hid_t"], 1)

                def turn_pick(e):
                    pe.wait_ge(s["ht_out"], seen("ht_out"))
                    for t in range(TT):
                        pe.matmul(ps[0:SLOTS, 6, P:P + 1], pick[:, t, :].bitcast(F32), aff[:, t, bass.ds(e, 1)], start=(t == 0), stop=(t == TT - 1))
                    pe.transpose(ps[0:SLOTS, 6, 0:P], pick[:, 4, :].bitcast(F32), ident[:])
                    for t in range(4):
                        ins = pe.transpose(ps[0:SLOTS, 7, t * P:(t + 1) * P], pick[:, t, :].bitcast(F32), ident[:])
                    ins.then_inc(s["pt_ps"], 1)

                def two(out, i, a, b):
                    pe.matmul(out, ye_hi[:, i * P:(i + 1) * P], ptk[:, a:b], start=True, stop=False)
                    return pe.matmul(out, ye_lo[:, i * P:(i + 1) * P], ptk[:, a:b], start=False, stop=True)

                def expert(e, last):
                    pe.wait_ge(s["xs_out"], seen("xs_out"))
                    for n in range(6):
                        product(n)
                    turn_hid(0)
                    product(6)
                    product(7)
                    turn_pick(e)
                    pe.wait_ge(s["scat_out"], seen("scat_out", 0) + 1)
                    product(8)
                    pe.wait_ge(s["pt_out"], seen("pt_out"))
                    turn_hid(1)
                    product(9)
                    pe.wait_ge(s["ht_out"], seen("ht_out"))
                    product(10)
                    product(11)
                    if not last:
                        gather()
                        pe.wait_ge(s["xg_out"], seen("xg_out"))
                    pe.wait_ge(s["ye_hi"], seen("ye_hi"))
                    pe.wait_ge(s["ye_lo"], seen("ye_lo"))
                    for i in range(KT):
                        ins = two(ps[:, 6 + i // 4, (i % 4) * P:(i % 4 + 1) * P], i, LAT, TOK)
                    ins.then_inc(s["scat"], 1)
                    for i in range(KT):
                        if i == 2 and not last:
                            turn_rows()
                        if i >= 4:
                            pe.wait_ge(s["scat_out"], seen("scat_out", 0) + i - 2)
                        two(ps[:, LATBANK[i % 4], :], i, 0, LAT).then_inc(s["scat"], 1)
                    pe.wait_ge(s["scat_out"], seen("scat_out", 0) + 7)
                    seen("scat_out", KT)

                pe.wait_ge(s["h2tok_lo"], seen("h2tok_lo", 2))
                gather()
                pe.wait_ge(s["xg_out"], seen("xg_out"))
                turn_rows()
                with seen.loop("experts", EXPERTS - 1) as e:
                    expert(e, False)
                expert(EXPERTS - 1, True)
                pe.wait_ge(s["scat_out"], seen("scat_out", 0) + 1)
            for t in range(TT):
                if t >= 2:
                    pe.wait_ge(s["out_sb"], seen("out_sb"))
                b = 2 * (t % 2)
                for k in range(KT):
                    ins = pe.transpose(flat[:, b * 512 + k * P:b * 512 + (k + 1) * P], x[:, k, t * P:(t + 1) * P], ident[:])
                ins.then_inc(s["out_ps"], 1)


def constants():
    ident = np.eye(P, dtype=np.float32)
    rows, cols = np.divmod(np.arange(LAT), 64)
    inv = (10000.0 ** (-np.arange(16, dtype=np.float32) / np.float32(16))).astype(np.float32)
    c = np.ones((TT, P, 4, 2, 2, 16), np.float32)
    sn = np.zeros((TT, P, 4, 2, 2, 16), np.float32)
    for a, at in enumerate((rows, cols)):
        ang = (at.astype(np.float32)[:, None] * inv[None]).reshape(4, P, 1, 1, 16)
        c[:4, :, :, a] = np.cos(ang)
        sn[:4, :, :, a] = np.sin(ang) * np.array([-1, 1], np.float32)[:, None]
    cos = np.ascontiguousarray(c.transpose(1, 0, 2, 3, 4, 5)).reshape(P, TT * CW)
    sin = np.ascontiguousarray(sn.transpose(1, 0, 2, 3, 4, 5)).reshape(P, TT * CW)
    cnt = np.zeros((GROUPS, PRUN), np.float32)
    for g in range(GROUPS):
        w = 1 << g
        for at, n in ((0, LAT), (LAT + PPAD, CTX)):
            t = np.arange(n)
            cnt[g, at:at + n] = 1.0 / (np.clip(t + w, 0, n) - np.clip(t - w, 0, n))
    slot = np.ascontiguousarray(np.broadcast_to(np.arange(SLOTS, dtype=np.float32), (P, SLOTS)))
    return ident, cos, sin, cnt, slot


def kernel(**inputs):
    import math
    import concourse.bacc as _bacc
    from concourse.bass_utils import run_bass_kernel_spmd as _run

    a = {k: np.ascontiguousarray(v) for k, v in inputs.items()}

    def cols(v, n):
        return v.reshape(DEPTH, n, P).transpose(0, 2, 1)

    def rows(v):
        return np.broadcast_to(v.reshape(DEPTH, 1, -1), (DEPTH, P, v[0].size))

    qg, kg = a["q_norm_g"], a["k_norm_g"]
    qkg = np.concatenate([qg, qg, kg, kg], 1)
    swapped = qkg.reshape(DEPTH, 8, 2, 16)[:, :, ::-1].reshape(DEPTH, 256)
    lam_init = np.array([0.8 - 0.6 * math.exp(-0.3 * l) for l in range(DEPTH)], np.float32)
    one_minus = np.array([1.0 - (0.8 - 0.6 * math.exp(-0.3 * l)) for l in range(DEPTH)], np.float32)
    parts = {
        "rms1": cols(a["rms1_g"], 8), "rms2": cols(a["rms2_g"], 8), "b_ada": cols(a["b_ada"], 48),
        "pool_scale": cols(a["pool_scale"], 4), "conv_b": cols(a["conv_b"], 4), "ln_g": cols(a["conv_ln_g"], 4),
        "ln_b": cols(a["conv_ln_b"], 4), "b_gate": cols(a["b_gate"], 24), "subln": cols(a["subln_g"], 1),
        "conv_w": a["conv_w"].reshape(DEPTH, TAPS, 4, P).transpose(0, 3, 2, 1).reshape(DEPTH, P, 4 * TAPS),
        "router": a["w_router"].reshape(DEPTH, 8, P, 16).transpose(0, 2, 1, 3).reshape(DEPTH, P, 128),
        "lam_vec": rows(a["lam_vec"]),
        "lam_init": rows(lam_init), "one_minus": rows(one_minus),
        "pool_w": a["pool_w"].transpose(0, 2, 1, 3).reshape(DEPTH, P, 512),
    }
    small = np.concatenate([parts[n] for n in SMALL], axis=2)
    ident, cos, sin, cnt, slot = constants()
    cvecs = np.stack([a["c_ctx"], a["c"][0]], 1).reshape(KT, P, 2).transpose(1, 0, 2)
    given = {
        "x_prompt": a["x_prompt"], "x_sample": a["x_sample"], "cvecs": cvecs, "cache_k": a["cache_k"], "cache_v": a["cache_v"],
        "small": small, "gains_in": np.stack([rows(qkg), rows(swapped)], 2), "w_ada": a["w_ada"], "w_in": a["w_in"], "w_proj_a": a["w_proj_a"], "w_proj_b": a["w_proj_b"],
        "w_proj_c": a["w_proj_c"], "w_gate": a["w_gate"], "w_out": a["w_out"], "w1": a["w1"], "w3": a["w3"], "w2": a["w2"],
        "ident_in": ident, "cos_in": cos, "sin_in": sin, "inv_in": cnt, "slot_in": slot,
    }
    shapes = [a["x_prompt"].shape, a["x_sample"].shape, (1, DEPTH, CTX, HEADS, 2, HD), (1, DEPTH, CTX, HEADS, DV)]

    def program():
        nc = _bacc.Bacc("TRN2", target_bir_lowering=False, num_devices=1)
        args = [nc.dram_tensor(f"in_{n}", v.shape, F32, kind="ExternalInput").ap() for n, v in given.items()]
        args += [nc.dram_tensor(f"out_{i}", sh, F32, kind="ExternalOutput").ap() for i, sh in enumerate(shapes)]
        build(nc, *args)
        return nc

    for _ in range(6):
        PER_TURN.pop("changed", None)
        nc = program()
        if not PER_TURN.get("changed"):
            break
    arrays = {f"in_{n}": np.ascontiguousarray(v) for n, v in given.items()}
    r = _run(nc, [arrays], core_ids=[0])
    return tuple(r.results[0][f"out_{i}"] for i in range(4))
```

```python
from contextlib import ExitStack, contextmanager

import numpy as np

import concourse.bass as bass
from concourse import mybir

F32 = mybir.dt.float32
F32R = mybir.dt.float32r
ACT = mybir.ActivationFunctionType
ALU = mybir.AluOpType
AX = mybir.AxisListType

P = 128
D = 1024
KT = D // P
LAT, CTX = 512, 128
TOK = LAT + CTX
HALF = TOK // 2
TT = TOK // P
DEPTH = 2
HEADS, HD, DV = 8, 64, 128
PAIRS = HEADS // 2
CW = 256
EXPERTS, FF = 16, 1024
CAP_LAT, CAP_CTX = 2 * LAT // EXPERTS, 2 * CTX // EXPERTS
SLOTS = CAP_LAT + CAP_CTX
EPS = 1e-6
SCALE = HD ** -0.5
GROUPS = 4
TAPS, CPAD = 31, 15
CLEN = CPAD + LAT + CPAD + CTX + CPAD
CRUN = LAT + CPAD + CTX
PPAD = 8
PLEN = PPAD + LAT + PPAD + CTX + PPAD
PRUN = LAT + PPAD + CTX
Q0, K0, V0, POOL0, CONVA0, CONVB0 = 0, 1024, 2048, 3072, 3584, 4096
EW = 512
EK = 4
RING = 4
CHUNKS = [(0, 0, 0, 0), (0, 4, 0, 0), (1, 0, 0, 1), (1, 4, 0, 1), (0, 0, 1, 2), (0, 4, 1, 2), (1, 0, 1, 3), (1, 4, 1, 3),
          (2, 0, 0, 4), (2, 0, 1, 5), (2, 4, 0, 4), (2, 4, 1, 5)]
NCH = len(CHUNKS)
SCAT0 = 4
MERGE = [(q, b) for q in range(2) for b in (1, 0, 2)]
PIECES = ((0, 0, HALF, 1), (1, HALF, LAT, 1), (1, LAT, TOK, 2))
LATBANK = (4, 5, 0, 1, 0, 1, 4, 5)

SMALL = {}
_at = 0
for _name, _n in (("rms1", 8), ("rms2", 8), ("b_ada", 48), ("pool_scale", 4), ("conv_b", 4), ("ln_g", 4),
                  ("ln_b", 4), ("b_gate", 24), ("subln", 1), ("conv_w", 4 * TAPS), ("router", 8 * 16),
                  ("lam_vec", 256), ("lam_init", 1), ("one_minus", 1),
                  ("pool_w", 512)):
    SMALL[_name] = (_at, _at + _n)
    _at += _n
NSMALL = _at

PER_TURN = {}


class Seen:

    def __init__(self, eng, name, settled):
        self.eng, self.name, self.n, self.base, self.settled = eng, name, {}, {}, settled

    def settle(self):
        self.eng.sem_inc(self.settled, 1)

    def __call__(self, sem, k=1):
        self.n[sem] = self.n.get(sem, 0) + k
        return self.base.get(sem, 0) + self.n[sem]

    @contextmanager
    def loop(self, what, count):
        key = f"{self.name}.{what}"
        per = PER_TURN.get(key, {})
        n, base = dict(self.n), dict(self.base)
        self.settle()
        with self.eng.Fori(0, count) as i:
            for sem in set(n) | set(per):
                b = base.get(sem, 0) + n.get(sem, 0)
                self.base[sem] = b + per[sem] * i if per.get(sem) else b
            self.n = {}
            yield i
            used = {k: v for k, v in self.n.items() if v}
            if used != per:
                PER_TURN[key] = used
                PER_TURN["changed"] = True
        self.base = base
        self.n = {s: n.get(s, 0) + count * used.get(s, 0) for s in set(n) | set(used)}


def build(nc, x_prompt, x_sample, cvecs, cache_k, cache_v, small, gains_in, w_ada, w_in, w_proj_a, w_proj_b,
          w_proj_c, w_gate, w_out, w1, w3, w2, ident_in, cos_in, sin_in, inv_in, slot_in,
          y_prompt, y_sample, new_k, new_v, dbg=None):
    ctx = ExitStack()
    with ctx:
        start = (nc.sbuf_base + 63) // 64 * 64
        free = {"at": start}

        def region(nbytes):
            at = free["at"]
            free["at"] = at + (nbytes + 31) // 32 * 32
            return at

        def sb(name, shape, at, dt=F32):
            return nc.alloc_sbuf_tensor_at(name, shape, dt, offset=at)

        r_x, r_m, r_ring, r_raw, r_t2 = region(20480), region(22176), region(98304), region(16384), region(40960)
        x = sb("x", [P, KT, TOK], r_x)
        mm_ = sb("m", [P, KT, TOK], r_m)
        xtok = sb("xtok", [P, TT, D], r_m)
        sg = sb("conv_gate", [P, GROUPS, TOK], r_m)
        inv = sb("inv_count", [P, GROUPS, PRUN], r_m + 10240)
        rope_c = sb("rope_c", [P, TT * CW], r_m)
        rope_s = sb("rope_s", [P, TT * CW], r_m + 5120)
        qk_a = sb("qk_a", [P, TT * CW], r_m + 10240)
        qk_b = sb("qk_b", [P, TT * CW], r_m + 15360)
        gains = sb("gains", [P, 2, CW], r_m + 15360)
        xg = sb("xg", [SLOTS, D], r_m)
        xs_hi = sb("xs_hi", [P, KT, SLOTS], r_m + 4096, F32R)
        xs_lo = sb("xs_lo", [P, KT, SLOTS], r_m + 6656, F32R)
        pick = sb("pick", [P, TT, SLOTS], r_m + 9216, F32R)
        hid = sb("hid", [SLOTS, EW], r_m + 10816)
        ht_hi = sb("hid_t_hi", [P, KT, SLOTS], r_m + 12864, F32R)
        ht_lo = sb("hid_t_lo", [P, KT, SLOTS], r_m + 15424, F32R)
        ye_lo = sb("ye_lo", [SLOTS, D], r_m + 17984, F32R)
        m_raw = sb("m_raw", [P, RING, EK, EW], r_ring)
        m_hi = sb("m_hi", [P, RING, EK, EW], r_ring + 32768, F32R)
        m_lo = sb("m_lo", [P, RING, EK, EW], r_ring + 65536, F32R)
        ada_row = sb("ada_row", [2, 8 * CW], r_ring)
        ada_row2 = sb("ada_row2", [2, 4 * CW], r_ring + 73728)
        h_hi = sb("h_hi", [P, KT, TOK], r_ring, F32R)
        h_lo = sb("h_lo", [P, KT, TOK], r_ring + 20480, F32R)
        w_hi = sb("w_hi", [P, 2, KT, CW], r_ring + 40960, F32R)
        w_lo = sb("w_lo", [P, 2, KT, CW], r_ring + 57344, F32R)
        ot = sb("ot", [P, HEADS, TOK], r_ring + 73728)
        at_ = sb("attn_t", [P, TT, P], r_ring + 94208)
        ck = sb("cache_k_tok", [P, CW], r_ring + 94208 + 2560)
        raw = sb("raw", [P, 2, KT, CW], r_raw)
        affw = sb("affw", [EXPERTS, TOK], r_raw)
        cum = sb("cum", [EXPERTS, TOK], r_raw + 2560)
        mask = sb("mask", [EXPERTS, TOK], r_raw + 5120)
        zc = sb("zc", [P, GROUPS + 1, CLEN], r_t2)
        brp = sb("pool_branch", [P, GROUPS, TOK], r_t2 + 13728)
        up = sb("up", [P, GROUPS, PLEN], r_t2 + 23968)
        pt1 = sb("pool_t1", [P, PLEN], r_t2 + 34592)
        pt2 = sb("pool_t2", [P, PLEN], r_t2 + 37248)
        qk_t = sb("qk_t", [P, 2, TOK + TOK + CTX], r_t2 + 23968)
        probs = sb("probs", [P, 2, TOK], r_t2 + 23968 + 11264)
        brc = sb("conv_branch", [P, GROUPS, TOK], r_t2 + 23968)
        sigd = sb("sigd", [P, 4, HALF], r_t2 + 34208)
        prod = sb("prod", [P, 4, HALF], r_t2)
        t_hi = sb("h2tok_hi", [P, TT, D], r_t2, F32R)
        t_lo = sb("h2tok_lo", [P, TT, D], r_t2 + 20480, F32R)
        t_all = sb("h2tok", [P, TT, D], r_t2 + 20480)
        ident = sb("ident", [P, P], region(512))
        ones = sb("ones", [P, P], region(512))
        sm = sb("small", [P, NSMALL], region(4 * NSMALL))
        mods = sb("mods", [P, 48, 2], region(384))
        coef = sb("coef", [P, KT, 2], region(64))
        cs = sb("cs", [P, KT, 2], region(64))
        slot_no = sb("slot_no", [P, SLOTS], region(4 * SLOTS))
        pos = sb("pos", [P, TT, EXPERTS + 1], region(352))
        aff = sb("aff", [P, TT, EXPERTS], region(320))
        st = sb("stats", [P, 64], region(256))
        sel = sb("column_of_ones", [P, 2 * HEADS], region(64))
        top8 = sb("top8", [EXPERTS, 8], region(32))
        r_v = region(6656)
        vb = sb("v_pair", [P, TT + 1, CW], r_v)
        row = sb("row", [P, TOK], r_v)
        row2 = sb("row2", [P, TOK], r_v + 2560)
        ye_hi = sb("ye_hi", [SLOTS, D], r_v, F32R)
        ptk = sb("pick_t", [SLOTS, TOK], r_v + 4096, F32R)
        assert free["at"] <= nc.sbuf_usable_end, (free["at"], nc.sbuf_usable_end)

        ps = ctx.enter_context(nc.psum_tensor("ps", [P, 8, 512], F32))
        flat = ps[:].rearrange("p b n -> p (b n)")
        ada_ps = ps[:, 7, 0:96].rearrange("p (m c) -> p m c", c=2)

        def small_at(name):
            a, b = SMALL[name]
            return sm[:, a:b]

        names = """raw_full0 raw_full1 raw_free0 raw_free1 hi_done split0 split1 split_free0 split_free1 proj
        set_free0 set_free1 const_in x_in small_in small_free tr_in tr_out sq ss row_a row_b row_c tnorm hnorm hready
        cs_ready ada ada_row ada_t mods_ready lam_a lam_b z_ready pads up_ready pool_in pooled poolmm pool_br table_in
        qksq qkss qksqrt qkt2 roped qkT qkT_out newk_out newv_out newk_free newv_free v_ready cache_in s_done expd logits_out logits_t
        maxd a_ready aT aT_out av o_out conv_done ln_sum ln_d ln_sq ln_var ln_sqrt ln_n branch_c o_sq o_ss o_var
        o_sqrt o_inv o_norm mg_high mg_low sig merged xo_done logits rt_a rt_b aff_r affT topk posT pos_r h2tok_ps h2tok_hi h2tok_lo
        mfull0 mfull1 mfull2 mfull3 m_high msplit mdone silu hidd hid_t ht_high ht_out picked pt_ps pt_out xg_ps xg_out xs_ps
        xs_high xs_out ye_hi ye_lo scat scat_out layer_done m_ready ada_out out_ps out_sb y_out attn_free d_done
        dve act pool settled""".split()
        s = {n: ctx.enter_context(nc.semaphore("s_" + n)) for n in names}
        assert len(set(names)) == len(names)

        block = ctx.enter_context(nc.Block())
        xin = (x_sample, x_prompt)
        yout = (y_sample, y_prompt)

        @block.sync
        def _(sp):
            seen = Seen(sp, "sp", s["settled"])
            sp.dma_start(ident[:], ident_in).then_inc(s["const_in"], 16)
            sp.dma_start(slot_no[:], slot_in).then_inc(s["const_in"], 16)
            sp.dma_start(cs[:], cvecs).then_inc(s["const_in"], 16)
            sp.dma_start(xtok[:, 0:4, :], x_sample[0].rearrange("(t p) d -> p t d", p=P)).then_inc(s["x_in"], 16)
            sp.dma_start(xtok[:, 4, :], x_prompt[0]).then_inc(s["x_in"], 16)
            sp.sem_inc(s["raw_free0"], 1)
            sp.sem_inc(s["raw_free1"], 1)

            def chunk(slot, *parts):
                sp.wait_ge(s[f"raw_free{slot}"], seen(f"raw_free{slot}"))
                for dst, src in parts:
                    sp.dma_start(dst, src).then_inc(s[f"raw_full{slot}"], 16)

            def wide(slot, src):
                chunk(slot, (raw[:, slot, 0:4, :], src[:, 0:4, :]), (raw[:, slot, 4:8, :], src[:, 4:8, :]))

            ada_v = w_ada.rearrange("l (k p) (c n) -> l c p k n", p=P, n=CW)
            in_v = w_in.rearrange("l (k p) (c n) -> l c p k n", p=P, n=CW)
            in_h = w_in.rearrange("l (k p) (c n) -> l c p k n", p=P, n=P)
            gate_v = w_gate.rearrange("l (k p) (c n) -> l c p k n", p=P, n=CW)
            pa_v = w_proj_a.rearrange("l (k p) (c n) -> l c p k n", p=P, n=CW)
            pb_v = w_proj_b.rearrange("l (k p) (c n) -> l c p k n", p=P, n=CW)
            pc_v = w_proj_c.rearrange("l (k p) (c n) -> l c p k n", p=P, n=CW)
            out_v = w_out.rearrange("l (k p) (c n) -> l c p k n", p=P, n=CW)
            ex_v = [w.rearrange("l e (k p) n -> l e p k n", p=P) for w in (w1, w3, w2)]
            with seen.loop("layer", DEPTH) as l:
                with seen.loop("ada1", 4) as i:
                    for u in range(2):
                        wide(u, ada_v[l, 2 * i + u])
                for n, c0 in enumerate((POOL0, CONVB0, CONVA0)):
                    for u in range(2):
                        wide(u, in_v[l, c0 // CW + u])
                with seen.loop("ada2", 2) as i:
                    for u in range(2):
                        wide(u, ada_v[l, 2 * i + u + 8])
                with seen.loop("pair", PAIRS) as g:
                    for u in range(2):
                        chunk(0, (raw[:, 0, :, 0:P], in_h[l, Q0 // P + 2 * g + u]),
                              (raw[:, 0, :, P:CW], in_h[l, K0 // P + 2 * g + u]))
                        if u == 0:
                            wide(1, ada_v[l, 3 * g + 12])
                    wide(0, in_v[l, g + V0 // CW])
                    for u in (1, 2):
                        wide(1, ada_v[l, 3 * g + 12 + u])
                with seen.loop("merge", 2) as m:
                    for i, (q, b) in enumerate(MERGE):
                        wide(0, gate_v[l, 2 * m + (q + 4 * b)])
                        if b == 0:
                            wide(1, pa_v[l, 2 * m + q])
                        else:
                            src = (pb_v, pc_v)[b - 1][l, 2 * m + q]
                            chunk(1, (raw[:, 1, 0:2, :], src[:, 0:2, :]), (raw[:, 1, 2:4, :], src[:, 2:4, :]))
                with seen.loop("out", 2) as i:
                    for u in range(2):
                        wide(u, out_v[l, 2 * i + u])
                sp.wait_ge(s["d_done"], seen("d_done"))
                seen.settle()
                def expert_chunk(e, n, wait=True):
                    w, k, c, _ = CHUNKS[n]
                    if wait:
                        sp.wait_ge(s["msplit"], seen("msplit"))
                        seen.settle()
                    sp.dma_start(m_raw[:, n % RING], ex_v[w][l, e][:, k:k + EK, c * EW:(c + 1) * EW]).then_inc(s[f"mfull{n % RING}"], 16)

                for n in range(RING):
                    expert_chunk(0, n, False)
                with seen.loop("experts", EXPERTS - 1) as e:
                    for n in range(RING, NCH):
                        expert_chunk(e, n)
                    for n in range(RING):
                        expert_chunk(e + 1, n)
                for n in range(RING, NCH):
                    expert_chunk(EXPERTS - 1, n)
                seen("msplit", RING)
            y_v = y_sample[0].rearrange("(t p) d -> p t d", p=P)
            for t in range(TT):
                sp.wait_ge(s["out_sb"], seen("out_sb"))
                sp.dma_start(y_v[:, t] if t < 4 else y_prompt[0], xtok[:, t, :]).then_inc(s["y_out"], 16)
            sp.wait_ge(s["y_out"], 16 * TT)

        @block.gpsimd
        def _(pool):
            seen = Seen(pool, "pool", s["settled"])
            nc.gpsimd.memset(sel[:, 0:HEADS], 0.0)
            nc.gpsimd.memset(sel[:, HEADS:HEADS + 1], 1.0)
            nc.gpsimd.memset(sel[:, HEADS + 1:], 0.0)
            nc.gpsimd.memset(ones[:], 1.0).then_inc(s["const_in"], 16)
            nk_v = new_k.rearrange("b l s h m d -> (b l) h s (m d)")
            nv_v = new_v.rearrange("b l s (g h) d -> (b l) g s (h d)", h=2)
            ck_v = cache_k.rearrange("b l s (g h) m d -> (b l) g s (h m d)", h=2)
            cv_v = cache_v.rearrange("b l s (g h) d -> (b l) g s (h d)", h=2)
            pool.sem_inc(s["small_free"], 1)
            pool.sem_inc(s["attn_free"], 1)
            pool.sem_inc(s["newk_free"], 1)
            pool.sem_inc(s["newv_free"], 1)

            def link(ins):
                ins.then_inc(s["pool"], 1)
                pool.wait_ge(s["pool"], seen("pool"))

            with seen.loop("layer", DEPTH) as l:
                pool.wait_ge(s["small_free"], seen("small_free"))
                seen.settle()
                pool.dma_start(sm[:], small[l]).then_inc(s["small_in"], 16)
                pool.wait_ge(s["hready"], seen("hready"))
                seen.settle()
                pool.dma_start(inv[:], inv_in.partition_broadcast(P)).then_inc(s["pool_in"], 16)
                for a in (0, CPAD + LAT, CLEN - CPAD):
                    nc.gpsimd.memset(zc[:, 1:, a:a + CPAD], 0.0)
                for n, a in enumerate((0, PPAD + LAT, PLEN - PPAD)):
                    ins = nc.gpsimd.memset(up[:, :, a:a + PPAD], 0.0)
                ins.then_inc(s["pads"], 1)
                pool.wait_ge(s["pads"], seen("pads"))
                pool.wait_ge(s["pool_in"], seen("pool_in", 16))
                pool.wait_ge(s["up_ready"], seen("up_ready", 2))
                for g in range(GROUPS):
                    src, dst = up[:, g], pt1
                    link(nc.gpsimd.tensor_tensor(dst[:, 1:PLEN], src[:, 0:PLEN - 1], src[:, 1:PLEN], ALU.add))
                    lo, hi = 1, PLEN
                    cur, nxt = pt1, pt2
                    for j in range(g):
                        w = 1 << j
                        lo, hi = lo + w, hi - w
                        link(nc.gpsimd.tensor_tensor(nxt[:, lo:hi], cur[:, lo - w:hi - w], cur[:, lo + w:hi + w], ALU.add))
                        cur, nxt = nxt, cur
                    link(nc.gpsimd.tensor_tensor(nxt[:, PPAD:PPAD + PRUN], cur[:, PPAD:PPAD + PRUN], inv[:, g], ALU.mult))
                    nc.gpsimd.tensor_tensor(up[:, g, PPAD:PPAD + PRUN], nxt[:, PPAD:PPAD + PRUN],
                                            up[:, g, PPAD:PPAD + PRUN], ALU.subtract).then_inc(s["pooled"], 1)
                    pool.wait_ge(s["pooled"], seen("pooled"))
                pool.wait_ge(s["z_ready"], seen("z_ready", 2))
                seen.settle()
                pool.dma_start(rope_c[:], cos_in).then_inc(s["table_in"], 16)
                seen.settle()
                pool.dma_start(rope_s[:], sin_in).then_inc(s["table_in"], 16)
                pool.dma_start(gains[:], gains_in[l]).then_inc(s["table_in"], 16)
                with seen.loop("pair", PAIRS) as g:
                    pool.wait_ge(s["attn_free"], seen("attn_free"))
                    seen.settle()
                    pool.dma_start(ck[:], ck_v[l, g]).then_inc(s["cache_in"], 16)
                    seen.settle()
                    pool.dma_start(vb[:, 4, :], cv_v[l, g]).then_inc(s["cache_in"], 16)
                    for u in range(2):
                        pool.wait_ge(s["qkt2"], seen("qkt2"))
                        nc.gpsimd.tensor_tensor(qk_a[:], qk_a[:], qk_b[:], ALU.add).then_inc(s["roped"], 1)
                        pool.wait_ge(s["roped"], seen("roped"))
                        seen.settle()
                        pool.dma_start(nk_v[l, 2 * g + u], qk_a[:, 4 * CW + P:5 * CW]).then_inc(s["newk_out"], 16)
                        pool.wait_ge(s["newk_out"], seen("newk_out", 16))
                        pool.sem_inc(s["newk_free"], 1)
                    pool.wait_ge(s["v_ready"], seen("v_ready", 2))
                    seen.settle()
                    pool.dma_start(nv_v[l, g], vb[:, 5, :]).then_inc(s["newv_out"], 16)
                    pool.wait_ge(s["newv_out"], seen("newv_out", 16))
                    pool.sem_inc(s["newv_free"], 1)
                for t in range(TT):
                    pool.wait_ge(s["h2tok_hi"], seen("h2tok_hi"))
                    nc.gpsimd.tensor_tensor(t_lo[:, t], t_all[:, t], t_hi[:, t].bitcast(F32), ALU.subtract).then_inc(s["h2tok_lo"], 1)

        def qkT_evac(act, seen, u):
            act.wait_ge(s["qkT"], seen("qkT"))
            nc.scalar.copy(qk_t[:, u, 0:2 * TOK].rearrange("p (a n) -> p a n", a=2)[:, :, 0:LAT], ps[:, 6:8, :])
            ins = nc.scalar.copy(qk_t[:, u, :].rearrange("p (a n) -> p a n", n=P)[:, 4:11:6, :],
                                 ps[:, 2 + 3 * u, 256:512].rearrange("p (a n) -> p a n", a=2))
            if u == 0:
                ins = nc.scalar.copy(qk_t[:, :, 1152:1280], ps[:, 2, 0:CW].rearrange("p (u n) -> p u n", u=2))
            ins.then_inc(s["qkT_out"], 1)

        def exp_unit(act, seen, t):
            for m in range(2):
                act.wait_ge(s["maxd"], seen("maxd"))
                if m == 0:
                    act.wait_ge(s["aT"], seen("aT"))
                src = ps[:, 3 * m:3 * m + 2, 0:HALF] if t < 4 else ps[:, 3 * m, 0:CTX]
                dst = probs[:, m].rearrange("p (a n) -> p a n", a=2) if t < 4 else probs[:, m, 0:CTX]
                nc.scalar.activation(dst, src, ACT.Exp, scale=SCALE, bias=st[:, 36 + m:37 + m],
                                     accum_out=st[:, 40 + m:41 + m]).then_inc(s["expd"], 1)
            act.wait_ge(s["aT"], seen("aT", 0) + 1)
            act.wait_ge(s["av"], seen("av"))
            if t < 4:
                nc.scalar.copy(at_[:].rearrange("p a n -> p (a n)"), flat[:, 6 * 512:6 * 512 + TOK]).then_inc(s["aT_out"], 1)
            else:
                nc.scalar.copy(at_[:, 0], ps[:, 6, 0:P]).then_inc(s["aT_out"], 1)

        @block.scalar
        def _(act):
            seen = Seen(act, "act", s["settled"])

            def link(ins):
                ins.then_inc(s["act"], 1)
                act.wait_ge(s["act"], seen("act"))

            def split_high(slot, rslot):
                act.wait_ge(s[f"raw_full{rslot}"], seen(f"raw_full{rslot}", 32))
                act.wait_ge(s[f"split_free{slot}"], seen(f"split_free{slot}"))
                nc.scalar.copy(w_hi[:, slot], raw[:, rslot]).then_inc(s["hi_done"], 1)

            def skip_raw(rslot, n=1):
                seen(f"raw_full{rslot}", 32 * n)

            def ada_out(bank, dst, chunks):
                act.wait_ge(s["ada"], seen("ada", chunks))
                nc.scalar.copy(dst[:], flat[0:2, bank * 512:bank * 512 + CW * chunks]).then_inc(s["ada_row"], 1)

            def h_high(k):
                act.wait_ge(s["hnorm"], seen("hnorm"))
                nc.scalar.copy(h_hi[:, k], mm_[:, k]).then_inc(s["row_c"], 1)

            def squares(a, b):
                for k in range(a, b):
                    nc.scalar.activation(mm_[:, k], x[:, k], ACT.Square).then_inc(s["sq"], 1)

            def norm(shift):
                if shift == 0:
                    squares(0, KT)
                act.wait_ge(s["row_a"], seen("row_a"))
                nc.scalar.activation(row[:], row[:], ACT.Sqrt).then_inc(s["row_b"], 1)
                if shift == 0:
                    ada_out(2, ada_row, 8)
                    split_high(0, 0)
                    split_high(1, 1)
                act.wait_ge(s["mods_ready"], seen("mods_ready"))
                for k in range(KT):
                    act.wait_ge(s["tnorm"], seen("tnorm"))
                    for c, (a, b) in ((1, (0, LAT)), (0, (LAT, TOK))):
                        ins = nc.scalar.activation(mm_[:, k, a:b], mm_[:, k, a:b], ACT.Identity,
                                                   scale=coef[:, k, c:c + 1], bias=mods[:, shift + k, c:c + 1])
                    ins.then_inc(s["hnorm"], 1)
                    if shift == 0:
                        if k:
                            h_high(k - 1)
                        if k == KT - 1:
                            h_high(k)

            act.wait_ge(s["const_in"], 64)
            nc.scalar.activation(cs[:], cs[:], ACT.Silu).then_inc(s["cs_ready"], 1)
            for k in range(KT):
                act.wait_ge(s["tr_in"], seen("tr_in"))
                b = 2 * (k % 2)
                nc.scalar.copy(x[:, k], flat[:, b * 512:b * 512 + TOK]).then_inc(s["tr_out"], 1)
            act.wait_ge(s["tr_out"], seen("tr_out", KT))
            with seen.loop("layer", DEPTH) as l:
                skip_raw(0, 4)
                skip_raw(1, 4)
                norm(0)
                act.wait_ge(s["lam_a"], seen("lam_a"))
                nc.scalar.activation(st[:, 2:4], st[:, 0:2], ACT.Exp).then_inc(s["lam_b"], 1)
                act.wait_ge(s["pads"], seen("pads"))
                act.wait_ge(s["hready"], seen("hready"))
                for n in range(3):
                    for u in range(2):
                        if n < 2:
                            split_high(u, u)
                        act.wait_ge(s["proj"], seen("proj"))
                        if n == 1:
                            nc.scalar.activation(sg[:, 2 * u:2 * u + 2].rearrange("p j (h q) -> p (j h) q", h=2), ps[:, 4 * u:4 * u + 4, 0:HALF],
                                                 ACT.Sigmoid).then_inc(s[f"set_free{u}"], 1)
                        if n == 0:
                            for h, a, e, pad in PIECES:
                                src = ps[:, 4 * u:4 * u + 4, :].rearrange("p (j h) q -> p j h q", h=2)[:, :, h, a - h * HALF:e - h * HALF]
                                ins = nc.scalar.copy(up[:, 2 * u:2 * u + 2, pad * PPAD + a:pad * PPAD + e], src)
                            ins.then_inc(s["up_ready"], 1)
                            act.wait_ge(s["up_ready"], seen("up_ready"))
                            act.sem_inc(s[f"set_free{u}"], 1)
                skip_raw(0, 2)
                skip_raw(1, 2)
                ada_out(4, ada_row2, 4)
                split_high(0, 0)
                for g in range(GROUPS):
                    act.wait_ge(s["poolmm"], seen("poolmm"))
                    b = 2 * (g % 2)
                    nc.scalar.mul(brp[:, g], flat[:, b * 512:b * 512 + TOK],
                                  small_at("pool_scale")[:, g:g + 1]).then_inc(s["pool_br"], 1)
                with seen.loop("pair", PAIRS) as g:
                    split_high(1, 0)
                    skip_raw(1, 2)
                    seen("ada", 3)
                    for u in range(2):
                        act.wait_ge(s["proj"], seen("proj"))
                        act.wait_ge(s["newk_free"], seen("newk_free"))
                        nc.scalar.activation(qk_a[:], flat[:, 1536 * u:1536 * u + 1280], ACT.Square).then_inc(s["qksq"], 1)
                        act.wait_ge(s["qkss"], seen("qkss"))
                        nc.scalar.activation(st[:, 8:28], st[:, 8:28], ACT.Sqrt).then_inc(s["qksqrt"], 1)
                        if u == 0:
                            split_high(0, 0)
                            skip_raw(1)
                            qkT_evac(act, seen, 0)
                    act.wait_ge(s["proj"], seen("proj"))
                    act.wait_ge(s["newv_free"], seen("newv_free"))
                    nc.scalar.copy(vb[:, 0:4, :], flat[:, 0:1024].rearrange("p (t n) -> p t n", n=CW)).then_inc(s["v_ready"], 1)
                    nc.scalar.copy(vb[:, 5, :], flat[:, 1024:1280]).then_inc(s["v_ready"], 1)
                    split_high(0, 0)
                    qkT_evac(act, seen, 1)
                    act.wait_ge(s["qkT_out"], seen("qkT_out", 2))
                    for u in range(2):
                        for t in range(TT):
                            exp_unit(act, seen, t)
                        act.wait_ge(s["av"], seen("av", 0) + 1)
                        nc.scalar.copy(ot[:, 2 * g + u, 0:LAT], ps[:, 2, :])
                        nc.scalar.copy(ot[:, 2 * g + u, LAT:TOK], ps[:, 5, 0:CTX]).then_inc(s["o_out"], 1)
                act.wait_ge(s["o_out"], seen("o_out", 2 * PAIRS))
                act.wait_ge(s["newk_free"], seen("newk_free", 0) + 1)
                act.wait_ge(s["newv_free"], seen("newv_free", 0) + 1)
                for h in range(HEADS):
                    nc.scalar.activation(mm_[:, h], ot[:, h], ACT.Square).then_inc(s["o_sq"], 1)
                act.wait_ge(s["o_var"], seen("o_var"))
                nc.scalar.activation(row[0:HEADS], row[0:HEADS], ACT.Sqrt).then_inc(s["o_sqrt"], 1)
                act.wait_ge(s["ln_d"], seen("ln_d"))
                for j in range(GROUPS):
                    nc.scalar.activation(mm_[:, j, 0:LAT], zc[:, j, 0:LAT], ACT.Square)
                    nc.scalar.activation(mm_[:, j, LAT:TOK], zc[:, j, LAT + CPAD:CRUN], ACT.Square).then_inc(s["ln_sq"], 1)
                act.wait_ge(s["ln_var"], seen("ln_var"))
                nc.scalar.activation(row2[:], row2[:], ACT.Sqrt).then_inc(s["ln_sqrt"], 1)
                act.wait_ge(s["ln_n"], seen("ln_n"))
                for j in range(GROUPS):
                    for a, b, z in ((0, LAT, 0), (LAT, TOK, CPAD)):
                        ins = nc.scalar.activation(brc[:, j, a:b], zc[:, j, a + z:b + z], ACT.Silu,
                                                   scale=small_at("ln_g")[:, j:j + 1], bias=small_at("ln_b")[:, j:j + 1])
                    ins.then_inc(s["branch_c"], 1)
                seen("branch_c", GROUPS)
                with seen.loop("merge", 2) as m:
                    for i, (q, b) in enumerate(MERGE):
                        split_high((i + 1) % 2, 0)
                        skip_raw(1)
                        act.wait_ge(s["proj"], seen("proj"))
                        act.wait_ge(s["merged"], seen("merged"))
                        for j in range(2):
                            for h in range(2):
                                ins = nc.scalar.activation(sigd[:, 2 * j + h], ps[:, 2 * j + h, 0:HALF], ACT.Sigmoid,
                                                           bias=sm[:, bass.ds(4 * m + (SMALL["b_gate"][0] + 8 * b + 2 * q + j), 1)])
                        ins.then_inc(s["sig"], 1)
                        act.wait_ge(s["sig"], seen("sig"))
                        act.sem_inc(s["set_free0"], 1)
                        seen("proj")
                act.wait_ge(s["m_ready"], seen("m_ready"))
                for k in range(KT):
                    nc.scalar.copy(h_hi[:, k], mm_[:, k]).then_inc(s["mg_high"], 1)
                for c in range(4):
                    if c < 3:
                        split_high((c + 1) % 2, (c + 1) % 2)
                    act.wait_ge(s["xo_done"], seen("xo_done"))
                    squares(2 * c, 2 * c + 2)
                seen("proj", 4)
                norm(24)
                seen("hnorm", KT)
                act.wait_ge(s["rt_a"], seen("rt_a"))
                nc.scalar.activation(aff[:], aff[:], ACT.Exp).then_inc(s["rt_b"], 1)
                for t in range(TT):
                    act.wait_ge(s["h2tok_ps"], seen("h2tok_ps"))
                    b = 2 * (t % 2)
                    nc.scalar.copy(t_all[:, t], flat[:, b * 512:b * 512 + D])
                    nc.scalar.copy(t_hi[:, t], flat[:, b * 512:b * 512 + D]).then_inc(s["h2tok_hi"], 1)

                def high(n, done):
                    r = n % RING
                    act.wait_ge(s[f"mfull{r}"], seen(f"mfull{r}", 16))
                    if done:
                        act.wait_ge(s["mdone"], seen("mdone", 0) + done)
                    nc.scalar.copy(m_hi[:, r], m_raw[:, r]).then_inc(s["m_high"], 1)

                def silu(c):
                    nc.scalar.activation(hid[:], ps[0:SLOTS, 2 * c, :], ACT.Silu).then_inc(s["silu"], 1)

                def turned_high(c):
                    act.wait_ge(s["hid_t"], seen("hid_t"))
                    nc.scalar.copy(ht_hi[:, 4 * c:4 * c + 4], ps[:, 6 + c, :].rearrange("p (k n) -> p k n", k=4)[:, :, 0:SLOTS]).then_inc(s["ht_high"], 1)

                def rows_out():
                    act.wait_ge(s["xg_ps"], seen("xg_ps"))
                    nc.scalar.copy(xg[:], flat[0:SLOTS, 0:D]).then_inc(s["xg_out"], 1)
                    act.wait_ge(s["xs_ps"], seen("xs_ps"))
                    nc.scalar.copy(xs_hi[:], ps[:, 2:4, :].rearrange("p b (k n) -> p (b k) n", k=4)[:, :, 0:SLOTS]).then_inc(s["xs_high"], 1)

                def expert(last):
                    high(4, 1)
                    high(5, 2)
                    silu(0)
                    for n in (6, 7, 8, 9):
                        high(n, n - 3)
                    turned_high(0)
                    silu(1)
                    high(10, 7)
                    high(11, 8)
                    act.wait_ge(s["pt_ps"], seen("pt_ps"))
                    nc.scalar.copy(st[0:SLOTS, 32:33], ps[0:SLOTS, 6, P:P + 1])
                    nc.scalar.copy(ptk[:, 0:LAT], ps[0:SLOTS, 7, :])
                    nc.scalar.copy(ptk[:, LAT:TOK], ps[0:SLOTS, 6, 0:CTX]).then_inc(s["pt_out"], 1)
                    turned_high(1)
                    if not last:
                        high(0, 9)
                        high(1, 10)
                        high(2, 11)
                    act.wait_ge(s["mdone"], seen("mdone", 0) + NCH)
                    act.wait_ge(s["pt_out"], seen("pt_out"))
                    nc.scalar.activation(ye_hi[:], flat[0:SLOTS, 4 * 512:6 * 512], ACT.Copy, scale=st[0:SLOTS, 32:33]).then_inc(s["ye_hi"], 1)
                    if not last:
                        high(3, NCH)
                        rows_out()
                    seen("mdone", NCH)

                for n in range(RING):
                    high(n, 0)
                rows_out()
                with seen.loop("experts", EXPERTS - 1) as e:
                    expert(False)
                expert(True)
                act.wait_ge(s["layer_done"], seen("layer_done"))
            for t in range(TT):
                act.wait_ge(s["out_ps"], seen("out_ps"))
                b = 2 * (t % 2)
                nc.scalar.copy(xtok[:, t], flat[:, b * 512:b * 512 + D]).then_inc(s["out_sb"], 1)

        @block.vector
        def _(dve):
            seen = Seen(dve, "dve", s["settled"])

            def link(ins):
                ins.then_inc(s["dve"], 1)
                dve.wait_ge(s["dve"], seen("dve"))

            def link2(ins):
                ins.then_inc(s["ada_out"], 1)
                dve.wait_ge(s["ada_out"], seen("ada_out"))

            def add_mods_of(a):
                dve.wait_ge(s["ada"], seen("ada"))
                b0 = SMALL["b_ada"][0]
                nc.vector.tensor_tensor(mods[:, bass.ds(2 * a, 2), :], ada_ps[:, 0:2, :],
                                        sm[:, bass.ds(2 * a + b0, 2)].unsqueeze(2).to_broadcast([P, 2, 2]), ALU.add).then_inc(s["ada_out"], 1)
                seen("ada_out")

            def split_low(slot, rslot):
                dve.wait_ge(s["hi_done"], seen("hi_done"))
                nc.vector.tensor_tensor(w_lo[:, slot], raw[:, rslot], w_hi[:, slot].bitcast(F32),
                                        ALU.subtract).then_inc(s[f"split{slot}"], 1)
                dve.wait_ge(s[f"split{slot}"], seen(f"split{slot}"))
                dve.sem_inc(s[f"raw_free{rslot}"], 1)

            def norm():
                dve.wait_ge(s["ss"], seen("ss"))
                nc.vector.tensor_scalar(row[:].rearrange("p (a n) -> p a n", a=2), ps[:, 0:2, 0:HALF], 1.0 / D, EPS,
                                        ALU.mult, ALU.add).then_inc(s["row_a"], 1)
                dve.wait_ge(s["row_b"], seen("row_b"))
                link(nc.vector.reciprocal(row[:], row[:]))
                for k in range(KT):
                    nc.vector.tensor_tensor(mm_[:, k], x[:, k], row[:], ALU.mult).then_inc(s["tnorm"], 1)

            def coefficients(scale, g):
                for c in range(2):
                    ins = nc.vector.scalar_tensor_tensor(coef[:, :, c], mods[:, scale:scale + KT, c], 1.0, small_at(g), ALU.add, ALU.mult)
                ins.then_inc(s["mods_ready"], 1)

            def add_mods(a, b):
                link2(nc.vector.tensor_tensor(mods[:, a:b, :], ada_ps[:, a:b, :],
                                             small_at("b_ada")[:, a:b].unsqueeze(2).to_broadcast([P, b - a, 2]), ALU.add))

            dve.sem_inc(s["set_free0"], 1)
            dve.sem_inc(s["set_free1"], 1)
            dve.sem_inc(s["merged"], 1)
            dve.sem_inc(s["scat_out"], SCAT0)
            with seen.loop("layer", DEPTH) as l:
                dve.wait_ge(s["small_in"], seen("small_in", 16))
                lv = small_at("lam_vec").rearrange("p (a b n) -> p a b n", a=2, b=2)
                link(nc.vector.tensor_tensor(row2[:, 0:128].rearrange("p (a n) -> p a n", a=2), lv[:, :, 0, :], lv[:, :, 1, :], ALU.mult))
                nc.vector.tensor_reduce(st[:, 0:2], row2[:, 0:128].rearrange("p (a n) -> p a n", a=2), AX.X, ALU.add).then_inc(s["lam_a"], 1)
                norm()
                seen("ada", 8)
                dve.wait_ge(s["ada_t"], seen("ada_t"))
                add_mods(0, 16)
                coefficients(8, "rms1")
                split_low(0, 0)
                split_low(1, 1)
                for k in range(KT):
                    dve.wait_ge(s["row_c"], seen("row_c"))
                    ins = nc.vector.tensor_tensor(h_lo[:, k], mm_[:, k], h_hi[:, k].bitcast(F32), ALU.subtract)
                ins.then_inc(s["hready"], 1)
                dve.wait_ge(s["lam_b"], seen("lam_b"))
                link(nc.vector.scalar_tensor_tensor(st[:, 4:5], st[:, 3:4], small_at("lam_init"), st[:, 2:3], ALU.subtract, ALU.subtract))
                link(nc.vector.tensor_tensor(st[:, 5:6], small_at("subln"), small_at("one_minus"), ALU.mult))
                for n in range(3):
                    for u in range(2):
                        if n < 2:
                            split_low(u, u)
                        if n == 2:
                            dve.wait_ge(s["proj"], seen("proj", 5 if u == 0 else 1))
                            if u == 0:
                                dve.wait_ge(s["pads"], seen("pads"))
                            for h, a, e, pad in PIECES:
                                src = ps[:, 4 * u:4 * u + 4, :].rearrange("p (j h) q -> p j h q", h=2)[:, :, h, a - h * HALF:e - h * HALF]
                                ins = nc.vector.tensor_tensor(zc[:, 2 * u + 1:2 * u + 3, pad * CPAD + a:pad * CPAD + e], src, sg[:, 2 * u:2 * u + 2, a:e], ALU.mult)
                            ins.then_inc(s["z_ready"], 1)
                            dve.wait_ge(s["z_ready"], seen("z_ready"))
                            dve.sem_inc(s[f"set_free{u}"], 1)
                split_low(0, 0)
                seen("ada", 4)
                dve.wait_ge(s["ada_t"], seen("ada_t"))
                add_mods(16, 24)
                dve.wait_ge(s["table_in"], seen("table_in", 48))
                for g, tab in enumerate((rope_c, rope_s)):
                    v = tab[:].rearrange("p (t n) -> p t n", n=CW)
                    link(nc.vector.tensor_tensor(v, v, gains[:, g:g + 1, :].to_broadcast([P, TT, CW]), ALU.mult))

                with seen.loop("pair", PAIRS) as g:
                    taps = [0]

                    def conv(n):
                        for _ in range(n):
                            j = taps[0]
                            if j == TAPS:
                                return
                            w = sm[:, bass.ds(TAPS * g + (SMALL["conv_w"][0] + j), 1)]
                            src = zc[:, bass.ds(g + 1, 1), j:j + CRUN].rearrange("p a n -> p (a n)")
                            dst = zc[:, bass.ds(g, 1), 0:CRUN].rearrange("p a n -> p (a n)")
                            if j == 0:
                                link(nc.vector.tensor_scalar(dst, src, w, sm[:, bass.ds(g + SMALL["conv_b"][0], 1)], ALU.mult, ALU.add))
                            else:
                                link(nc.vector.scalar_tensor_tensor(dst, src, w, dst, ALU.mult, ALU.add))
                            taps[0] += 1

                    split_low(1, 0)
                    conv(13)
                    add_mods_of(3 * g + 12)
                    seen("proj", 3)
                    for u in range(2):
                        main = flat[:, 1536 * u:1536 * u + 1280]
                        dve.wait_ge(s["qksq"], seen("qksq"))
                        link(nc.vector.tensor_reduce(st[:, 8:28], qk_a[:].rearrange("p (a n) -> p a n", n=HD), AX.X, ALU.add))
                        nc.vector.tensor_scalar(st[:, 8:28], st[:, 8:28], 1.0 / HD, EPS, ALU.mult, ALU.add).then_inc(s["qkss"], 1)
                        dve.wait_ge(s["qksqrt"], seen("qksqrt"))
                        link(nc.vector.reciprocal(st[:, 8:28], st[:, 8:28]))
                        main3 = main.rearrange("p (a n) -> p a n", n=HD)
                        link(nc.vector.tensor_tensor(main3, main3, st[:, 8:28].unsqueeze(2).to_broadcast([P, 20, HD]), ALU.mult))
                        nc.vector.tensor_tensor(qk_a[:], main, rope_c[:], ALU.mult)
                        m4 = main.rearrange("p (a r n) -> p a r n", r=2, n=16)
                        b4 = qk_b[:].rearrange("p (a r n) -> p a r n", r=2, n=16)
                        s4 = rope_s[:].rearrange("p (a r n) -> p a r n", r=2, n=16)
                        nc.vector.tensor_tensor(b4[:, :, 0], m4[:, :, 1], s4[:, :, 0], ALU.mult)
                        nc.vector.tensor_tensor(b4[:, :, 1], m4[:, :, 0], s4[:, :, 1], ALU.mult).then_inc(s["qkt2"], 1)
                        if u == 0:
                            split_low(0, 0)
                            conv(8)
                            add_mods_of(3 * g + 13)
                            conv(4)
                    conv(6)
                    add_mods_of(3 * g + 14)
                    split_low(0, 0)
                    for u in range(2):
                        for t in range(TT):
                            n = TOK if t < 4 else CTX
                            for m in range(2):
                                dve.wait_ge(s["s_done"], seen("s_done"))
                                src = ps[:, 3 * m:3 * m + 2, 0:HALF] if t < 4 else ps[:, 3 * m, 0:CTX]
                                link(nc.vector.tensor_reduce(st[:, 44 + m:45 + m], src, AX.XY if t < 4 else AX.X, ALU.max))
                                nc.vector.tensor_scalar(st[:, 36 + m:37 + m], st[:, 44 + m:45 + m], -SCALE, None, ALU.mult).then_inc(s["maxd"], 1)
                            dve.wait_ge(s["expd"], seen("expd", 2))
                            link(nc.vector.reciprocal(st[:, 48:50], st[:, 40:42]))
                            link(nc.vector.tensor_scalar(st[:, 50:51], st[:, 49:50], st[:, 4:5], None, ALU.mult))
                            link(nc.vector.tensor_scalar(probs[:, 1, 0:n], probs[:, 1, 0:n], st[:, 50:51], None, ALU.mult))
                            nc.vector.scalar_tensor_tensor(probs[:, 0, 0:n], probs[:, 0, 0:n], st[:, 48:49], probs[:, 1, 0:n],
                                                           ALU.mult, ALU.add).then_inc(s["a_ready"], 1)
                    assert taps[0] == TAPS
                dve.sem_inc(s["conv_done"], 1)
                dve.wait_ge(s["o_ss"], seen("o_ss"))
                nc.vector.tensor_scalar(row[0:HEADS].rearrange("p (a n) -> p a n", a=2), ps[0:HEADS, 0:2, 0:HALF], 1.0 / DV, EPS,
                                        ALU.mult, ALU.add).then_inc(s["o_var"], 1)
                dve.wait_ge(s["ln_sum"], seen("ln_sum"))
                link(nc.vector.tensor_scalar(row2[:], flat[:, 4 * 512:4 * 512 + TOK], 1.0 / 512, None, ALU.mult))
                dve.wait_ge(s["o_sqrt"], seen("o_sqrt"))
                nc.vector.reciprocal(row[0:HEADS], row[0:HEADS]).then_inc(s["o_inv"], 1)
                for j in range(GROUPS):
                    nc.vector.tensor_tensor(zc[:, j, 0:LAT], zc[:, j, 0:LAT], row2[:, 0:LAT], ALU.subtract)
                    ins = nc.vector.tensor_tensor(zc[:, j, LAT + CPAD:CRUN], zc[:, j, LAT + CPAD:CRUN], row2[:, LAT:TOK], ALU.subtract)
                ins.then_inc(s["ln_d"], 1)
                for h in range(HEADS):
                    b = 2 * (h % 2)
                    dve.wait_ge(s["o_ss"], seen("o_ss"))
                    nc.vector.scalar_tensor_tensor(ot[:, h].rearrange("p (a n) -> p a n", a=2), ot[:, h].rearrange("p (a n) -> p a n", a=2),
                                                   st[:, 5:6], ps[:, b:b + 2, 0:HALF], ALU.mult, ALU.mult).then_inc(s["o_norm"], 1)
                dve.wait_ge(s["ln_sum"], seen("ln_sum"))
                dve.wait_ge(s["ln_d"], seen("ln_d"))
                nc.vector.tensor_scalar(row2[:], flat[:, 6 * 512:6 * 512 + TOK], 1.0 / 512, EPS, ALU.mult, ALU.add).then_inc(s["ln_var"], 1)
                dve.wait_ge(s["ln_sqrt"], seen("ln_sqrt"))
                link(nc.vector.reciprocal(row2[:], row2[:]))
                for j in range(GROUPS):
                    nc.vector.tensor_tensor(zc[:, j, 0:LAT], zc[:, j, 0:LAT], row2[:, 0:LAT], ALU.mult)
                    ins = nc.vector.tensor_tensor(zc[:, j, LAT + CPAD:CRUN], zc[:, j, LAT + CPAD:CRUN], row2[:, LAT:TOK], ALU.mult)
                ins.then_inc(s["ln_n"], 1)
                merged4 = mm_[:].rearrange("p (n j) (h q) -> p n (j h) q", j=2, h=2)
                dve.wait_ge(s["branch_c"], seen("branch_c", GROUPS))
                with seen.loop("merge", 2) as m:
                    for i, (q, b) in enumerate(MERGE):
                        split_low((i + 1) % 2, 0)
                        dve.wait_ge(s["sig"], seen("sig"))
                        dve.wait_ge(s["proj"], seen("proj", 2))
                        if i % 3 == 0:
                            nc.vector.tensor_tensor(merged4[:, 2 * m + q], ps[:, 4:8, 0:HALF], sigd[:], ALU.mult).then_inc(s["merged"], 1)
                            dve.wait_ge(s["merged"], seen("merged") + 1)
                        else:
                            nc.vector.tensor_tensor(prod[:], ps[:, 4:8, 0:HALF], sigd[:], ALU.mult).then_inc(s["merged"], 1)
                            dve.wait_ge(s["merged"], seen("merged") + 1)
                            link(nc.vector.tensor_tensor(merged4[:, 2 * m + q], merged4[:, 2 * m + q], prod[:], ALU.add))
                        dve.sem_inc(s["set_free1"], 1)
                dve.sem_inc(s["m_ready"], 1)
                for k in range(KT):
                    dve.wait_ge(s["mg_high"], seen("mg_high"))
                    nc.vector.tensor_tensor(h_lo[:, k], mm_[:, k], h_hi[:, k].bitcast(F32), ALU.subtract).then_inc(s["mg_low"], 1)
                for c in range(4):
                    u = c % 2
                    if c < 3:
                        split_low((c + 1) % 2, (c + 1) % 2)
                    dve.wait_ge(s["proj"], seen("proj"))
                    for j in range(2):
                        ct = 2 * c + j
                        for col, h, a, e in ((1, 0, 0, HALF), (1, 1, HALF, LAT), (0, 1, LAT, TOK)):
                            ins = nc.vector.scalar_tensor_tensor(x[:, ct, a:e], ps[:, 4 * u + 2 * j + h, a - h * HALF:e - h * HALF],
                                                                 mods[:, 16 + ct, col:col + 1], x[:, ct, a:e], ALU.mult, ALU.add)
                    ins.then_inc(s["xo_done"], 1)
                    dve.wait_ge(s["xo_done"], seen("xo_done"))
                    dve.sem_inc(s[f"set_free{u}"], 1)
                coefficients(32, "rms2")
                norm()
                dve.wait_ge(s["logits"], seen("logits"))
                nc.vector.tensor_copy(cum[:].rearrange("p (a n) -> p a n", a=2), ps[0:EXPERTS, 4:6, 0:HALF]).then_inc(s["logits_out"], 1)
                dve.wait_ge(s["logits_t"], seen("logits_t"))
                lg = ps[:, 7, 0:TT * EXPERTS].rearrange("p (t e) -> p t e", e=EXPERTS)
                link(nc.vector.tensor_reduce(st[:, 8:13], lg, AX.X, ALU.max))
                nc.vector.tensor_tensor(aff[:], lg, st[:, 8:13].unsqueeze(2).to_broadcast([P, TT, EXPERTS]), ALU.subtract).then_inc(s["rt_a"], 1)
                dve.wait_ge(s["rt_b"], seen("rt_b"))
                link(nc.vector.tensor_reduce(st[:, 8:13], aff[:], AX.X, ALU.add))
                link(nc.vector.reciprocal(st[:, 8:13], st[:, 8:13]))
                nc.vector.tensor_tensor(aff[:], aff[:], st[:, 8:13].unsqueeze(2).to_broadcast([P, TT, EXPERTS]), ALU.mult).then_inc(s["aff_r"], 1)
                dve.sem_inc(s["small_free"], 1)
                dve.wait_ge(s["affT"], seen("affT"))
                link(nc.vector.tensor_copy(affw[:], flat[0:EXPERTS, 5 * 512:5 * 512 + TOK]))
                for a, b, rounds, tag in ((0, LAT, CAP_LAT // 8, "top_lat"), (LAT, TOK, CAP_CTX // 8, "top_ctx")):
                    with seen.loop(tag, rounds) as i:
                        link(nc.vector.max(top8[:], affw[:, a:b]))
                        seen.settle()
                        link(nc.vector.match_replace(affw[:, a:b], top8[:], affw[:, a:b], -1.0))
                link(nc.vector.tensor_scalar(mask[:], affw[:], 0.0, None, ALU.is_lt))
                link(nc.vector.memset(affw[:], 1.0))
                nc.vector.tensor_tensor_scan(cum[:, 0:LAT], affw[:, 0:LAT], mask[:, 0:LAT], 0.0, ALU.mult, ALU.add)
                link(nc.vector.tensor_tensor_scan(cum[:, LAT:TOK], affw[:, LAT:TOK], mask[:, LAT:TOK], float(CAP_LAT), ALU.mult, ALU.add))
                link(nc.vector.tensor_tensor(cum[:], cum[:], mask[:], ALU.mult))
                nc.vector.tensor_scalar(cum[:], cum[:], -1.0, None, ALU.add).then_inc(s["topk"], 1)
                nc.vector.memset(pos[:], -1.0).then_inc(s["pos_r"], 1)
                dve.wait_ge(s["posT"], seen("posT"))
                dve.wait_ge(s["pos_r"], seen("pos_r"))
                link(nc.vector.tensor_copy(pos[:, :, 0:EXPERTS], ps[:, 7, 0:TT * EXPERTS].rearrange("p (t e) -> p t e", e=EXPERTS)))

                def choose(e):
                    nc.vector.tensor_tensor(pick[:], slot_no[:].unsqueeze(1).to_broadcast([P, TT, SLOTS]),
                                            pos[:, :, bass.ds(e, 1)].to_broadcast([P, TT, SLOTS]), ALU.is_equal).then_inc(s["picked"], 1)

                def low(n):
                    r = n % RING
                    dve.wait_ge(s["m_high"], seen("m_high"))
                    nc.vector.tensor_tensor(m_lo[:, r], m_raw[:, r], m_hi[:, r].bitcast(F32), ALU.subtract).then_inc(s["msplit"], 1)

                def gate_up(c):
                    dve.wait_ge(s["silu"], seen("silu"))
                    dve.wait_ge(s["mdone"], seen("mdone", 0) + 4 * c + 4)
                    nc.vector.tensor_tensor(hid[:], hid[:], ps[0:SLOTS, 2 * c + 1, :], ALU.mult).then_inc(s["hidd"], 1)

                def turned_low(c):
                    dve.wait_ge(s["ht_high"], seen("ht_high"))
                    nc.vector.tensor_tensor(ht_lo[:, 4 * c:4 * c + 4], ps[:, 6 + c, :].rearrange("p (k n) -> p k n", k=4)[:, :, 0:SLOTS],
                                            ht_hi[:, 4 * c:4 * c + 4].bitcast(F32), ALU.subtract).then_inc(s["ht_out"], 1)

                def rows_low():
                    dve.wait_ge(s["xs_high"], seen("xs_high"))
                    nc.vector.tensor_tensor(xs_lo[:], ps[:, 2:4, :].rearrange("p b (k n) -> p (b k) n", k=4)[:, :, 0:SLOTS],
                                            xs_hi[:].bitcast(F32), ALU.subtract).then_inc(s["xs_out"], 1)

                def expert(e, last):
                    for n in (4, 5, 6):
                        low(n)
                    gate_up(0)
                    for n in (7, 8, 9):
                        low(n)
                    turned_low(0)
                    low(10)
                    gate_up(1)
                    low(11)
                    turned_low(1)
                    dve.wait_ge(s["pt_ps"], seen("pt_ps"))
                    if not last:
                        choose(e + 1)
                        low(0)
                        low(1)
                        low(2)
                    dve.wait_ge(s["ye_hi"], seen("ye_hi"))
                    nc.vector.scalar_tensor_tensor(ye_lo[:], flat[0:SLOTS, 4 * 512:6 * 512], st[0:SLOTS, 32:33], ye_hi[:].bitcast(F32),
                                                   ALU.mult, ALU.subtract).then_inc(s["ye_lo"], 1)
                    for i in range(KT):
                        if i == 2 and not last:
                            rows_low()
                        dve.wait_ge(s["scat"], seen("scat", 2 if i == 4 else 1))
                        nc.vector.scalar_tensor_tensor(x[:, i, 0:LAT], ps[:, LATBANK[i], :], mods[:, 40 + i, 1:2], x[:, i, 0:LAT],
                                                       ALU.mult, ALU.add).then_inc(s["scat_out"], 1)
                    for i in range(KT):
                        ins = nc.vector.scalar_tensor_tensor(x[:, i, LAT:TOK], ps[:, 6 + i // 4, (i % 4) * P:(i % 4 + 1) * P],
                                                             mods[:, 40 + i, 0:1], x[:, i, LAT:TOK], ALU.mult, ALU.add)
                    ins.then_inc(s["scat_out"], 1)
                    if not last:
                        low(3)
                    seen("mdone", NCH)
                    dve.wait_ge(s["scat_out"], seen("scat_out", KT + 1) + SCAT0)

                choose(0)
                for n in range(RING):
                    low(n)
                rows_low()
                with seen.loop("experts", EXPERTS - 1) as e:
                    expert(e, False)
                expert(EXPERTS - 1, True)
                dve.sem_inc(s["layer_done"], 1)

        @block.tensor
        def _(pe):
            seen = Seen(pe, "pe", s["settled"])
            pe.sem_inc(s["split_free0"], 1)
            pe.sem_inc(s["split_free1"], 1)
            pe.sem_inc(s["aT"], 1)
            pe.sem_inc(s["av"], 1)

            def three(out, wh, wl, xh, xl, first, last):
                pe.matmul(out, wh, xh, start=first, stop=False, skip_group_check=True)
                pe.matmul(out, wh, xl, start=False, stop=False, skip_group_check=True)
                return pe.matmul(out, wl, xh, start=False, stop=last, skip_group_check=True)

            def wait_split(slot):
                pe.wait_ge(s[f"split{slot}"], seen(f"split{slot}"))

            def wait_set(u):
                pe.wait_ge(s[f"set_free{u}"], seen(f"set_free{u}"))

            halves = ((0, HALF), (HALF, TOK))

            def feature_split(slot, u, cuts, release=None):
                for j in range(2):
                    for c, (a, b) in enumerate(cuts):
                        if release and (j, c) == (0, 1):
                            release()
                        for k in range(KT):
                            ins = three(ps[:, 4 * u + 2 * j + c, 0:b - a], w_hi[:, slot, k, j * P:(j + 1) * P],
                                        w_lo[:, slot, k, j * P:(j + 1) * P], h_hi[:, k, a:b], h_lo[:, k, a:b], k == 0, k == KT - 1)
                ins.then_inc(s["proj"], 1)

            def out_first(slot, u):
                for k in range(KT):
                    pe.wait_ge(s["mg_low"], seen("mg_low"))
                    for j in range(2):
                        for c, (a, b) in enumerate(halves):
                            ins = three(ps[:, 4 * u + 2 * j + c, 0:b - a], w_hi[:, slot, k, j * P:(j + 1) * P],
                                        w_lo[:, slot, k, j * P:(j + 1) * P], h_hi[:, k, a:b], h_lo[:, k, a:b], k == 0, k == KT - 1)
                ins.then_inc(s["proj"], 1)

            def feature_raw(rslot, u, cuts, src, kt):
                for j in range(2):
                    for c, (a, b) in enumerate(cuts):
                        for k in range(kt):
                            ins = pe.matmul(ps[:, 4 * u + 2 * j + c, 0:b - a], raw[:, rslot, k, j * P:(j + 1) * P],
                                            src[:, k, a:b], start=(k == 0), stop=(k == kt - 1))
                ins.then_inc(s["proj"], 1)

            def ada(a, rslot):
                pe.wait_ge(s[f"raw_full{rslot}"], seen(f"raw_full{rslot}", 32))
                for j in range(2):
                    for k in range(KT):
                        out = ps[:, 7, 2 * j:2 * j + 2] if a is None else flat[:, bass.ds(4 * a + (7 * 512 + 2 * j), 2)]
                        ins = pe.matmul(out, raw[:, rslot, k, j * P:(j + 1) * P], cs[:, k, :], start=(k == 0), stop=(k == KT - 1))
                ins.then_inc(s["ada"], 1)
                seen("ada")

            def used(split_slot):
                pe.wait_ge(s["ada"], seen("ada", 0))
                pe.sem_inc(s[f"split_free{split_slot}"], 1)
                pe.sem_inc(s["raw_free1"], 1)

            def ada_wide(at, rslot):
                pe.wait_ge(s[f"raw_full{rslot}"], seen(f"raw_full{rslot}", 32))
                for k in range(KT):
                    ins = pe.matmul(flat[0:2, bass.ds(at, CW)], cs[:, k, :], raw[:, rslot, k, :], start=(k == 0), stop=(k == KT - 1))
                ins.then_inc(s["ada"], 1)
                pe.wait_ge(s["ada"], seen("ada"))
                pe.sem_inc(s[f"raw_free{rslot}"], 1)

            def turn_ada(src, a, b):
                pe.wait_ge(s["ada_row"], seen("ada_row"))
                seen.settle()
                for m in range(a, b):
                    ins = pe.transpose(ada_ps[:, m, :], src[:, (m - a) * P:(m - a + 1) * P], ident[0:2, 0:2])
                ins.then_inc(s["ada_t"], 1)

            def sum_squares(n_in, sem_in):
                for k in range(n_in):
                    pe.wait_ge(s[sem_in], seen(sem_in))
                    for c, (a, b) in enumerate(halves):
                        ins = pe.matmul(ps[:, c, 0:HALF], ones[:], mm_[:, k, a:b], start=(k == 0), stop=(k == n_in - 1), skip_group_check=True)
                ins.then_inc(s["ss"], 1)

            def token_major(slot, off, last_wait=False, release=None):
                for t in range(TT):
                    if t == 1 and release is not None:
                        used(release)
                    if last_wait and t == 4:
                        pe.wait_ge(s["qkT_out"], seen("qkT_out"))
                    for k in range(KT):
                        ins = three(flat[:, off + t * CW:off + (t + 1) * CW], h_hi[:, k, t * P:(t + 1) * P], h_lo[:, k, t * P:(t + 1) * P],
                                    w_hi[:, slot, k, :], w_lo[:, slot, k, :], k == 0, k == KT - 1)
                ins.then_inc(s["proj"], 1)

            def turn_qk(u):
                pe.wait_ge(s["roped"], seen("roped"))
                for b in range(2):
                    if b == 1:
                        pe.wait_ge(s["ada_out"], seen("ada_out"))
                    for t in range(4):
                        pe.transpose(ps[:, 6 + b, t * P:(t + 1) * P], qk_a[:, t * CW + b * P:t * CW + (b + 1) * P], ident[:])
                for b in range(2):
                    ins = pe.transpose(ps[:, 2 + 3 * u, 256 + b * P:256 + (b + 1) * P], qk_a[:, 4 * CW + b * P:4 * CW + (b + 1) * P], ident[:])
                if u == 0:
                    pe.wait_ge(s["cache_in"], seen("cache_in", 32))
                    for i in range(2):
                        ins = pe.transpose(ps[:, 2, i * P:(i + 1) * P], ck[:, i * P:(i + 1) * P], ident[:])
                ins.then_inc(s["qkT"], 1)

            def scores(i, ms):
                u, t = divmod(i, TT)
                for m in ms:
                    if i:
                        pe.wait_ge(s["expd"], seen("expd"))
                    q = qk_t[64 * m:64 * m + 64, u, t * P:(t + 1) * P]
                    if t < 4:
                        for c in range(2):
                            ins = pe.matmul(ps[:, 3 * m + c, 0:HALF], q, qk_t[64 * m:64 * m + 64, u, TOK + c * HALF:TOK + (c + 1) * HALF],
                                            start=True, stop=True)
                    else:
                        ins = pe.matmul(ps[:, 3 * m, 0:CTX], q, qk_t[64 * m:64 * m + 64, u, 2 * TOK:2 * TOK + CTX], start=True, stop=True)
                    ins.then_inc(s["s_done"], 1)

            def turn_probs(i):
                t = i % TT
                pe.wait_ge(s["a_ready"], seen("a_ready"))
                nk = TT if t < 4 else 1
                for c in range(nk):
                    ins = pe.transpose(flat[:, 6 * 512 + c * P:6 * 512 + (c + 1) * P], probs[:, 0, c * P:(c + 1) * P], ident[:])
                ins.then_inc(s["aT"], 1)

            def values(i):
                u, t = divmod(i, TT)
                nk = TT if t < 4 else 1
                pe.wait_ge(s["aT_out"], seen("aT_out"))
                if t == 0 and u == 1:
                    pe.wait_ge(s["o_out"], seen("o_out"))
                out = ps[:, 2, t * P:(t + 1) * P] if t < 4 else ps[:, 5, 0:P]
                for c in range(nk):
                    ins = pe.matmul(out, vb[:, c if t < 4 else 5, u * P:(u + 1) * P], at_[:, c, :], start=(c == 0), stop=(c == nk - 1))
                ins.then_inc(s["av"], 1)

            pe.wait_ge(s["const_in"], 64)
            pe.wait_ge(s["x_in"], 32)
            for k in range(KT):
                if k >= 2:
                    pe.wait_ge(s["tr_out"], seen("tr_out"))
                b = 2 * (k % 2)
                for t in range(TT):
                    ins = pe.transpose(flat[:, b * 512 + t * P:b * 512 + (t + 1) * P], xtok[:, t, k * P:(k + 1) * P], ident[:])
                ins.then_inc(s["tr_in"], 1)
            pe.wait_ge(s["tr_out"], seen("tr_out", 2))
            pe.wait_ge(s["cs_ready"], 1)
            with seen.loop("layer", DEPTH) as l:
                sum_squares(KT, "sq")
                with seen.loop("ada1", 4) as i:
                    for u in range(2):
                        ada_wide(CW * (2 * i + u) + 2 * 512, u)
                turn_ada(ada_row, 0, 16)
                seen("raw_full0", 96)
                seen("raw_full1", 96)
                pe.wait_ge(s["row_a"], seen("row_a"))
                pe.wait_ge(s["hready"], seen("hready"))
                pe.wait_ge(s["ada_out"], seen("ada_out"))
                with seen.loop("conv_pool", 3) as i:
                    for u in range(2):
                        wait_split(u)
                        wait_set(u)
                        feature_split(u, u, halves)
                        pe.wait_ge(s["proj"], seen("proj"))
                        pe.sem_inc(s[f"split_free{u}"], 1)
                pe.wait_ge(s["z_ready"], seen("z_ready", 2))
                with seen.loop("ada2", 2) as i:
                    for u in range(2):
                        ada_wide(CW * (2 * i + u) + 4 * 512, u)
                for g in range(GROUPS):
                    pe.wait_ge(s["pooled"], seen("pooled"))
                    if g >= 2:
                        pe.wait_ge(s["pool_br"], seen("pool_br"))
                    b = 2 * (g % 2)
                    pw = small_at("pool_w")[:, g * P:(g + 1) * P]
                    pe.matmul(ps[:, b, :], pw, up[:, g, PPAD:PPAD + LAT], start=True, stop=True)
                    pe.matmul(ps[:, b + 1, 0:CTX], pw, up[:, g, 2 * PPAD + LAT:2 * PPAD + TOK], start=True, stop=True).then_inc(s["poolmm"], 1)
                turn_ada(ada_row2, 16, 24)
                pe.wait_ge(s["pool_br"], seen("pool_br", 2))
                pe.wait_ge(s["ada_out"], seen("ada_out"))
                with seen.loop("pair", PAIRS) as g:
                    for u in range(2):
                        wait_split(u)
                        seen("raw_full0", 32)
                        seen("proj")
                        token_major(u, 1536 * u, release=0 if u else None)
                        if u == 1:
                            pe.wait_ge(s["ada_out"], seen("ada_out"))
                        ada(None, 1)
                    turn_qk(0)
                    wait_split(0)
                    seen("raw_full0", 32)
                    seen("proj")
                    token_major(0, 0, True, release=1)
                    ada(None, 1)
                    turn_qk(1)
                    pe.wait_ge(s["v_ready"], seen("v_ready", 2))
                    scores(0, (0, 1))
                    used(0)
                    for i in range(2 * TT):
                        if i + 1 < 2 * TT:
                            scores(i + 1, (0,))
                        if i == 0:
                            pe.wait_ge(s["qkT_out"], seen("qkT_out"))
                        turn_probs(i)
                        if i + 1 < 2 * TT:
                            scores(i + 1, (1,))
                        values(i)
                    pe.wait_ge(s["av"], seen("av", 10) + 1)
                    pe.sem_inc(s["attn_free"], 1)
                    pe.wait_ge(s["expd"], seen("expd", 2))
                    pe.wait_ge(s["o_out"], seen("o_out"))
                for h in range(HEADS):
                    pe.wait_ge(s["o_sq"], seen("o_sq"))
                    for c, (a, e) in enumerate(halves):
                        ins = pe.matmul(ps[0:HEADS, c, 0:HALF], sel[:, HEADS - h:2 * HEADS - h], mm_[:, h, a:e],
                                        start=(h == 0), stop=(h == HEADS - 1), skip_group_check=True)
                ins.then_inc(s["o_ss"], 1)
                pe.wait_ge(s["conv_done"], seen("conv_done"))
                for j in range(GROUPS):
                    pe.matmul(ps[:, 4, :], ones[:], zc[:, j, 0:LAT], start=(j == 0), stop=(j == GROUPS - 1), skip_group_check=True)
                    ins = pe.matmul(ps[:, 5, 0:CTX], ones[:], zc[:, j, LAT + CPAD:CRUN], start=(j == 0), stop=(j == GROUPS - 1), skip_group_check=True)
                ins.then_inc(s["ln_sum"], 1)
                pe.wait_ge(s["o_inv"], seen("o_inv"))
                seen("o_var")
                for h in range(HEADS):
                    b = 2 * (h % 2)
                    if h >= 2:
                        pe.wait_ge(s["o_norm"], seen("o_norm"))
                    for c, (a, e) in enumerate(halves):
                        ins = pe.matmul(ps[:, b + c, 0:HALF], ident[0:HEADS, h:h + 1].to_broadcast([HEADS, P]), row[0:HEADS, a:e], start=True, stop=True)
                    ins.then_inc(s["o_ss"], 1)
                for j in range(GROUPS):
                    pe.wait_ge(s["ln_sq"], seen("ln_sq"))
                    pe.matmul(ps[:, 6, :], ones[:], mm_[:, j, 0:LAT], start=(j == 0), stop=(j == GROUPS - 1), skip_group_check=True)
                    ins = pe.matmul(ps[:, 7, 0:CTX], ones[:], mm_[:, j, LAT:TOK], start=(j == 0), stop=(j == GROUPS - 1), skip_group_check=True)
                ins.then_inc(s["ln_sum"], 1)
                pe.wait_ge(s["o_norm"], seen("o_norm", 2))
                seen("ln_var")
                seen("branch_c", GROUPS)
                with seen.loop("merge", 2) as m:
                    def release(slot):
                        pe.wait_ge(s["proj"], seen("proj", 0) - 1)
                        pe.sem_inc(s["raw_free1"], 1)
                        pe.sem_inc(s[f"split_free{slot}"], 1)

                    for i, (q, b) in enumerate(MERGE):
                        wait_split(i % 2)
                        seen("raw_full0", 32)
                        wait_set(0)
                        seen("proj")
                        feature_split(i % 2, 0, halves, (lambda: release((i + 1) % 2)) if i else None)
                        pe.wait_ge(s["raw_full1"], seen("raw_full1", 32))
                        wait_set(1)
                        seen("proj")
                        if i == 0:
                            pe.wait_ge(s["ln_var"], seen("ln_var", 0))
                        if i == 2:
                            pe.wait_ge(s["branch_c"], seen("branch_c", 0))
                        src, kt = ((ot, KT), (brp, GROUPS), (brc, GROUPS))[b]
                        feature_raw(1, 1, halves, src, kt)
                    pe.wait_ge(s["proj"], seen("proj", 0))
                    pe.sem_inc(s["raw_free1"], 1)
                    pe.sem_inc(s["split_free1"], 1)
                for c in range(4):
                    u = c % 2
                    wait_split(u)
                    seen(f"raw_full{u}", 32)
                    wait_set(u)
                    seen("proj")
                    if c == 0:
                        out_first(u, u)
                    else:
                        feature_split(u, u, halves)
                    pe.wait_ge(s["proj"], seen("proj", 0))
                    pe.sem_inc(s[f"split_free{u}"], 1)
                pe.sem_inc(s["d_done"], 1)
                seen("xo_done", 3)
                pe.wait_ge(s["xo_done"], seen("xo_done"))
                sum_squares(KT, "sq")
                seen("hnorm", KT)
                for k in range(KT):
                    pe.wait_ge(s["hnorm"], seen("hnorm"))
                    for c, (a, b) in enumerate(halves):
                        ins = pe.matmul(ps[0:EXPERTS, 4 + c, 0:HALF], small_at("router")[:, k * EXPERTS:(k + 1) * EXPERTS], mm_[:, k, a:b],
                                        start=(k == 0), stop=(k == KT - 1), skip_group_check=True)
                ins.then_inc(s["logits"], 1)
                pe.wait_ge(s["logits_out"], seen("logits_out"))
                seen.settle()
                for t in range(TT):
                    ins = pe.transpose(ps[:, 7, t * EXPERTS:(t + 1) * EXPERTS], cum[:, t * P:(t + 1) * P], ident[0:EXPERTS, 0:EXPERTS])
                ins.then_inc(s["logits_t"], 1)
                pe.wait_ge(s["row_a"], seen("row_a"))
                for t in range(TT):
                    if t >= 2:
                        pe.wait_ge(s["h2tok_hi"], seen("h2tok_hi"))
                    b = 2 * (t % 2)
                    for k in range(KT):
                        ins = pe.transpose(flat[:, b * 512 + k * P:b * 512 + (k + 1) * P], mm_[:, k, t * P:(t + 1) * P], ident[:])
                    ins.then_inc(s["h2tok_ps"], 1)
                    if t == 1:
                        pe.wait_ge(s["aff_r"], seen("aff_r"))
                        for c in range(TT):
                            ins = pe.transpose(flat[0:EXPERTS, 5 * 512 + c * P:5 * 512 + (c + 1) * P], aff[:, c, :], ident[:])
                        ins.then_inc(s["affT"], 1)
                pe.wait_ge(s["topk"], seen("topk"))
                seen.settle()
                for c in range(TT):
                    ins = pe.transpose(ps[:, 7, c * EXPERTS:(c + 1) * EXPERTS], cum[:, c * P:(c + 1) * P], ident[0:EXPERTS, 0:EXPERTS])
                ins.then_inc(s["posT"], 1)

                def gather():
                    pe.wait_ge(s["picked"], seen("picked"))
                    for c in range(2):
                        for t in range(TT):
                            for part in (t_hi, t_lo):
                                ins = pe.matmul(ps[0:SLOTS, c, :], pick[:, t, :], part[:, t, c * EW:(c + 1) * EW],
                                                start=(t == 0 and part is t_hi), stop=(t == TT - 1 and part is t_lo))
                    ins.then_inc(s["xg_ps"], 1)

                def turn_rows():
                    for k in range(KT):
                        ins = pe.transpose(flat[:, 2 * 512 + k * P:2 * 512 + k * P + SLOTS], xg[:, k * P:(k + 1) * P], ident[0:SLOTS, 0:SLOTS])
                    ins.then_inc(s["xs_ps"], 1)

                def product(n):
                    w, k0, c, bank = CHUNKS[n]
                    hi, lo = (xs_hi, xs_lo) if w < 2 else (ht_hi, ht_lo)
                    pe.wait_ge(s["msplit"], seen("msplit"))
                    for k in range(EK):
                        ins = three(ps[0:SLOTS, bank, :], hi[:, k0 + k, :], lo[:, k0 + k, :], m_hi[:, n % RING, k, :], m_lo[:, n % RING, k, :],
                                    k0 + k == 0, k0 + k == KT - 1)
                    ins.then_inc(s["mdone"], 1)

                def turn_hid(c):
                    pe.wait_ge(s["hidd"], seen("hidd"))
                    for k in range(4):
                        ins = pe.transpose(ps[:, 6 + c, k * P:k * P + SLOTS], hid[:, k * P:(k + 1) * P], ident[0:SLOTS, 0:SLOTS])
                    ins.then_inc(s["hid_t"], 1)

                def turn_pick(e):
                    pe.wait_ge(s["ht_out"], seen("ht_out"))
                    for t in range(TT):
                        pe.matmul(ps[0:SLOTS, 6, P:P + 1], pick[:, t, :].bitcast(F32), aff[:, t, bass.ds(e, 1)], start=(t == 0), stop=(t == TT - 1))
                    pe.transpose(ps[0:SLOTS, 6, 0:P], pick[:, 4, :].bitcast(F32), ident[:])
                    for t in range(4):
                        ins = pe.transpose(ps[0:SLOTS, 7, t * P:(t + 1) * P], pick[:, t, :].bitcast(F32), ident[:])
                    ins.then_inc(s["pt_ps"], 1)

                def two(out, i, a, b):
                    pe.matmul(out, ye_hi[:, i * P:(i + 1) * P], ptk[:, a:b], start=True, stop=False)
                    return pe.matmul(out, ye_lo[:, i * P:(i + 1) * P], ptk[:, a:b], start=False, stop=True)

                def expert(e, last):
                    pe.wait_ge(s["xs_out"], seen("xs_out"))
                    for n in range(6):
                        if n == 2:
                            pe.wait_ge(s["scat_out"], seen("scat_out", 0) + SCAT0 - 3)
                        product(n)
                    turn_hid(0)
                    product(6)
                    product(7)
                    turn_pick(e)
                    pe.wait_ge(s["scat_out"], seen("scat_out", 0) + SCAT0)
                    product(8)
                    pe.wait_ge(s["pt_out"], seen("pt_out"))
                    turn_hid(1)
                    product(9)
                    pe.wait_ge(s["ht_out"], seen("ht_out"))
                    product(10)
                    product(11)
                    if not last:
                        gather()
                    pe.wait_ge(s["ye_hi"], seen("ye_hi"))
                    pe.wait_ge(s["ye_lo"], seen("ye_lo"))
                    for i in range(KT):
                        if i == 2 and not last:
                            pe.wait_ge(s["xg_out"], seen("xg_out"))
                            turn_rows()
                        if i == 4:
                            for c in range(KT):
                                ins = two(ps[:, 6 + c // 4, (c % 4) * P:(c % 4 + 1) * P], c, LAT, TOK)
                            ins.then_inc(s["scat"], 1)
                        if 4 <= i < 6:
                            pe.wait_ge(s["scat_out"], seen("scat_out", 0) + SCAT0 + i - 1)
                        two(ps[:, LATBANK[i], :], i, 0, LAT).then_inc(s["scat"], 1)
                    pe.wait_ge(s["scat_out"], seen("scat_out", 0) + SCAT0 + 5)
                    seen("scat_out", KT + 1)

                seen("h2tok_hi", 2)
                pe.wait_ge(s["h2tok_lo"], seen("h2tok_lo", TT))
                gather()
                pe.wait_ge(s["xg_out"], seen("xg_out"))
                turn_rows()
                with seen.loop("experts", EXPERTS - 1) as e:
                    expert(e, False)
                expert(EXPERTS - 1, True)
                pe.wait_ge(s["scat_out"], seen("scat_out", 0) + SCAT0)
            for t in range(TT):
                if t >= 2:
                    pe.wait_ge(s["out_sb"], seen("out_sb"))
                b = 2 * (t % 2)
                for k in range(KT):
                    ins = pe.transpose(flat[:, b * 512 + k * P:b * 512 + (k + 1) * P], x[:, k, t * P:(t + 1) * P], ident[:])
                ins.then_inc(s["out_ps"], 1)


def constants():
    ident = np.eye(P, dtype=np.float32)
    rows, cols = np.divmod(np.arange(LAT), 64)
    inv = (10000.0 ** (-np.arange(16, dtype=np.float32) / np.float32(16))).astype(np.float32)
    c = np.ones((TT, P, 4, 2, 2, 16), np.float32)
    sn = np.zeros((TT, P, 4, 2, 2, 16), np.float32)
    for a, at in enumerate((rows, cols)):
        ang = (at.astype(np.float32)[:, None] * inv[None]).reshape(4, P, 1, 1, 16)
        c[:4, :, :, a] = np.cos(ang)
        sn[:4, :, :, a] = np.sin(ang) * np.array([-1, 1], np.float32)[:, None]
    cos = np.ascontiguousarray(c.transpose(1, 0, 2, 3, 4, 5)).reshape(P, TT * CW)
    sin = np.ascontiguousarray(sn.transpose(1, 0, 2, 3, 4, 5)).reshape(P, TT * CW)
    cnt = np.zeros((GROUPS, PRUN), np.float32)
    for g in range(GROUPS):
        w = 1 << g
        for at, n in ((0, LAT), (LAT + PPAD, CTX)):
            t = np.arange(n)
            cnt[g, at:at + n] = 1.0 / (np.clip(t + w, 0, n) - np.clip(t - w, 0, n))
    slot = np.ascontiguousarray(np.broadcast_to(np.arange(SLOTS, dtype=np.float32), (P, SLOTS)))
    return ident, cos, sin, cnt, slot


def kernel(**inputs):
    import math
    import concourse.bacc as _bacc
    from concourse.bass_utils import run_bass_kernel_spmd as _run

    a = {k: np.ascontiguousarray(v) for k, v in inputs.items()}

    def cols(v, n):
        return v.reshape(DEPTH, n, P).transpose(0, 2, 1)

    def rows(v):
        return np.broadcast_to(v.reshape(DEPTH, 1, -1), (DEPTH, P, v[0].size))

    qg, kg = a["q_norm_g"], a["k_norm_g"]
    qkg = np.concatenate([qg, qg, kg, kg], 1)
    swapped = qkg.reshape(DEPTH, 8, 2, 16)[:, :, ::-1].reshape(DEPTH, 256)
    lam_init = np.array([0.8 - 0.6 * math.exp(-0.3 * l) for l in range(DEPTH)], np.float32)
    one_minus = np.array([1.0 - (0.8 - 0.6 * math.exp(-0.3 * l)) for l in range(DEPTH)], np.float32)
    parts = {
        "rms1": cols(a["rms1_g"], 8), "rms2": cols(a["rms2_g"], 8), "b_ada": cols(a["b_ada"], 48),
        "pool_scale": cols(a["pool_scale"], 4), "conv_b": cols(a["conv_b"], 4), "ln_g": cols(a["conv_ln_g"], 4),
        "ln_b": cols(a["conv_ln_b"], 4), "b_gate": cols(a["b_gate"], 24), "subln": cols(a["subln_g"], 1),
        "conv_w": a["conv_w"].reshape(DEPTH, TAPS, 4, P).transpose(0, 3, 2, 1).reshape(DEPTH, P, 4 * TAPS),
        "router": a["w_router"].reshape(DEPTH, 8, P, 16).transpose(0, 2, 1, 3).reshape(DEPTH, P, 128),
        "lam_vec": rows(a["lam_vec"]),
        "lam_init": rows(lam_init), "one_minus": rows(one_minus),
        "pool_w": a["pool_w"].transpose(0, 2, 1, 3).reshape(DEPTH, P, 512),
    }
    small = np.concatenate([parts[n] for n in SMALL], axis=2)
    ident, cos, sin, cnt, slot = constants()
    cvecs = np.stack([a["c_ctx"], a["c"][0]], 1).reshape(KT, P, 2).transpose(1, 0, 2)
    given = {
        "x_prompt": a["x_prompt"], "x_sample": a["x_sample"], "cvecs": cvecs, "cache_k": a["cache_k"], "cache_v": a["cache_v"],
        "small": small, "gains_in": np.stack([rows(qkg), rows(swapped)], 2), "w_ada": a["w_ada"], "w_in": a["w_in"], "w_proj_a": a["w_proj_a"], "w_proj_b": a["w_proj_b"],
        "w_proj_c": a["w_proj_c"], "w_gate": a["w_gate"], "w_out": a["w_out"], "w1": a["w1"], "w3": a["w3"], "w2": a["w2"],
        "ident_in": ident, "cos_in": cos, "sin_in": sin, "inv_in": cnt, "slot_in": slot,
    }
    shapes = [a["x_prompt"].shape, a["x_sample"].shape, (1, DEPTH, CTX, HEADS, 2, HD), (1, DEPTH, CTX, HEADS, DV)]

    def program():
        nc = _bacc.Bacc("TRN2", target_bir_lowering=False, num_devices=1)
        args = [nc.dram_tensor(f"in_{n}", v.shape, F32, kind="ExternalInput").ap() for n, v in given.items()]
        args += [nc.dram_tensor(f"out_{i}", sh, F32, kind="ExternalOutput").ap() for i, sh in enumerate(shapes)]
        build(nc, *args)
        return nc

    for _ in range(6):
        PER_TURN.pop("changed", None)
        nc = program()
        if not PER_TURN.get("changed"):
            break
    arrays = {f"in_{n}": np.ascontiguousarray(v) for n, v in given.items()}
    r = _run(nc, [arrays], core_ids=[0])
    return tuple(r.results[0][f"out_{i}"] for i in range(4))
```
